# Optimizing a Trainium2 kernel written in Bass

```python
import jax, jax.numpy as jnp
from jax import lax
import numpy as np

D_MODEL = 1024
BATCH = 1
SEQ = 256
DEPTH = 2

CHUNK = 64
N_A = DEPTH // 2
N_B = DEPTH - N_A
RET_HEADS = 4
RET_DK = D_MODEL // RET_HEADS
RET_DV = 2 * RET_DK
RET_V = RET_HEADS * RET_DV
MLA_HEADS = 8
QK_NOPE = 128
QK_ROPE = 64
V_HEAD = 128
Q_LORA = 256
KV_LORA = 128
Q_BLOCK = 128
N_EXPERTS = 16
N_GROUPS = 4
EXPERTS_PER_GROUP = N_EXPERTS // N_GROUPS
TOP_K = 2
D_EXPERT = 512
ROPE_THETA = 10000.0
EPS = 1e-6

kernel_name = "yoco_retention_mla_grouped_moe"

def rms_norm(x, g):
    xf = x.astype(jnp.float32)
    y = xf * lax.rsqrt(jnp.mean(xf * xf, axis=-1, keepdims=True) + EPS)
    return (y * g.astype(jnp.float32)).astype(x.dtype)

def modulate(xn, shift, scale):
    return xn * (1 + scale[:, None, :]) + shift[:, None, :]

def rope(x, pos):
    half = x.shape[-1] // 2
    inv = ROPE_THETA ** (-jnp.arange(half, dtype=jnp.float32) / half)
    ang = pos.astype(jnp.float32)[:, :, None] * inv
    cos = jnp.cos(ang)[:, :, None, :]
    sin = jnp.sin(ang)[:, :, None, :]
    xf = x.astype(jnp.float32)
    x1, x2 = xf[..., :half], xf[..., half:]
    return jnp.concatenate([x1 * cos - x2 * sin, x1 * sin + x2 * cos], axis=-1).astype(x.dtype)

def retention(q, k, v):
    B, S, H, dk = q.shape
    dv = v.shape[-1]
    n = S // CHUNK
    log_g = jnp.log1p(-(2.0 ** (-5.0 - jnp.arange(H, dtype=jnp.float32))))
    t = jnp.arange(CHUNK, dtype=jnp.float32)
    diff = t[:, None] - t[None, :]
    decay_intra = jnp.where(diff >= 0, jnp.exp(log_g[:, None, None] * jnp.maximum(diff, 0.0)), 0.0)
    decay_q = jnp.exp(log_g[:, None] * (t + 1.0))[None, :, :, None]
    decay_k = jnp.exp(log_g[:, None] * (CHUNK - 1.0 - t))[None, :, :, None]
    decay_chunk = jnp.exp(log_g * CHUNK)[None, :, None, None]

    def to_chunks(a):
        return a.reshape(B, n, CHUNK, H, a.shape[-1]).transpose(1, 0, 3, 2, 4)

    def step(state, inp):
        qc, kc, vc = inp
        inner = jnp.einsum('bhnd,bhmd->bhnm', qc, kc) * decay_intra
        out = jnp.einsum('bhnm,bhmv->bhnv', inner, vc) + \
            jnp.einsum('bhnd,bhdv->bhnv', qc, state) * decay_q
        state = state * decay_chunk + jnp.einsum('bhmd,bhmv->bhdv', kc * decay_k, vc)
        return state, out

    state0 = jnp.zeros((B, H, dk, dv), jnp.float32)
    _, o = lax.scan(step, state0, (to_chunks(q), to_chunks(k), to_chunks(v)))
    return o.transpose(1, 0, 3, 2, 4).reshape(B, S, H, dv)

def retention_mixer(xn, pos, w_in, w_out):
    B, S, _ = xn.shape
    proj = xn @ w_in
    q = proj[..., :D_MODEL].reshape(B, S, RET_HEADS, RET_DK)
    k = proj[..., D_MODEL:2 * D_MODEL].reshape(B, S, RET_HEADS, RET_DK)
    v = proj[..., 2 * D_MODEL:2 * D_MODEL + RET_V].reshape(B, S, RET_HEADS, RET_DV)
    g = proj[..., 2 * D_MODEL + RET_V:]
    q = rope(q, pos).astype(jnp.float32)
    k = rope(k, pos).astype(jnp.float32) * (RET_DK ** -0.5)
    o = retention(q, k, v.astype(jnp.float32))
    mu = jnp.mean(o, axis=-1, keepdims=True)
    var = jnp.mean(jnp.square(o - mu), axis=-1, keepdims=True)
    o = (o - mu) * lax.rsqrt(var + EPS)
    y = (jax.nn.silu(g.astype(jnp.float32)) * o.reshape(B, S, RET_V)).astype(xn.dtype)
    return y @ w_out

def mla_shared_kv(hn, pos, w_kv_a, kv_norm, w_kv_b):
    B, S, _ = hn.shape
    a = hn @ w_kv_a
    c_kv = rms_norm(a[..., :KV_LORA], kv_norm)
    k_rope = rope(a[..., KV_LORA:][:, :, None, :], pos)[:, :, 0, :]
    kv = (c_kv @ w_kv_b).reshape(B, S, MLA_HEADS, QK_NOPE + V_HEAD)
    return kv[..., :QK_NOPE], k_rope, kv[..., QK_NOPE:]

def mla_attention(xn, pos, w_q_a, q_norm, w_q_b, w_o, k_nope, k_rope, v):
    B, S, _ = xn.shape
    q = (rms_norm(xn @ w_q_a, q_norm) @ w_q_b).reshape(B, S, MLA_HEADS, QK_NOPE + QK_ROPE)
    q_nope = q[..., :QK_NOPE]
    q_rope = rope(q[..., QK_NOPE:], pos)
    scale = (QK_NOPE + QK_ROPE) ** -0.5
    nb = S // Q_BLOCK
    qn_b = q_nope.reshape(B, nb, Q_BLOCK, MLA_HEADS, QK_NOPE).transpose(1, 0, 2, 3, 4)
    qr_b = q_rope.reshape(B, nb, Q_BLOCK, MLA_HEADS, QK_ROPE).transpose(1, 0, 2, 3, 4)
    key_chunk = jnp.arange(S) // CHUNK

    def block(args):
        qn, qr, i = args
        s = (jnp.einsum('bqhd,bkhd->bhqk', qn, k_nope, preferred_element_type=jnp.float32)
             + jnp.einsum('bqhr,bkr->bhqk', qr, k_rope, preferred_element_type=jnp.float32)) * scale
        q_chunk = (i * Q_BLOCK + jnp.arange(Q_BLOCK)) // CHUNK
        mask = key_chunk[None, :] <= q_chunk[:, None]
        p = jax.nn.softmax(jnp.where(mask, s, -jnp.inf), axis=-1)
        return jnp.einsum('bhqk,bkhv->bqhv', p.astype(v.dtype), v)

    o = lax.map(block, (qn_b, qr_b, jnp.arange(nb)))
    o = o.transpose(1, 0, 2, 3, 4).reshape(B, S, MLA_HEADS * V_HEAD)
    return o @ w_o

def grouped_moe(xn, w_router, b_router, w_gate, w_up, w_down):
    B, S, D = xn.shape
    xt = xn.reshape(B * S, D)
    scores = jax.nn.sigmoid((xt @ w_router).astype(jnp.float32))
    biased = scores + b_router.astype(jnp.float32)
    grouped = biased.reshape(-1, N_GROUPS, EXPERTS_PER_GROUP)
    group_score = lax.top_k(grouped, TOP_K)[0].sum(-1)
    g_sel = jnp.argmax(group_score, axis=-1)
    in_group = jnp.take_along_axis(grouped, g_sel[:, None, None], axis=1)[:, 0]
    _, local = lax.top_k(in_group, TOP_K)
    idx = g_sel[:, None] * EXPERTS_PER_GROUP + local
    w = jnp.take_along_axis(scores, idx, axis=-1)
    w = w / jnp.sum(w, axis=-1, keepdims=True)
    combine = jnp.sum(jax.nn.one_hot(idx, N_EXPERTS, dtype=jnp.float32) * w[..., None], axis=1)
    y = jnp.zeros((B * S, D), jnp.float32)
    for e in range(N_EXPERTS):
        hdn = jax.nn.silu(xt @ w_gate[e]) * (xt @ w_up[e])
        y = y + combine[:, e:e + 1] * (hdn @ w_down[e]).astype(jnp.float32)
    return y.astype(xn.dtype).reshape(B, S, D)

def setup_inputs(seed: int = 0) -> dict:
    key = jax.random.key(seed)
    ks = jax.random.split(key, 32)
    f32 = jnp.float32
    D = D_MODEL

    def nrm(k, shape, fan_in, mult=1.0):
        return jax.random.normal(k, shape, f32) * (mult * fan_in ** -0.5)

    def gain(k, shape):
        return 1.0 + 0.02 * jax.random.normal(k, shape, f32)

    offset = jax.random.randint(ks[2], (BATCH, 1), 0, 4096, dtype=jnp.int32)
    positions = offset + jnp.arange(SEQ, dtype=jnp.int32)[None, :]
    return {
        "x": jax.random.normal(ks[0], (BATCH, SEQ, D), f32),
        "c": jax.random.normal(ks[1], (BATCH, D), f32),
        "positions": positions,
        "w_mod": nrm(ks[3], (DEPTH, D, 6 * D), D, 0.5),
        "b_mod": 0.02 * jax.random.normal(ks[4], (DEPTH, 6 * D), f32),
        "norm_mix": gain(ks[5], (DEPTH, D)),
        "norm_ffn": gain(ks[6], (DEPTH, D)),
        "ret_w_in": nrm(ks[7], (N_A, D, 2 * D + 2 * RET_V), D),
        "ret_w_out": nrm(ks[8], (N_A, RET_V, D), RET_V),
        "w_mod_kv": nrm(ks[9], (D, 2 * D), D, 0.5),
        "b_mod_kv": 0.02 * jax.random.normal(ks[10], (2 * D,), f32),
        "norm_kv": gain(ks[11], (D,)),
        "mla_w_kv_a": nrm(ks[12], (D, KV_LORA + QK_ROPE), D),
        "mla_kv_norm": gain(ks[13], (KV_LORA,)),
        "mla_w_kv_b": nrm(ks[14], (KV_LORA, MLA_HEADS * (QK_NOPE + V_HEAD)), KV_LORA),
        "mla_w_q_a": nrm(ks[15], (N_B, D, Q_LORA), D),
        "mla_q_norm": gain(ks[16], (N_B, Q_LORA)),
        "mla_w_q_b": nrm(ks[17], (N_B, Q_LORA, MLA_HEADS * (QK_NOPE + QK_ROPE)), Q_LORA),
        "mla_w_o": nrm(ks[18], (N_B, MLA_HEADS * V_HEAD, D), MLA_HEADS * V_HEAD),
        "router_w": nrm(ks[19], (D, N_EXPERTS), D),
        "router_b": 0.01 * jax.random.normal(ks[20], (N_EXPERTS,), f32),
        "moe_w_gate": nrm(ks[21], (DEPTH, N_EXPERTS, D, D_EXPERT), D),
        "moe_w_up": nrm(ks[22], (DEPTH, N_EXPERTS, D, D_EXPERT), D),
        "moe_w_down": nrm(ks[23], (DEPTH, N_EXPERTS, D_EXPERT, D), D_EXPERT),
        "final_norm": gain(ks[24], (D,)),
    }

def reference(x, c, positions, w_mod, b_mod, norm_mix, norm_ffn, ret_w_in, ret_w_out,
              w_mod_kv, b_mod_kv, norm_kv, mla_w_kv_a, mla_kv_norm, mla_w_kv_b,
              mla_w_q_a, mla_q_norm, mla_w_q_b, mla_w_o, router_w, router_b,
              moe_w_gate, moe_w_up, moe_w_down, final_norm):
    c_act = jax.nn.silu(c)
    h = x
    k_nope = k_rope = v_shared = None
    for layer in range(DEPTH):
        mod = c_act @ w_mod[layer] + b_mod[layer]
        sh1, sc1, g1, sh2, sc2, g2 = jnp.split(mod, 6, axis=-1)
        if layer < N_A:
            xn = modulate(rms_norm(h, norm_mix[layer]), sh1, sc1)
            mix = retention_mixer(xn, positions, ret_w_in[layer], ret_w_out[layer])
        else:
            if layer == N_A:
                kv_mod = c_act @ w_mod_kv + b_mod_kv
                sh_kv, sc_kv = jnp.split(kv_mod, 2, axis=-1)
                hn = modulate(rms_norm(h, norm_kv), sh_kv, sc_kv)
                k_nope, k_rope, v_shared = mla_shared_kv(hn, positions, mla_w_kv_a, mla_kv_norm, mla_w_kv_b)
            j = layer - N_A
            xn = modulate(rms_norm(h, norm_mix[layer]), sh1, sc1)
            mix = mla_attention(xn, positions, mla_w_q_a[j], mla_q_norm[j], mla_w_q_b[j], mla_w_o[j],
                                k_nope, k_rope, v_shared)
        h = h + g1[:, None, :] * mix
        xn = modulate(rms_norm(h, norm_ffn[layer]), sh2, sc2)
        h = h + g2[:, None, :] * grouped_moe(xn, router_w, router_b, moe_w_gate[layer],
                                             moe_w_up[layer], moe_w_down[layer])
    return rms_norm(h, final_norm)


_drawn_inputs = setup_inputs


def setup_inputs(seed=0):
    import zlib

    import numpy as np

    out = dict(_drawn_inputs(seed))
    spreads = {}
    factors = {'b_mod_kv': 4.69,
     'norm_kv': 8.0,
     'mla_kv_norm': 8.0,
     'mla_q_norm': 8.0,
     'final_norm': 2.86}
    for name, (base, spread) in spreads.items():
        noise = np.random.default_rng([zlib.crc32(name.encode()), seed]).standard_normal(out[name].shape)
        drawn = base * np.exp(spread * noise) if base else spread * noise
        out[name] = __import__('jax').numpy.asarray(drawn.astype(out[name].dtype))
    for name, factor in factors.items():
        out[name] = (out[name] * factor).astype(out[name].dtype)
    return out
```

```python
from contextlib import ExitStack

import numpy as np

import concourse.bass as bass
from concourse import mybir

F32 = mybir.dt.float32
I32 = mybir.dt.int32
ALU = mybir.AluOpType
ACT = mybir.ActivationFunctionType
AX = mybir.AxisListType

P = 128
D = 1024
KT = D // P
SEQ = 256
TT = SEQ // P
EPS = 1e-6
RH, RDK, RDV = 4, 256, 512
MH, NOPE, ROPE, VH = 8, 128, 64, 128
HALF = ROPE // 2
QL, KVL = 256, 128
NE, NG, EG = 16, 4, 4
DE = 512
PAIRS = NE // 2
SLOTS = 64
ROUNDS = SEQ // SLOTS
CH = 64
SOFT = float(NOPE + ROPE) ** -0.5
RING = 6

C_IDENT = 0
C_TRI = C_IDENT + P
C_ONES = C_TRI + P
C_SEL = C_ONES + P
C_SLOT = C_SEL + P
C_EARLIER = C_SLOT + SLOTS
C_FREQ = C_EARLIER + EG * EG
C_DECAY = C_FREQ + 2
C_ALL = C_DECAY + RH * SEQ


def constants():
    c = np.zeros((P, C_ALL), np.float32)
    i = np.arange(P)
    c[:, C_IDENT:C_IDENT + P] = np.eye(P)
    c[:, C_TRI:C_TRI + P] = i[:, None] < i[None, :]
    c[:, C_ONES:C_ONES + P] = 1
    c[::32, C_SEL:C_SEL + P] = 1
    c[:, C_SLOT:C_SLOT + SLOTS] = np.arange(SLOTS)
    j = np.arange(EG)
    c[:, C_EARLIER:C_EARLIER + EG * EG] = (j[None, :] < j[:, None]).reshape(-1)
    c[:, C_FREQ] = 10000.0 ** (-i / P)
    c[:, C_FREQ + 1] = np.tile(10000.0 ** (-i[:HALF] / HALF), P // HALF)
    n = np.arange(SEQ)
    for h in range(RH):
        g = np.log1p(-(2.0 ** (-5.0 - h)))
        d = n[None, :] - i[:, None]
        c[:, C_DECAY + h * SEQ:C_DECAY + (h + 1) * SEQ] = np.where(d >= 0, np.exp(g * np.maximum(d, 0)), 0) * RDK ** -0.5
    return c


MOD = [(0, b) for b in range(12)] + [(2, b) for b in range(4)] + [(1, b) for b in range(12)]
FIRST_MOD = 4
MOD_COL = {0: 0, 1: 48, 2: 96}
GATES = {(0, 4): 0, (0, 5): 0, (0, 10): 1, (0, 11): 1, (1, 4): 2, (1, 5): 2, (1, 10): 3, (1, 11): 3}
WIN = [0, 2, 1, 3] + [b for h in range(RH) for b in (4 + h, 8 + h)]

STREAM = [("mod", m) for m in range(FIRST_MOD)]
for _r in range(12):
    STREAM += [("win", _r), ("mod", FIRST_MOD + 2 * _r), ("mod", FIRST_MOD + 2 * _r + 1)]
STREAM += [("wout", i) for i in range(4)]
N_RET = len(STREAM)
MOE_AT = [N_RET, N_RET + 6 * PAIRS + 6]
MLA_AT = N_RET + 6 * PAIRS
MLA_ITEMS = ["kva", "qa", "kvb", "qb", "wo0", "wo1"]
AT = {item: i for i, item in enumerate(STREAM)}
AT.update({(name, 0): MLA_AT + i for i, name in enumerate(MLA_ITEMS)})


def build_kernel(nc, t, out):
    with ExitStack() as ctx:
        def sb(name, shape, dt=F32):
            return ctx.enter_context(nc.sbuf_tensor(name, shape, dt))

        def sem(name):
            return ctx.enter_context(nc.semaphore(name))

        ring = sb("ring", [P, RING, 4096])
        h = sb("h", [P, TT, D])
        y = sb("y", [P, TT, D])
        xnT = sb("xnT", [P, KT, SEQ])
        acc = sb("acc", [P, TT, D])
        gate = sb("gate", [P, 4, D])
        part = sb("part", [P, 2, 512])
        cst = sb("cst", [P, C_ALL])
        rows = sb("rows", [120, P])
        gains = sb("gains", [43, P])
        cols = sb("cols", [P, 120])
        gcol = sb("gcol", [P, 43])
        cact = sb("cact", [P, KT, 32])
        cs1 = sb("cs1", [P, KT])
        modc = sb("modc", [P, 112])
        scale = sb("scale", [P, 5, KT])
        wr = sb("wr", [P, KT, NE])
        br = sb("br", [P, NE])
        stat = sb("stat", [P, 32])
        msq, var, root, rstd = stat[:, 0:4], stat[:, 4:8], stat[:, 8:12], stat[:, 12:16]
        mv = stat[:, 16:20].rearrange("p (t s) -> p t s", t=2)
        bn = sb("bn", [P, 2, 6])
        score = sb("score", [P, TT, NE])
        biased = sb("biased", [P, TT, NE])
        cmp1 = sb("cmp1", [P, TT * NG * EG * EG])
        cmp2 = sb("cmp2", [P, TT * NG * EG * EG])
        chosen = sb("chosen", [P, TT, NE])
        rank = sb("rank", [P, TT * NE])
        gsum = sb("gsum", [P, TT * NG])
        grank = sb("grank", [P, TT * NG])
        den = sb("den", [P, TT])
        combine = sb("combine", [P, TT, NE])
        place = sb("place", [P, TT, NE])
        most = sb("most", [P, 3, PAIRS])
        bounds = [sb(f"bounds{l}", [P, 16], I32) for l in range(2)]
        boundf = sb("boundf", [P, 16])
        slot_id = sb("slot_id", [P, SLOTS])

        arena = sb("arena", [P, 11800])
        at = [0]

        def take(n):
            at[0] += n
            assert at[0] <= 11800, at[0]
            return arena[:, at[0] - n:at[0]]

        trig = take(1024).rearrange("p (w f s) -> p w f s", w=2, f=2)
        kept = at[0]
        qT = take(2048).rearrange("p (k s) -> p k s", s=SEQ)
        kT = take(2048).rearrange("p (k s) -> p k s", s=SEQ)
        vh = take(2048).rearrange("p (b t n) -> p b t n", b=2, t=TT)
        inner = take(384)
        prod = take(1024).rearrange("p (f s) -> p f s", f=2)
        on, sg = acc[:, :, 0:512], acc[:, :, 512:1024]
        yTs = [y[:].rearrange("p t d -> p (t d)").rearrange("p (k s) -> p k s", s=SEQ),
               take(2048).rearrange("p (k s) -> p k s", s=SEQ)]

        def yT(k):
            return yTs[k // 8][:, k % 8, :]

        ang, turns, rem, crem = (qT[:, 2 * i:2 * i + 2, :] for i in range(4))
        posi = kT[:, 0, :].bitcast(I32)
        posf = kT[:, 1, :]
        at[0] = kept
        xgT = take(1024).rearrange("p (k s) -> p k s", s=P)
        sil = take(DE)
        hid = take(DE)
        hidT = take(DE).rearrange("p (k s) -> p k s", s=P)
        yg = take(D)
        pick = take(256).rearrange("p (t s) -> p t s", t=TT)
        pickw = take(256).rearrange("p (t s) -> p t s", t=TT)
        pickwT = take(256).rearrange("p (t s) -> p t s", t=TT)
        at[0] = kept
        hnT = take(2048).rearrange("p (k s) -> p k s", s=SEQ)
        oT = hnT
        knT = take(2048).rearrange("p (k s) -> p k s", s=SEQ)
        vm = take(2048).rearrange("p (t n) -> p t n", t=TT)
        qnT = take(2048).rearrange("p (k s) -> p k s", s=SEQ)
        ckT = take(256)
        qaT = take(512).rearrange("p (k s) -> p k s", s=SEQ)
        krT = take(512).rearrange("p (f s) -> p f s", f=2)
        qrT = take(1024).rearrange("p (f g s) -> p f g s", f=2, g=2)
        mprod = acc[:].rearrange("p t d -> p (t d)").rearrange("p (i s) -> p i s", i=4)
        cn = take(256).rearrange("p (t n) -> p t n", t=TT)
        qn = xnT[:, 0:2, :]
        prob, probT = y[:, :, 0:384], y[:, :, 384:768]
        smax = take(4).rearrange("p (b n) -> p b n", b=2)
        ssum = take(4).rearrange("p (b n) -> p b n", b=2)
        srec = take(4).rearrange("p (b n) -> p b n", b=2)

        bank = [ctx.enter_context(nc.psum_tensor(f"bank{i}", [P, 512], F32)) for i in range(8)]

        ident = cst[:, C_IDENT:C_IDENT + P]
        tri = cst[:, C_TRI:C_TRI + P]
        ones = cst[:, C_ONES:C_ONES + P]
        selm = cst[:, C_SEL:C_SEL + P]
        slots0 = cst[:, C_SLOT:C_SLOT + SLOTS]

        def tok(tt):
            return slice(tt * P, (tt + 1) * P)

        def slot(i):
            return ring[:, i % RING, :]

        kr_w = slot(MLA_AT)[:, 2048:4096].rearrange("p (f k n) -> p f k n", f=2, k=KT)
        qr_w = slot(MLA_AT + 3)[:, 3072:4096].rearrange("p (f k n) -> p f k n", f=2, k=2)

        landed = [sem(f"landed{i}") for i in range(RING)]
        wo_used = sem("wo_used")
        small_in, x_in, pos_in, cst_in, gb_in, fn_in = (
            sem(n) for n in ("small_in", "x_in", "pos_in", "cst_in", "gb_in", "fn_in"))
        rows_turned, cols_copied, c_silu, c_spread = (
            sem(n) for n in ("rows_turned", "cols_copied", "c_silu", "c_spread"))
        angles_ready, trig_ready = sem("angles_ready"), sem("trig_ready")
        dstep = sem("dstep")
        squares, meansq, roots, y_ready = (sem(n) for n in ("squares", "meansq", "roots", "y_ready"))
        y_turned, xn_dve, xn_act = sem("y_turned"), sem("xn_dve"), sem("xn_act")
        mod_sum, mod_copied, mod_folded, mod_stored = (
            sem(n) for n in ("mod_sum", "mod_copied", "mod_folded", "mod_stored"))
        win_done, rope_mult, rope_done, v_copied, g_silu = (
            sem(n) for n in ("win_done", "rope_mult", "rope_done", "v_copied", "g_silu"))
        ret_scores, inner_ready, o_done, o_var, o_root, o_norm, yh_ready, yh_turned, yT_copied = (
            sem(n) for n in ("ret_scores", "inner_ready", "o_done", "o_var", "o_root", "o_norm",
                             "yh_ready", "yh_turned", "yT_copied"))
        mix_done, h_prod, h_ready = sem("mix_done"), sem("h_prod"), sem("h_ready")
        logits, sig_ready, chosen_ready, ranked, bounds_ready = (
            sem(n) for n in ("logits", "sig_ready", "chosen_ready", "ranked", "bounds_ready"))
        stored = sem("stored")
        rope_w = sem("rope_w")
        ck_raw, kr_raw, qa_raw, lat_sq, lat_ms, lat_root, lat_norm, lat_turned, ckT_ready, qaT_ready = (
            sem(n) for n in ("ck_raw", "kr_raw", "qa_raw", "lat_sq", "lat_ms", "lat_root", "lat_norm",
                             "lat_turned", "ckT_ready", "qaT_ready"))
        kv_done, kv_act, kv_dve, qb_done, qb_act, qb_dve, kr_mult, kr_ready, qr_mult, qr_ready = (
            sem(n) for n in ("kv_done", "kv_act", "kv_dve", "qb_done", "qb_act", "qb_dve", "kr_mult",
                             "kr_ready", "qr_mult", "qr_ready"))
        att_score, att_max, att_exp, att_prob, prob_turned, probT_ready, att_o, oT_ready = (
            sem(n) for n in ("att_score", "att_max", "att_exp", "att_prob", "prob_turned",
                             "probT_ready", "att_o", "oT_ready"))
        MOE = ["slots_ready", "picked", "weights_turned", "gathered", "xg_dve", "xg_act", "pickwT_ready", "gate_done", "up_done",
               "sil_ready", "hid_ready", "hid_turned", "hidT_act", "hidT_dve", "down_done", "yg_ready",
               "comb_done", "acc_added"]
        moe = [{n: sem(f"{n}{l}") for n in MOE} for l in range(2)]

        class Count:

            def __init__(self, s):
                self.s, self.n = s, 0

            def step(self, eng, ins):
                self.n += 1
                ins.then_inc(self.s, 1)
                eng.wait_ge(self.s, self.n)

        block = ctx.enter_context(nc.Block())

        @block.sync
        def _(sp):
            sp.dma_start(h[:], t["x"].rearrange("b (t p) d -> p (b t) d", p=P)).then_inc(x_in, 16)

            def source(kind, n):
                if kind == "mod":
                    m, b = MOD[n]
                    w = t["w_mod_kv"] if m == 2 else t["w_mod"][m]
                    return w[:, b * 512:(b + 1) * 512].rearrange("(k p) n -> p k n", p=P)
                if kind == "win":
                    b = WIN[n]
                    return t["ret_w_in"][0, :, b * 512:(b + 1) * 512].rearrange("(k p) n -> p k n", p=P)
                if kind == "wout":
                    return t["ret_w_out"][0, n * 512:(n + 1) * 512, :].rearrange("(k p) n -> p k n", p=P)
                if kind == "kva":
                    return t["mla_w_kv_a"].rearrange("(k p) n -> p k n", p=P)
                if kind == "qa":
                    return t["mla_w_q_a"][0].rearrange("(k p) n -> p k n", p=P)
                if kind == "kvb":
                    return t["mla_w_kv_b"].rearrange("(k p) n -> p k n", p=P)
                if kind == "qb":
                    return t["mla_w_q_b"][0].rearrange("(k p) n -> p k n", p=P)
                n = int(kind[2])
                return t["mla_w_o"][0, n * 512:(n + 1) * 512, :].rearrange("(k p) n -> p k n", p=P)

            def load(i, src):
                k, n = src.shape[1], src.shape[2]
                dst = slot(i)[:, 0:k * n].rearrange("p (k n) -> p k n", k=k)
                sp.dma_start(dst, src).then_inc(landed[i % RING], 16)

            def experts(l, pair, before):
                base = MOE_AT[l]
                for j in range(6):
                    w = t[("moe_w_gate", "moe_w_up", "moe_w_down")[j // 2]][l]
                    w = w[bass.ds(pair * 2 + j % 2, 1)]
                    before(j)
                    load(base + j, w.rearrange("e (k p) n -> p (e k) n", p=P))

            def released(i):
                kind, n = STREAM[i] if i < N_RET else (MLA_ITEMS[i - MLA_AT], 0)
                s, v = {"mod": (mod_sum, n + 1), "win": (win_done, 2 * n + 2), "wout": (wo_used, n + 1),
                        "kva": (kr_raw, 1), "qa": (qa_raw, 1), "kvb": (kv_done, 8), "qb": (qb_done, 6),
                        "wo0": (wo_used, 4), "wo1": (mix_done, 8)}[kind]
                if (kind, n) == ("wout", 3):
                    s, v = mix_done, 4
                sp.wait_ge(s, v)

            for i, (kind, n) in enumerate(STREAM):
                if i >= RING:
                    released(i - RING)
                load(i, source(kind, n))
            for l in range(2):
                S = moe[l]
                base = MOE_AT[l]

                def first(j):
                    released(base - RING + j)

                experts(l, 0, first)
                sp.wait_ge(bounds_ready, l + 1)
                with sp.Fori(1, PAIRS) as pair:
                    begun = sp.value_load(bounds[l][0:1, bass.ds(pair, 1)], min_val=1, max_val=ROUNDS * PAIRS)

                    def rest(j):
                        if j == 0:
                            sp.wait_ge(S["gate_done"], begun)
                        if j == 2:
                            sp.wait_ge(S["up_done"], begun * 2)
                        if j == 4:
                            sp.wait_ge(S["down_done"], begun * 2)

                    experts(l, pair, rest)
                if l == 0:
                    total = sp.value_load(bounds[l][0:1, PAIRS:PAIRS + 1], min_val=PAIRS, max_val=ROUNDS * PAIRS)
                    for j, kind in enumerate(MLA_ITEMS):
                        if j == 0:
                            sp.wait_ge(S["gate_done"], total)
                        if j == 2:
                            sp.wait_ge(S["up_done"], total * 2)
                        if j == 4:
                            sp.wait_ge(S["down_done"], total * 2)
                        load(MLA_AT + j, source(kind, 0))
            for tt in range(TT):
                sp.wait_ge(h_ready, 16 + tt + 1)
                sp.dma_start(out[0, tok(tt), :], acc[:, tt, :]).then_inc(stored, 16)
            sp.wait_ge(stored, 16 * TT)

        @block.tensor
        def _(pe):
            def arrived(i, extra=None):
                v = 16 * (i // RING + 1)
                pe.wait_ge(landed[i % RING], v if extra is None else extra * 16 + v)

            def turn_y(n):
                for b in range(4):
                    for f in range(2):
                        for tt in range(TT):
                            if b == 0 and f == 0:
                                pe.wait_ge(y_ready, 2 * n + tt + 1)
                            k = 2 * b + f
                            ins = pe.transpose(bank[b][:, f * SEQ + tt * P:f * SEQ + (tt + 1) * P],
                                               y[:, tt, k * P:(k + 1) * P], ident)
                    ins.then_inc(y_turned, 1)

            pe.wait_ge(cst_in, 16)
            pe.wait_ge(small_in, 16 * 10)
            pe.transpose(bank[4][:, 0:120], rows[:], ident[0:120, 0:120]).then_inc(rows_turned, 1)
            pe.transpose(bank[5][:, 0:43], gains[:], ident[0:43, 0:43]).then_inc(rows_turned, 1)
            pe.wait_ge(c_spread, 1)

            def mod_main(m):
                i = AT[("mod", m)]
                w = slot(i).rearrange("p (k n) -> p k n", k=KT)
                arrived(i)
                if m == 0:
                    pe.wait_ge(cols_copied, 1)
                else:
                    pe.wait_ge(mod_copied, m)
                for k in range(KT):
                    g = k % 4
                    ins = pe.matmul(bank[4][32 * g:32 * g + 32, :], cact[:, k, :], w[:, k, :],
                                    start=(k < 4), stop=(k >= 4))
                ins.then_inc(mod_sum, 1)

            def mod_fold(m):
                pe.wait_ge(mod_copied, m + 1)
                if m == 0:
                    pe.wait_ge(cols_copied, 2)
                else:
                    pe.wait_ge(mod_stored, m)
                if MOD[m] in GATES:
                    ins = pe.matmul(bank[5][:], selm, part[:, m % 2, :], start=True, stop=True)
                else:
                    for j in range(4):
                        ins = pe.matmul(bank[5][:, j:j + 1], part[:, m % 2, j * P:(j + 1) * P],
                                        selm[:, 0:1], start=True, stop=True)
                ins.then_inc(mod_folded, 1)

            for m in range(FIRST_MOD):
                mod_main(m)
                if m:
                    mod_fold(m - 1)
            mod_fold(FIRST_MOD - 1)
            turn_y(0)

            def turn_head(hd, g):
                pe.wait_ge(yh_ready, 2 * hd + 2)
                if 2 * hd + g:
                    pe.wait_ge(yT_copied, 2 * hd + g)
                for j in range(2):
                    for tt in range(TT):
                        ins = pe.transpose(bank[7][:, (2 * j + tt) * P:(2 * j + tt + 1) * P],
                                           on[:, tt, (2 * g + j) * P:(2 * g + j + 1) * P], ident)
                ins.then_inc(yh_turned, 1)

            for r in range(12):
                i = AT[("win", r)]
                w = slot(i).rearrange("p (k n) -> p k n", k=KT)
                arrived(i)
                hd = (r - 4) // 2
                pair = (bank[0], bank[1]) if r % 2 == 0 else (bank[2], bank[3])
                if r == 0:
                    pe.wait_ge(xn_dve, 4)
                    pe.wait_ge(xn_act, 4)
                elif 2 <= r < 6:
                    pe.wait_ge(rope_mult, 2 * (r - 1))
                elif r >= 6 and r % 2 == 0:
                    pe.wait_ge(v_copied, 2 * hd)
                elif r >= 6:
                    pe.wait_ge(o_norm, 2 * hd)
                if r < 4:
                    for b in range(2):
                        for f in range(2):
                            c = (2 * b + f) * P
                            for k in range(KT):
                                ins = pe.matmul(pair[b][:, f * SEQ:(f + 1) * SEQ], w[:, k, c:c + P], xnT[:, k, :],
                                                start=(k == 0), stop=(k == KT - 1))
                        ins.then_inc(win_done, 1)
                else:
                    for tt in range(TT):
                        for k in range(KT):
                            ins = pe.matmul(pair[tt][:], xnT[:, k, tok(tt)], w[:, k, :],
                                            start=(k == 0), stop=(k == KT - 1))
                        ins.then_inc(win_done, 1)
                m0 = FIRST_MOD + 2 * r
                if r >= 4 and r % 2 == 0:
                    if hd:
                        turn_head(hd - 1, 0)
                    pe.wait_ge(rope_done, 8)
                    if hd:
                        pe.wait_ge(inner_ready, 2 * hd)
                    for f in range(2):
                        pe.matmul(bank[6][:, 0:SEQ], kT[:, 2 * hd + f, 0:P], qT[:, 2 * hd + f, :],
                                  start=(f == 0), stop=(f == 1))
                    for f in range(2):
                        ins = pe.matmul(bank[6][:, SEQ:SEQ + P], kT[:, 2 * hd + f, P:SEQ], qT[:, 2 * hd + f, P:SEQ],
                                        start=(f == 0), stop=(f == 1))
                    ins.then_inc(ret_scores, 1)
                mod_main(m0)
                if r:
                    mod_fold(m0 - 1)
                if r >= 4 and r % 2 == 0 and hd:
                    turn_head(hd - 1, 1)
                if r >= 4 and r % 2 == 1:
                    pe.wait_ge(g_silu, 2 * hd + 2)
                    pe.wait_ge(v_copied, 2 * hd + 2)
                    pe.wait_ge(inner_ready, 2 * hd + 2)
                    v = vh[:, hd % 2]
                    pe.matmul(bank[2][:], inner[:, 0:P], v[:, 0, :], start=True, stop=True).then_inc(o_done, 1)
                    pe.matmul(bank[3][:], inner[:, P:SEQ], v[:, 0, :], start=True, stop=False)
                    pe.matmul(bank[3][:], inner[:, SEQ:SEQ + P], v[:, 1, :], start=False, stop=True).then_inc(o_done, 1)
                mod_main(m0 + 1)
                mod_fold(m0)
            mod_fold(len(MOD) - 1)

            def wout(i, tt):
                it = AT[("wout", i)]
                w = slot(it).rearrange("p (k n) -> p k n", k=4)
                arrived(it)
                for n in range(2):
                    for kk in range(4):
                        ins = pe.matmul(bank[2 * tt + n][:], yT(4 * i + kk)[:, tok(tt)], w[:, kk, n * 512:(n + 1) * 512],
                                        start=(i == 0 and kk == 0), stop=(i == 3 and kk == 3))
                    if i == 3:
                        ins.then_inc(mix_done, 1)
                return ins

            pe.wait_ge(yT_copied, 6)
            for i in range(3):
                wout(i, 0)
            turn_head(3, 0)
            pe.wait_ge(o_norm, 8)
            wout(0, 1).then_inc(wo_used, 1)
            turn_head(3, 1)
            wout(1, 1).then_inc(wo_used, 1)
            wout(2, 1).then_inc(wo_used, 1)
            pe.wait_ge(yT_copied, 8)
            wout(3, 0)
            wout(3, 1)

            def experts(l):
                n = 1 + 2 * l
                S = moe[l]
                pe.wait_ge(h_prod, 8 * l + 4)
                turn_y(n)
                pe.wait_ge(xn_dve, 4 + 12 * l + 4)
                pe.wait_ge(xn_act, 4 + 12 * l + 4)
                for tt in range(TT):
                    for k in range(KT):
                        ins = pe.matmul(bank[4][:, tt * NE:(tt + 1) * NE], xnT[:, k, tok(tt)], wr[:, k, :],
                                        start=(k == 0), stop=(k == KT - 1))
                ins.then_inc(logits, 1)
                pe.wait_ge(chosen_ready, l + 1)
                pe.matmul(bank[5][:, 0:NE], tri, chosen[:, 0, :], start=True, stop=True)
                pe.matmul(bank[5][:, NE:2 * NE], ones, chosen[:, 0, :], start=True, stop=False)
                pe.matmul(bank[5][:, NE:2 * NE], tri, chosen[:, 1, :], start=False, stop=True)
                pe.matmul(bank[5][:, 2 * NE:3 * NE], ones, chosen[:, 0, :], start=True, stop=False)
                pe.matmul(bank[5][:, 2 * NE:3 * NE], ones, chosen[:, 1, :], start=False, stop=True).then_inc(ranked, 1)
                pe.wait_ge(bounds_ready, l + 1)
                base = MOE_AT[l]
                wv = [slot(base + j).rearrange("p (k n) -> p k n", k=(KT if j < 4 else 4)) for j in range(6)]
                with pe.Fori(0, PAIRS) as pair:
                    begin = pe.value_load(bounds[l][0:1, bass.ds(pair, 1)], min_val=0, max_val=ROUNDS * PAIRS)
                    end = pe.value_load(bounds[l][0:1, bass.ds(pair + 1, 1)], min_val=1, max_val=ROUNDS * PAIRS)
                    with pe.Fori(begin, end) as u:
                        pe.wait_ge(S["picked"], u * 2 + 1)
                        pe.wait_ge(S["acc_added"], u * 4 + 1)
                        for k in range(KT):
                            for tt in range(TT):
                                ins = pe.matmul(bank[2 + k // 4][:, (k % 4) * P:(k % 4 + 1) * P],
                                                y[:, tt, k * P:(k + 1) * P], pick[:, tt, :],
                                                start=(tt == 0), stop=(tt == TT - 1))
                            if k % 4 == 3:
                                ins.then_inc(S["gathered"], 1)
                        pe.wait_ge(S["picked"], u * 2 + 2)
                        for tt in range(TT):
                            ins = pe.transpose(bank[5][:, tok(tt)], pickw[:, tt, :], ident)
                        ins.then_inc(S["weights_turned"], 1)
                        arrived(base, pair)
                        arrived(base + 1, pair)
                        pe.wait_ge(S["xg_dve"], u + 1)
                        for k in range(KT):
                            if k == 4:
                                pe.wait_ge(S["xg_act"], u + 1)
                            for e in range(2):
                                ins = pe.matmul(bank[0][e * 64:(e + 1) * 64, :], xgT[:, k, e * 64:(e + 1) * 64],
                                                wv[e][:, k, :], start=(k == 0), stop=(k == KT - 1))
                        ins.then_inc(S["gate_done"], 1)
                        arrived(base + 2, pair)
                        arrived(base + 3, pair)
                        for f in range(2):
                            for k in range(KT):
                                for e in range(2):
                                    ins = pe.matmul(bank[(1, 6)[f]][e * 64:(e + 1) * 64, 0:256],
                                                    xgT[:, k, e * 64:(e + 1) * 64],
                                                    wv[2 + e][:, k, f * 256:(f + 1) * 256],
                                                    start=(k == 0), stop=(k == KT - 1))
                            ins.then_inc(S["up_done"], 1)
                        for f in range(2):
                            pe.wait_ge(S["hid_ready"], u * 2 + f + 1)
                            for j in range(2):
                                ins = pe.transpose(bank[(4, 7)[f]][:, j * P:(j + 1) * P],
                                                   hid[:, (2 * f + j) * P:(2 * f + j + 1) * P], ident)
                            ins.then_inc(S["hid_turned"], 1)
                        arrived(base + 4, pair)
                        arrived(base + 5, pair)
                        pe.wait_ge(S["hidT_act"], u + 1)
                        pe.wait_ge(S["hidT_dve"], u + 1)
                        for n2 in range(2):
                            for k in range(4):
                                for e in range(2):
                                    ins = pe.matmul(bank[6 + n2][e * 64:(e + 1) * 64, :],
                                                    hidT[:, k, e * 64:(e + 1) * 64],
                                                    wv[4 + e][:, k, n2 * 512:(n2 + 1) * 512],
                                                    start=(k == 0), stop=(k == 3))
                            ins.then_inc(S["down_done"], 1)
                        pe.wait_ge(S["pickwT_ready"], u + 1)
                        for n2 in range(2):
                            pe.wait_ge(S["yg_ready"], u * 2 + n2 + 1)
                            for tt in range(TT):
                                pe.matmul(bank[(2, 3, 0, 1)[2 * n2 + tt]][:], pickwT[:, tt, :],
                                          yg[:, n2 * 512:(n2 + 1) * 512], start=True, stop=True).then_inc(S["comb_done"], 1)

            experts(0)

            pe.wait_ge(h_ready, 8)
            turn_y(2)

            def item(name, k):
                i = AT[(name, 0)]
                arrived(i)
                return slot(i)

            kva = item("kva", 0)[:, 0:KT * 192].rearrange("p (k n) -> p k n", k=KT)
            pe.wait_ge(xn_dve, 12)
            pe.wait_ge(xn_act, 12)
            for tt in range(TT):
                for k in range(KT):
                    ins = pe.matmul(bank[4][:, tt * KVL:(tt + 1) * KVL], hnT[:, k, tok(tt)], kva[:, k, 0:KVL],
                                    start=(k == 0), stop=(k == KT - 1))
            ins.then_inc(ck_raw, 1)
            for f in range(2):
                pe.wait_ge(rope_w, f + 1)
                for k in range(KT):
                    ins = pe.matmul(bank[5][:, f * SEQ:(f + 1) * SEQ], kr_w[:, f, k, :], hnT[:, k, :],
                                    start=(k == 0), stop=(k == KT - 1))
            ins.then_inc(kr_raw, 1)
            qa = item("qa", 0)[:, 0:KT * QL].rearrange("p (k n) -> p k n", k=KT)
            pe.wait_ge(xn_dve, 16)
            pe.wait_ge(xn_act, 16)
            for tt in range(TT):
                for k in range(KT):
                    ins = pe.matmul(bank[6][:, tt * QL:(tt + 1) * QL], xnT[:, k, tok(tt)], qa[:, k, :],
                                    start=(k == 0), stop=(k == KT - 1))
            ins.then_inc(qa_raw, 1)
            pe.wait_ge(lat_norm, 2)
            for tt in range(TT):
                ins = pe.transpose(bank[7][:, tok(tt)], cn[:, tt, :], ident)
            ins.then_inc(lat_turned, 1)
            pe.wait_ge(lat_norm, 4)
            for j in range(2):
                for tt in range(TT):
                    ins = pe.transpose(bank[0][:, (2 * j + tt) * P:(2 * j + tt + 1) * P], qn[:, tt, j * P:(j + 1) * P], ident)
            ins.then_inc(lat_turned, 1)
            kvb = item("kvb", 0)[:, 0:2048].rearrange("p (h n) -> p h n", h=MH)
            pe.wait_ge(ckT_ready, 1)
            for b in range(4):
                for j in range(2):
                    ins = pe.matmul(bank[1 + b][:, j * SEQ:(j + 1) * SEQ], kvb[:, 2 * b + j, 0:NOPE], ckT, start=True, stop=True)
                ins.then_inc(kv_done, 1)
            pe.wait_ge(kr_mult, 2)
            pe.wait_ge(qaT_ready, 2)
            for tt in range(TT):
                for n in range(2):
                    b = (5, 6, 7, 0)[2 * tt + n]
                    ins = pe.matmul(bank[b][:], ckT[:, tok(tt)], kvb[:, 4 * n:4 * n + 4, NOPE:NOPE + VH], start=True, stop=True)
                    ins.then_inc(kv_done, 1)
            qb = item("qb", 0)[:, 0:2 * 1536].rearrange("p (k h n) -> p k h n", k=2, h=MH)
            for b in range(4):
                if b % 2 == 0:
                    pe.wait_ge(kv_act, b // 2 + 1)
                else:
                    pe.wait_ge(kv_dve, b // 2 + 1)
                for j in range(2):
                    for k in range(2):
                        ins = pe.matmul(bank[1 + b][:, j * SEQ:(j + 1) * SEQ], qb[:, k, 2 * b + j, 0:NOPE], qaT[:, k, :],
                                        start=(k == 0), stop=(k == 1))
                ins.then_inc(qb_done, 1)
            pe.wait_ge(kv_act, 4)
            pe.wait_ge(kv_dve, 4)
            for f in range(2):
                pe.wait_ge(rope_w, 3 + f)
                for g in range(2):
                    for k in range(2):
                        ins = pe.matmul(bank[5 + f][:, g * SEQ:(g + 1) * SEQ],
                                        qr_w[:, f, k, g * P:(g + 1) * P],
                                        qaT[:, k, :], start=(k == 0), stop=(k == 1))
                ins.then_inc(qb_done, 1)

            def scores(hd):
                b = bank[(7, 0)[hd % 2]]
                if hd >= 2:
                    pe.wait_ge(att_exp, 2 * (hd - 1))
                q = 32 * (hd % 4)
                for tt in range(TT):
                    o = b[:, 0:P] if tt == 0 else b[:, P:P + SEQ]
                    keys = slice(0, P * (tt + 1))
                    pe.matmul(o, qnT[:, hd, tok(tt)], knT[:, hd, keys], start=True, stop=False)
                    for f in range(2):
                        ins = pe.matmul(o, qrT[q:q + HALF, f, hd // 4, tok(tt)], krT[q:q + HALF, f, keys],
                                        start=False, stop=(f == 1), tile_position=(q, 0))
                ins.then_inc(att_score, 1)

            def turn_probs(hd):
                b = bank[1 + hd % 2]
                pe.wait_ge(att_prob, 2 * (hd + 1))
                if hd >= 2:
                    pe.wait_ge(probT_ready, hd - 1)
                for j in range(3):
                    ins = pe.transpose(b[:, tok(j)], prob[:, hd % 2, tok(j)], ident)
                ins.then_inc(prob_turned, 1)

            def attend(hd):
                b = bank[3 + hd % 2]
                pe.wait_ge(probT_ready, hd + 1)
                if hd >= 2:
                    pe.wait_ge(oT_ready, hd - 1)
                v = vm[:, :, hd * VH:(hd + 1) * VH]
                pe.matmul(b[:, 0:P], v[:, 0, :], probT[:, hd % 2, 0:P], start=True, stop=True)
                pe.matmul(b[:, P:SEQ], v[:, 0, :], probT[:, hd % 2, P:SEQ], start=True, stop=False)
                pe.matmul(b[:, P:SEQ], v[:, 1, :], probT[:, hd % 2, SEQ:SEQ + P], start=False, stop=True).then_inc(att_o, 1)

            pe.wait_ge(qb_act, 2)
            pe.wait_ge(qb_dve, 2)
            pe.wait_ge(qr_ready, 2)
            pe.wait_ge(kr_ready, 2)
            scores(0)
            for hd in range(MH):
                if hd + 1 < MH:
                    scores(hd + 1)
                turn_probs(hd)
                if hd:
                    attend(hd - 1)
            attend(MH - 1)
            pe.wait_ge(att_exp, 2 * MH)
            pe.wait_ge(oT_ready, MH)
            for i in range(2):
                w = item(f"wo{i}", 0).rearrange("p (k n) -> p k n", k=4)
                for tt in range(TT):
                    for n in range(2):
                        for kk in range(4):
                            ins = pe.matmul(bank[(5, 6, 7, 0)[2 * tt + n]][:], oT[:, 4 * i + kk, tok(tt)],
                                            w[:, kk, n * 512:(n + 1) * 512],
                                            start=(i == 0 and kk == 0), stop=(i == 1 and kk == 3))
                        if i == 1:
                            ins.then_inc(mix_done, 1)
                        elif tt == 1 and n == 1:
                            ins.then_inc(wo_used, 1)
            experts(1)

        @block.scalar
        def _(act):
            A = act.activation
            act.dma_start(cst[:], t["constants"]).then_inc(cst_in, 16)
            bm = t["b_mod"].rearrange("l (r c) -> l r c", c=P)
            act.dma_start(rows[0:8, :], t["c"].rearrange("b (r c) -> (b r) c", c=P)).then_inc(small_in, 16)
            act.dma_start(rows[8:56, :], bm[0]).then_inc(small_in, 16)
            act.dma_start(rows[56:104, :], bm[1]).then_inc(small_in, 16)
            act.dma_start(rows[104:120, :], t["b_mod_kv"].rearrange("(r c) -> r c", c=P)).then_inc(small_in, 16)
            act.dma_start(gains[0:16, :], t["norm_mix"].rearrange("l (r c) -> (l r) c", c=P)).then_inc(small_in, 16)
            act.dma_start(gains[16:32, :], t["norm_ffn"].rearrange("l (r c) -> (l r) c", c=P)).then_inc(small_in, 16)
            act.dma_start(gains[32:40, :], t["norm_kv"].rearrange("(r c) -> r c", c=P)).then_inc(small_in, 16)
            act.dma_start(gains[40:41, :], t["mla_kv_norm"].rearrange("(r c) -> r c", c=P)).then_inc(small_in, 16)
            act.dma_start(gains[41:43, :], t["mla_q_norm"].rearrange("l (r c) -> (l r) c", c=P)).then_inc(small_in, 16)
            act.dma_start(wr[:], t["router_w"].rearrange("(k p) n -> p k n", p=P)).then_inc(small_in, 16)
            act.dma_start(posi, t["positions"].to_broadcast([P, SEQ])).then_inc(pos_in, 16)
            act.dma_start(br[:], t["router_b"].unsqueeze(0).to_broadcast([P, NE])).then_inc(gb_in, 16)
            for i, (l, g) in enumerate(((0, 2), (0, 5), (1, 2), (1, 5))):
                act.dma_start(gate[:, i, :], t["b_mod"][l:l + 1, g * D:(g + 1) * D].to_broadcast([P, D])).then_inc(gb_in, 16)

            def squares_of(n):
                for tt in range(TT):
                    if n:
                        act.wait_ge(h_ready, 4 * (n - 1) + 2 * (tt + 1))
                    else:
                        act.wait_ge(x_in, 16)
                    A(y[:, tt, :], h[:, tt, :], ACT.Square, accum_out=msq[:, tt:tt + 1]).then_inc(squares, 1)
                act.wait_ge(meansq, n + 1)
                A(root[:, 0:2], var[:, 0:2], ACT.Sqrt).then_inc(roots, 1)

            def modulate(n, dst, which, shift):
                for b in (1, 3):
                    act.wait_ge(y_turned, 4 * n + b + 1)
                    for f in range(2):
                        k = 2 * b + f
                        A(dst[:, k, :], bank[b][:, f * SEQ:(f + 1) * SEQ], ACT.Identity,
                          bias=modc[:, shift + k:shift + k + 1],
                          scale=scale[:, which, k:k + 1]).then_inc(xn_act, 1)

            squares_of(0)
            act.wait_ge(cols_copied, 1)
            A(cs1[:], cols[:, 0:8], ACT.Silu).then_inc(c_silu, 1)
            act.wait_ge(angles_ready, 2)
            A(trig[:, :, 1, :], rem, ACT.Sin).then_inc(trig_ready, 1)
            A(trig[:, :, 0, :], crem, ACT.Sin).then_inc(trig_ready, 1)

            def mod_copy(m):
                act.wait_ge(mod_sum, m + 1)
                if m >= 2:
                    act.wait_ge(mod_folded, m - 1)
                A(part[:, m % 2, :], bank[4][:], ACT.Copy).then_inc(mod_copied, 1)

            def copy_head(hd, g):
                act.wait_ge(yh_turned, 2 * hd + g + 1)
                k = 4 * hd + 2 * g
                A(yTs[k // 8][:, k % 8:k % 8 + 2, :], bank[7][:].rearrange("p (k s) -> p k s", k=2),
                  ACT.Copy).then_inc(yT_copied, 1)

            for m in range(FIRST_MOD):
                mod_copy(m)
            act.wait_ge(dstep, D_SCALE0[0])
            modulate(0, xnT, 0, MOD_COL[0])
            for r in range(12):
                hd = (r - 4) // 2
                m0 = FIRST_MOD + 2 * r
                if r >= 4 and r % 2 == 0:
                    for tt in range(TT):
                        act.wait_ge(win_done, 2 * r + tt + 1)
                        if hd >= 2:
                            act.wait_ge(o_done, 2 * (hd - 1))
                        A(vh[:, hd % 2, tt, :], bank[tt][:], ACT.Copy).then_inc(v_copied, 1)
                    if hd:
                        copy_head(hd - 1, 0)
                if r >= 4 and r % 2 == 1:
                    for tt in range(TT):
                        act.wait_ge(win_done, 2 * r + tt + 1)
                        if hd:
                            act.wait_ge(yh_ready, 2 * hd)
                        A(sg[:, tt, :], bank[2 + tt][:], ACT.Silu).then_inc(g_silu, 1)
                mod_copy(m0)
                if r >= 4 and r % 2 == 0 and hd:
                    copy_head(hd - 1, 1)
                mod_copy(m0 + 1)
                if r >= 4 and r % 2 == 1:
                    act.wait_ge(o_var, hd + 1)
                    A(root[:, 0:2], var[:, 0:2], ACT.Sqrt).then_inc(o_root, 1)
            copy_head(3, 0)
            copy_head(3, 1)

            def experts(l):
                n = 1 + 2 * l
                S = moe[l]
                squares_of(n)
                modulate(n, xnT, 1 + 2 * l, MOD_COL[l] + 24)
                act.wait_ge(logits, l + 1)
                A(score[:].rearrange("p t e -> p (t e)"), bank[4][:, 0:TT * NE], ACT.Sigmoid).then_inc(sig_ready, 1)
                act.wait_ge(bounds_ready, l + 1)
                with act.Fori(0, PAIRS) as pair:
                    begin = act.value_load(bounds[l][0:1, bass.ds(pair, 1)], min_val=0, max_val=ROUNDS * PAIRS)
                    end = act.value_load(bounds[l][0:1, bass.ds(pair + 1, 1)], min_val=1, max_val=ROUNDS * PAIRS)
                    with act.Fori(begin, end) as u:
                        act.wait_ge(S["gathered"], u * 2 + 2)
                        for j in range(4):
                            k = 4 + j
                            ins = A(xgT[:, k, :], bank[3][:, tok(j)], ACT.Identity,
                                    bias=modc[:, MOD_COL[l] + 24 + k:MOD_COL[l] + 25 + k],
                                    scale=scale[:, 1 + 2 * l, k:k + 1])
                        ins.then_inc(S["xg_act"], 1)
                        act.wait_ge(S["weights_turned"], u + 1)
                        A(pickwT.rearrange("p t s -> p (t s)"), bank[5][:, 0:SEQ], ACT.Copy).then_inc(S["pickwT_ready"], 1)
                        act.wait_ge(S["gate_done"], u + 1)
                        A(sil, bank[0][:], ACT.Silu).then_inc(S["sil_ready"], 1)
                        act.wait_ge(S["hid_turned"], u * 2 + 1)
                        A(hidT[:, 0:2, :], bank[4][:, 0:SEQ].rearrange("p (k s) -> p k s", k=2), ACT.Copy).then_inc(S["hidT_act"], 1)
                        for n2 in range(2):
                            act.wait_ge(S["down_done"], u * 2 + n2 + 1)
                            A(yg[:, n2 * 512:(n2 + 1) * 512], bank[6 + n2][:], ACT.Copy).then_inc(S["yg_ready"], 1)

            experts(0)
            act.dma_start(gate[:, 0, :], t["final_norm"].unsqueeze(0).to_broadcast([P, D])).then_inc(fn_in, 16)
            squares_of(2)
            modulate(2, hnT, 4, MOD_COL[2])
            modulate(2, xnT, 2, MOD_COL[1])
            for tt in range(TT):
                act.wait_ge(ck_raw, 1)
                A(cn[:, tt, :], bank[4][:, tt * KVL:(tt + 1) * KVL], ACT.Square, accum_out=msq[:, tt:tt + 1]).then_inc(lat_sq, 1)
            for tt in range(TT):
                act.wait_ge(qa_raw, 1)
                A(qn[:, tt, :], bank[6][:, tt * QL:(tt + 1) * QL], ACT.Square, accum_out=msq[:, 2 + tt:3 + tt]).then_inc(lat_sq, 1)
            act.wait_ge(lat_ms, 2)
            A(root[:, 0:4], var[:, 0:4], ACT.Sqrt).then_inc(lat_root, 1)
            act.wait_ge(lat_turned, 1)
            A(ckT, bank[7][:, 0:SEQ], ACT.Copy, scale=gcol[:, 40:41]).then_inc(ckT_ready, 1)
            for b in (1, 3):
                act.wait_ge(kv_done, b)
                A(knT[:, 2 * (b - 1):2 * b, :], bank[b][:].rearrange("p (k s) -> p k s", k=2), ACT.Copy).then_inc(kv_act, 1)
            for b in (0, 2):
                act.wait_ge(kv_done, 4 + b + 1)
                A(vm[:, b // 2, 0:512], bank[5 + b][:], ACT.Copy).then_inc(kv_act, 1)
            for b in (1, 3):
                act.wait_ge(qb_done, b)
                A(qnT[:, 2 * (b - 1):2 * b, :], bank[b][:].rearrange("p (k s) -> p k s", k=2), ACT.Copy).then_inc(qb_act, 1)

            def head_exp(hd):
                act.wait_ge(att_max, 2 * (hd + 1))
                if hd >= 2:
                    act.wait_ge(prob_turned, hd - 1)
                b = bank[(7, 0)[hd % 2]]
                for tt in range(TT):
                    s = slice(0, P) if tt == 0 else slice(P, P + SEQ)
                    A(prob[:, hd % 2, s], b[:, s], ACT.Exp, bias=smax[:, hd % 2, tt:tt + 1], scale=SOFT,
                      accum_out=ssum[:, hd % 2, tt:tt + 1]).then_inc(att_exp, 1)

            def head_turned(hd):
                act.wait_ge(prob_turned, hd + 1)
                if hd >= 2:
                    act.wait_ge(att_o, hd - 1)
                A(probT[:, hd % 2, :], bank[1 + hd % 2][:, 0:384], ACT.Copy).then_inc(probT_ready, 1)

            def head_out(hd):
                act.wait_ge(att_o, hd + 1)
                A(oT[:, hd, :], bank[3 + hd % 2][:, 0:SEQ], ACT.Copy).then_inc(oT_ready, 1)

            head_exp(0)
            for hd in range(MH):
                if hd + 1 < MH:
                    head_exp(hd + 1)
                head_turned(hd)
                if hd:
                    head_out(hd - 1)
            head_out(MH - 1)
            experts(1)
            squares_of(4)

        @block.vector
        def _(dve):
            own = Count(dstep)

            def mean_square(n):
                dve.wait_ge(squares, 2 * (n + 1))
                dve.tensor_scalar(var[:, 0:2], msq[:, 0:2], 1.0 / D, EPS, ALU.mult, ALU.add).then_inc(meansq, 1)

            def normed(n, dst=y):
                dve.wait_ge(roots, n + 1)
                own.step(dve, dve.reciprocal(rstd[:, 0:2], root[:, 0:2]))
                for tt in range(TT):
                    dve.tensor_scalar(dst[:, tt, :], h[:, tt, :], rstd[:, tt:tt + 1], None, ALU.mult).then_inc(y_ready, 1)

            def modulate(n, dst, which, shift):
                for b in (0, 2):
                    dve.wait_ge(y_turned, 4 * n + b + 1)
                    for f in range(2):
                        k = 2 * b + f
                        dve.tensor_scalar(dst[:, k, :], bank[b][:, f * SEQ:(f + 1) * SEQ], scale[:, which, k:k + 1],
                                          modc[:, shift + k:shift + k + 1], ALU.mult, ALU.add).then_inc(xn_dve, 1)

            dve.wait_ge(rows_turned, 2)
            dve.tensor_copy(cols[:], bank[4][:, 0:120]).then_inc(cols_copied, 1)
            dve.tensor_copy(gcol[:], bank[5][:, 0:43]).then_inc(cols_copied, 1)
            mean_square(0)
            dve.wait_ge(c_silu, 1)
            dve.tensor_copy(cact[:], cs1[:].unsqueeze(2).to_broadcast([P, KT, 32])).then_inc(c_spread, 1)
            normed(0)

            dve.wait_ge(pos_in, 16)
            own.step(dve, dve.tensor_copy(posf, posi))
            own.step(dve, dve.tensor_scalar(ang[:, 0, :], posf, cst[:, C_FREQ:C_FREQ + 1], None, ALU.mult))
            own.step(dve, dve.tensor_scalar(ang[:, 1, :], posf, cst[:, C_FREQ + 1:C_FREQ + 2], None, ALU.mult))
            nearest = 12582912.0
            own.step(dve, dve.tensor_scalar(turns, ang, float(1 / (2 * np.pi)), nearest, ALU.mult, ALU.add))
            own.step(dve, dve.tensor_scalar(turns, turns, nearest, None, ALU.subtract))
            first = 6.28125
            second = float(np.float32(round((2 * np.pi - first) * 2 ** 22) / 2 ** 22))
            third = float(2 * np.pi - first - second)
            own.step(dve, dve.scalar_tensor_tensor(rem, turns, -first, ang, ALU.mult, ALU.add))
            own.step(dve, dve.scalar_tensor_tensor(rem, turns, -second, rem, ALU.mult, ALU.add))
            own.step(dve, dve.scalar_tensor_tensor(rem, turns, -third, rem, ALU.mult, ALU.add))
            dve.tensor_scalar(rem, rem, -3.1415925, 3.1415925, ALU.max, ALU.min).then_inc(angles_ready, 1)
            dve.wait_ge(angles_ready, 1)
            own.step(dve, dve.scalar_tensor_tensor(crem, rem, -1.0, rem, ALU.mult, ALU.max))
            dve.tensor_scalar(crem, crem, -1.0, float(np.pi / 2), ALU.mult, ALU.add).then_inc(angles_ready, 1)

            def mod_store(m):
                w, b = MOD[m]
                dve.wait_ge(mod_folded, m + 1)
                if (w, b) in GATES:
                    g = GATES[(w, b)]
                    if m == 4:
                        dve.wait_ge(gb_in, 16 * 5)
                    o = gate[:, g, (b % 2) * 512:(b % 2) * 512 + 512]
                    dve.tensor_tensor(o, bank[5][:], o, ALU.add).then_inc(mod_stored, 1)
                else:
                    c = MOD_COL[w] + 4 * b
                    dve.tensor_tensor(modc[:, c:c + 4], bank[5][:, 0:4], cols[:, 8 + c:12 + c], ALU.add).then_inc(mod_stored, 1)

            def scales(which, scol, gain):
                own.step(dve, dve.scalar_tensor_tensor(scale[:, which, :], modc[:, scol:scol + 8], 1.0,
                                                       gcol[:, gain:gain + 8], ALU.add, ALU.mult))

            for m in range(FIRST_MOD):
                mod_store(m)
            dve.wait_ge(mod_stored, FIRST_MOD)
            scales(0, MOD_COL[0] + 8, 0)
            assert own.n == D_SCALE0[0], own.n
            modulate(0, xnT, 0, MOD_COL[0])

            for r in range(12):
                hd = (r - 4) // 2
                m0 = FIRST_MOD + 2 * r
                if r < 4:
                    for b in range(2):
                        n = 2 * r + b
                        dve.wait_ge(win_done, n + 1)
                        dve.wait_ge(trig_ready, 2)
                        if n:
                            dve.wait_ge(rope_done, n)
                        src = bank[2 * (r % 2) + b][:].rearrange("p (f s) -> p f s", f=2)
                        for i in range(2):
                            w = trig[:, 0, i:i + 1, :].to_broadcast([P, 2, SEQ])
                            ins = dve.tensor_tensor(prod[:, i, :].rearrange("p (f s) -> p f s", f=2), src, w, ALU.mult)
                        ins.then_inc(rope_mult, 1)
                if r >= 4 and r % 2 == 0:
                    dec = cst[:, C_DECAY + hd * SEQ:C_DECAY + (hd + 1) * SEQ]
                    dve.wait_ge(ret_scores, hd + 1)
                    dve.tensor_tensor(inner[:, 0:SEQ], bank[6][:, 0:SEQ], dec, ALU.mult).then_inc(inner_ready, 1)
                    dve.tensor_tensor(inner[:, SEQ:SEQ + P], bank[6][:, SEQ:SEQ + P], dec[:, 0:P], ALU.mult).then_inc(inner_ready, 1)
                if r:
                    mod_store(m0 - 1)
                if r >= 4 and r % 2 == 1:
                    for tt in range(TT):
                        dve.wait_ge(o_done, 2 * hd + tt + 1)
                        own.step(dve, dve.bn_stats(bn[:, tt, :], bank[2 + tt][:]))
                        own.step(dve, dve.bn_aggr(mv[:, tt, :], bn[:, tt, :]))
                    dve.tensor_scalar(var[:, 0:2], mv[:, :, 1], EPS, None, ALU.add).then_inc(o_var, 1)
                    dve.wait_ge(o_root, hd + 1)
                    own.step(dve, dve.reciprocal(rstd[:, 0:2], root[:, 0:2]))
                    if hd:
                        dve.wait_ge(yh_turned, 2 * hd)
                    for tt in range(TT):
                        dve.tensor_scalar(on[:, tt, :], bank[2 + tt][:], mv[:, tt, 0:1], rstd[:, tt:tt + 1],
                                          ALU.subtract, ALU.mult).then_inc(o_norm, 1)
                    for tt in range(TT):
                        dve.wait_ge(o_norm, 2 * hd + tt + 1)
                        dve.wait_ge(g_silu, 2 * hd + tt + 1)
                        dve.tensor_tensor(on[:, tt, :], on[:, tt, :], sg[:, tt, :], ALU.mult).then_inc(yh_ready, 1)
                mod_store(m0)
            mod_store(len(MOD) - 1)
            dve.wait_ge(mod_stored, len(MOD))
            scales(1, MOD_COL[0] + 32, 16)
            scales(2, MOD_COL[1] + 8, 8)
            scales(3, MOD_COL[1] + 32, 24)
            scales(4, MOD_COL[2] + 8, 32)

            def mixed(l, banks):
                for i in range(4):
                    tt, n = i // 2, i % 2
                    s = slice(n * 512, (n + 1) * 512)
                    dve.wait_ge(mix_done, 4 * l + i + 1)
                    dve.tensor_tensor(acc[:, tt, s], bank[banks[i]][:], gate[:, 2 * l, s], ALU.mult).then_inc(h_prod, 1)

            def experts(l):
                n = 1 + 2 * l
                S = moe[l]
                mean_square(n)
                normed(n)
                modulate(n, xnT, 1 + 2 * l, MOD_COL[l] + 24)
                dve.wait_ge(sig_ready, l + 1)
                G = TT * NG
                own.step(dve, dve.tensor_tensor(biased[:], score[:], br[:].unsqueeze(1).to_broadcast([P, TT, NE]), ALU.add))
                flat = biased[:].rearrange("p t (g e) -> p (t g) e", g=NG)

                def ranks(values, groups, dst):
                    n = groups * EG * EG
                    c1 = cmp1[:, 0:n].rearrange("p (g i j) -> p g i j", i=EG, j=EG)
                    c2 = cmp2[:, 0:n].rearrange("p (g i j) -> p g i j", i=EG, j=EG)
                    mine = values.unsqueeze(3).to_broadcast([P, groups, EG, EG])
                    theirs = values.unsqueeze(2).to_broadcast([P, groups, EG, EG])
                    earlier = cst[:, C_EARLIER:C_EARLIER + EG * EG].unsqueeze(1).to_broadcast([P, groups, EG * EG])
                    own.step(dve, dve.tensor_tensor(c1, theirs, mine, ALU.is_gt))
                    own.step(dve, dve.tensor_tensor(c2, theirs, mine, ALU.is_equal))
                    f2 = cmp2[:, 0:n].rearrange("p (g i) -> p g i", i=EG * EG)
                    own.step(dve, dve.tensor_tensor(f2, f2, earlier, ALU.mult))
                    own.step(dve, dve.tensor_tensor(cmp1[:, 0:n], cmp1[:, 0:n], cmp2[:, 0:n], ALU.add))
                    own.step(dve, dve.tensor_reduce(dst, cmp1[:, 0:n].rearrange("p (i j) -> p i j", j=EG), AX.X, ALU.add))

                ranks(flat, G, rank[:])
                own.step(dve, dve.tensor_scalar(rank[:], rank[:], 2.0, None, ALU.is_lt))
                two = cmp1[:, 0:TT * NE]
                own.step(dve, dve.tensor_tensor(two, rank[:], biased[:].rearrange("p t e -> p (t e)"), ALU.mult))
                own.step(dve, dve.tensor_reduce(gsum[:], two.rearrange("p (g e) -> p g e", e=EG), AX.X, ALU.add))
                ranks(gsum[:].rearrange("p (t g) -> p t g", g=NG), TT, grank[:])
                own.step(dve, dve.tensor_scalar(grank[:], grank[:], 1.0, None, ALU.is_lt))
                dve.tensor_tensor(chosen[:].rearrange("p t (g e) -> p (t g) e", g=NG),
                                  rank[:].rearrange("p (g e) -> p g e", e=EG),
                                  grank[:].unsqueeze(2).to_broadcast([P, G, EG]), ALU.mult).then_inc(chosen_ready, 1)
                dve.wait_ge(chosen_ready, l + 1)
                own.step(dve, dve.tensor_tensor(combine[:], score[:], chosen[:], ALU.mult))
                own.step(dve, dve.tensor_reduce(den[:], combine[:], AX.X, ALU.add))
                own.step(dve, dve.reciprocal(den[:], den[:]))
                own.step(dve, dve.tensor_tensor(combine[:], combine[:], den[:].unsqueeze(2).to_broadcast([P, TT, NE]), ALU.mult))
                dve.wait_ge(ranked, l + 1)
                own.step(dve, dve.tensor_copy(cmp2[:, 0:3 * NE], bank[5][:, 0:3 * NE]))
                own.step(dve, dve.scalar_tensor_tensor(place[:].rearrange("p t e -> p (t e)"), cmp2[:, 0:2 * NE], 1.0,
                                                       chosen[:].rearrange("p t e -> p (t e)"), ALU.add, ALU.mult))
                own.step(dve, dve.tensor_scalar(place[:], place[:], 1.0, None, ALU.subtract))
                own.step(dve, dve.tensor_reduce(most[:, 0, :], cmp2[:, 2 * NE:3 * NE].rearrange("p (g e) -> p g e", e=2), AX.X, ALU.max))
                own.step(dve, dve.tensor_scalar(most[:, 1, :], most[:, 0, :], float(SLOTS) + 0.5, 1.0, ALU.is_gt, ALU.add))
                for r in range(2, ROUNDS):
                    own.step(dve, dve.scalar_tensor_tensor(most[:, 1, :], most[:, 0, :], float(r * SLOTS) + 0.5, most[:, 1, :], ALU.is_gt, ALU.add))
                own.step(dve, dve.memset(boundf[:], 0.0))
                for p in range(PAIRS):
                    own.step(dve, dve.tensor_tensor(boundf[:, p + 1:p + 2], boundf[:, p:p + 1], most[:, 1, p:p + 1], ALU.add))
                dve.tensor_copy(bounds[l][:], boundf[:]).then_inc(bounds_ready, 1)
                dve.wait_ge(bounds_ready, l + 1)
                with dve.Fori(0, PAIRS) as pair:
                    begin = dve.value_load(bounds[l][0:1, bass.ds(pair, 1)], min_val=0, max_val=ROUNDS * PAIRS)
                    end = dve.value_load(bounds[l][0:1, bass.ds(pair + 1, 1)], min_val=1, max_val=ROUNDS * PAIRS)
                    dve.tensor_copy(slot_id[:], slots0).then_inc(S["slots_ready"], 1)
                    with dve.Fori(begin, end) as u:
                        dve.wait_ge(S["slots_ready"], pair + u + 1)
                        four = [P, TT, 2, SLOTS]
                        v, vw = (x.rearrange("p t (e s) -> p t e s", e=2) for x in (pick, pickw))
                        dve.tensor_tensor(v, slot_id[:].unsqueeze(1).unsqueeze(1).to_broadcast(four),
                                          place[:, :, bass.ds(pair * 2, 2)].unsqueeze(3).to_broadcast(four),
                                          ALU.is_equal).then_inc(S["picked"], 1)
                        dve.wait_ge(S["picked"], u * 2 + 1)
                        dve.tensor_tensor(vw, v, combine[:, :, bass.ds(pair * 2, 2)].unsqueeze(3).to_broadcast(four),
                                          ALU.mult).then_inc(S["picked"], 1)
                        dve.tensor_scalar(slot_id[:], slot_id[:], float(SLOTS), None, ALU.add).then_inc(S["slots_ready"], 1)
                        dve.wait_ge(S["gathered"], u * 2 + 1)
                        for k in range(4):
                            ins = dve.tensor_scalar(xgT[:, k, :], bank[2][:, tok(k)], scale[:, 1 + 2 * l, k:k + 1],
                                                    modc[:, MOD_COL[l] + 24 + k:MOD_COL[l] + 25 + k], ALU.mult, ALU.add)
                        ins.then_inc(S["xg_dve"], 1)
                        dve.wait_ge(S["sil_ready"], u + 1)
                        for f in range(2):
                            s = slice(f * 256, (f + 1) * 256)
                            dve.wait_ge(S["up_done"], u * 2 + f + 1)
                            dve.tensor_tensor(hid[:, s], bank[(1, 6)[f]][:, 0:256], sil[:, s], ALU.mult).then_inc(S["hid_ready"], 1)
                        dve.wait_ge(S["hid_turned"], u * 2 + 2)
                        dve.tensor_copy(hidT[:, 2:4, :], bank[7][:, 0:SEQ].rearrange("p (k s) -> p k s", k=2)).then_inc(S["hidT_dve"], 1)
                        for i in range(4):
                            n2, tt = i // 2, i % 2
                            a = acc[:, tt, n2 * 512:(n2 + 1) * 512]
                            dve.wait_ge(S["comb_done"], u * 4 + i + 1)
                            dve.tensor_tensor(a, bank[(2, 3, 0, 1)[i]][:], a, ALU.add).then_inc(S["acc_added"], 1)
                total = dve.value_load(bounds[l][0:1, PAIRS:PAIRS + 1], min_val=PAIRS, max_val=ROUNDS * PAIRS)
                dve.wait_ge(S["acc_added"], total * 4 + 1)
                for i in range(4):
                    tt, n2 = i // 2, i % 2
                    s = slice(n2 * 512, (n2 + 1) * 512)
                    dve.tensor_tensor(acc[:, tt, s], acc[:, tt, s], gate[:, 2 * l + 1, s], ALU.mult).then_inc(h_prod, 1)

            mixed(0, (0, 1, 2, 3))
            experts(0)
            mean_square(2)
            normed(2)
            modulate(2, hnT, 4, MOD_COL[2])
            modulate(2, xnT, 2, MOD_COL[1])
            dve.wait_ge(kr_raw, 1)
            for i in range(2):
                w = trig[:, 1, i:i + 1, :].to_broadcast([P, 2, SEQ])
                dve.tensor_tensor(mprod[:, i, :].rearrange("p (f s) -> p f s", f=2),
                                  bank[5][:].rearrange("p (f s) -> p f s", f=2), w, ALU.mult).then_inc(kr_mult, 1)
            dve.wait_ge(lat_sq, 4)
            dve.tensor_scalar(var[:, 0:2], msq[:, 0:2], 1.0 / KVL, EPS, ALU.mult, ALU.add).then_inc(lat_ms, 1)
            dve.tensor_scalar(var[:, 2:4], msq[:, 2:4], 1.0 / QL, EPS, ALU.mult, ALU.add).then_inc(lat_ms, 1)
            dve.wait_ge(lat_root, 1)
            own.step(dve, dve.reciprocal(rstd[:, 0:4], root[:, 0:4]))
            for tt in range(TT):
                dve.tensor_scalar(cn[:, tt, :], bank[4][:, tt * KVL:(tt + 1) * KVL], rstd[:, tt:tt + 1], None, ALU.mult).then_inc(lat_norm, 1)
            for tt in range(TT):
                dve.tensor_scalar(qn[:, tt, :], bank[6][:, tt * QL:(tt + 1) * QL], rstd[:, 2 + tt:3 + tt], None, ALU.mult).then_inc(lat_norm, 1)
            dve.wait_ge(lat_turned, 2)
            for j in range(2):
                dve.tensor_scalar(qaT[:, j, :], bank[0][:, j * SEQ:(j + 1) * SEQ], gcol[:, 41 + j:42 + j], None, ALU.mult).then_inc(qaT_ready, 1)
            for b in (2, 4):
                dve.wait_ge(kv_done, b)
                dve.tensor_copy(knT[:, 2 * (b - 1):2 * b, :], bank[b][:].rearrange("p (k s) -> p k s", k=2)).then_inc(kv_dve, 1)
            for b in (1, 3):
                dve.wait_ge(kv_done, 4 + b + 1)
                dve.tensor_copy(vm[:, b // 2, 512:1024], bank[(5, 6, 7, 0)[b]][:]).then_inc(kv_dve, 1)
            for b in (2, 4):
                dve.wait_ge(qb_done, b)
                dve.tensor_copy(qnT[:, 2 * (b - 1):2 * b, :], bank[b][:].rearrange("p (k s) -> p k s", k=2)).then_inc(qb_dve, 1)
            dve.wait_ge(kr_ready, 2)
            for f in range(2):
                dve.wait_ge(qb_done, 5 + f)
                for i in range(2):
                    w = trig[:, 1, i:i + 1, :].to_broadcast([P, 2, SEQ])
                    dve.tensor_tensor(mprod[:, 2 * f + i, :].rearrange("p (f s) -> p f s", f=2),
                                      bank[5 + f][:].rearrange("p (f s) -> p f s", f=2), w, ALU.mult).then_inc(qr_mult, 1)

            def head_max(hd):
                b = bank[(7, 0)[hd % 2]]
                dve.wait_ge(att_score, hd + 1)
                if hd >= 2:
                    dve.wait_ge(att_exp, 2 * (hd - 1))
                for s in (slice(CH, P), slice(P + 3 * CH, P + 4 * CH)):
                    own.step(dve, dve.tensor_scalar(b[0:CH, s], b[0:CH, s], -3e38, None, ALU.add))
                for tt, s in enumerate((slice(0, P), slice(P, P + SEQ))):
                    own.step(dve, dve.tensor_reduce(smax[:, hd % 2, tt:tt + 1], b[:, s], AX.X, ALU.max))
                for tt in range(TT):
                    m = smax[:, hd % 2, tt:tt + 1]
                    dve.tensor_scalar(m, m, -SOFT, None, ALU.mult).then_inc(att_max, 1)

            def head_scale(hd):
                dve.wait_ge(att_exp, 2 * (hd + 1))
                own.step(dve, dve.reciprocal(srec[:, hd % 2, :], ssum[:, hd % 2, :]))
                for tt, s in enumerate((slice(0, P), slice(P, P + SEQ))):
                    dve.tensor_scalar(prob[:, hd % 2, s], prob[:, hd % 2, s], srec[:, hd % 2, tt:tt + 1], None,
                                      ALU.mult).then_inc(att_prob, 1)

            head_max(0)
            for hd in range(MH):
                if hd + 1 < MH:
                    head_max(hd + 1)
                head_scale(hd)
            mixed(1, (5, 6, 7, 0))
            experts(1)
            dve.wait_ge(fn_in, 16)
            mean_square(4)
            normed(4)
            for tt in range(TT):
                dve.wait_ge(y_ready, 8 + tt + 1)
                dve.tensor_tensor(acc[:, tt, :], y[:, tt, :], gate[:, 0, :], ALU.mult).then_inc(h_ready, 1)

        @block.gpsimd
        def _(pool):
            for n in range(8):
                pool.wait_ge(rope_mult, n + 1)
                r, b = n // 2, n % 2
                dst = (qT, kT)[r % 2]
                k = 4 * (r // 2) + 2 * b
                pool.tensor_tensor(dst[:, k, :], prod[:, 0, 0:SEQ], prod[:, 1, SEQ:2 * SEQ], ALU.subtract)
                pool.tensor_tensor(dst[:, k + 1, :], prod[:, 1, 0:SEQ], prod[:, 0, SEQ:2 * SEQ], ALU.add).then_inc(rope_done, 1)

            def into_h(s):
                for i in range(4):
                    tt, n = i // 2, i % 2
                    c = slice(n * 512, (n + 1) * 512)
                    pool.wait_ge(h_prod, 4 * s + i + 1)
                    pool.tensor_tensor(h[:, tt, c], h[:, tt, c], acc[:, tt, c], ALU.add).then_inc(h_ready, 1)

            def experts(l):
                S = moe[l]
                pool.wait_ge(h_ready, 8 * l + 4)
                pool.memset(acc[:].rearrange("p t n -> p (t n)"), 0.0).then_inc(S["acc_added"], 1)
                into_h(1 + 2 * l)

            into_h(0)
            experts(0)
            kva = slot(MLA_AT)[:, 0:KT * 192].rearrange("p (k n) -> p k n", k=KT)
            pool.wait_ge(landed[MLA_AT % RING], 16 * (MLA_AT // RING + 1))
            for f in range(2):
                src = kva[:, :, KVL + f * HALF:KVL + (f + 1) * HALF]
                pool.tensor_copy(kr_w[:, f].rearrange("p k (c n) -> p k c n", c=4),
                                 src.unsqueeze(2).to_broadcast([P, KT, 4, HALF])).then_inc(rope_w, 1)
            qb = slot(MLA_AT + 3)[:, 0:3072].rearrange("p (k h n) -> p k h n", k=2, h=MH)
            pool.wait_ge(landed[(MLA_AT + 3) % RING], 16 * ((MLA_AT + 3) // RING + 1))
            for f in range(2):
                pool.tensor_copy(qr_w[:, f].rearrange("p k (h n) -> p k h n", h=MH),
                                 qb[:, :, :, NOPE + f * HALF:NOPE + (f + 1) * HALF]).then_inc(rope_w, 1)
            pool.wait_ge(kr_mult, 2)
            pool.tensor_tensor(krT[:, 0, :], mprod[:, 0, 0:SEQ], mprod[:, 1, SEQ:2 * SEQ], ALU.subtract).then_inc(kr_ready, 1)
            pool.tensor_tensor(krT[:, 1, :], mprod[:, 1, 0:SEQ], mprod[:, 0, SEQ:2 * SEQ], ALU.add).then_inc(kr_ready, 1)
            pool.wait_ge(qr_mult, 4)
            pool.tensor_tensor(qrT[:, 0, :, :].rearrange("p g s -> p (g s)"), mprod[:, 0, :], mprod[:, 3, :], ALU.subtract).then_inc(qr_ready, 1)
            pool.tensor_tensor(qrT[:, 1, :, :].rearrange("p g s -> p (g s)"), mprod[:, 1, :], mprod[:, 2, :], ALU.add).then_inc(qr_ready, 1)
            into_h(2)
            experts(1)


D_SCALE0 = [11]

_INS = ["x", "c", "positions", "w_mod", "b_mod", "norm_mix", "norm_ffn", "ret_w_in", "ret_w_out", "w_mod_kv",
        "b_mod_kv", "norm_kv", "mla_w_kv_a", "mla_kv_norm", "mla_w_kv_b", "mla_w_q_a", "mla_q_norm", "mla_w_q_b",
        "mla_w_o", "router_w", "router_b", "moe_w_gate", "moe_w_up", "moe_w_down", "final_norm"]


def kernel(**inputs):
    import concourse.bacc as bacc
    from concourse.bass_utils import run_bass_kernel_spmd as run

    nc = bacc.Bacc("TRN2", target_bir_lowering=False, num_devices=1)
    arrays = {"constants": constants()}
    arrays.update({name: np.ascontiguousarray(inputs[name]) for name in _INS})
    args = {name: nc.dram_tensor(f"in_{name}", a.shape, mybir.dt.from_np(a.dtype), kind="ExternalInput").ap()
            for name, a in arrays.items()}
    out = nc.dram_tensor("out", (1, SEQ, D), F32, kind="ExternalOutput").ap()
    build_kernel(nc, args, out)
    r = run(nc, [{f"in_{name}": a for name, a in arrays.items()}], core_ids=[0])
    return r.results[0]["out"]
```

```python
from contextlib import ExitStack

import numpy as np

import concourse.bass as bass
from concourse import mybir

F32 = mybir.dt.float32
I32 = mybir.dt.int32
ALU = mybir.AluOpType
ACT = mybir.ActivationFunctionType
AX = mybir.AxisListType

P = 128
D = 1024
KT = D // P
SEQ = 256
TT = SEQ // P
EPS = 1e-6
RH, RDK, RDV = 4, 256, 512
MH, NOPE, ROPE, VH = 8, 128, 64, 128
HALF = ROPE // 2
QL, KVL = 256, 128
NE, NG, EG = 16, 4, 4
DE = 512
PAIRS = NE // 2
SLOTS = 64
ROUNDS = SEQ // SLOTS
CH = 64
SOFT = float(NOPE + ROPE) ** -0.5
RING = 6

C_IDENT = 0
C_TRI = C_IDENT + P
C_ONES = C_TRI + P
C_SLOT = C_ONES + P
C_EARLIER = C_SLOT + SLOTS
C_FREQ = C_EARLIER + EG * EG
C_DECAY = C_FREQ + 2
C_ALL = C_DECAY + RH * SEQ


def constants():
    c = np.zeros((P, C_ALL), np.float32)
    i = np.arange(P)
    c[:, C_IDENT:C_IDENT + P] = np.eye(P)
    c[:, C_TRI:C_TRI + P] = i[:, None] < i[None, :]
    c[:, C_ONES:C_ONES + P] = 1
    c[:, C_SLOT:C_SLOT + SLOTS] = np.arange(SLOTS)
    j = np.arange(EG)
    c[:, C_EARLIER:C_EARLIER + EG * EG] = (j[None, :] < j[:, None]).reshape(-1)
    c[:, C_FREQ] = 10000.0 ** (-i / P)
    c[:, C_FREQ + 1] = np.tile(10000.0 ** (-i[:HALF] / HALF), P // HALF)
    n = np.arange(SEQ)
    for h in range(RH):
        g = np.log1p(-(2.0 ** (-5.0 - h)))
        d = n[None, :] - i[:, None]
        c[:, C_DECAY + h * SEQ:C_DECAY + (h + 1) * SEQ] = np.where(d >= 0, np.exp(g * np.maximum(d, 0)), 0) * RDK ** -0.5
    return c


MOD = [(0, b) for b in range(12)] + [(2, b) for b in range(4)] + [(1, b) for b in range(12)]
FIRST_MOD = 4
MOD_COL = {0: 0, 1: 48, 2: 96}
GATES = {(0, 4): 0, (0, 5): 0, (0, 10): 1, (0, 11): 1, (1, 4): 2, (1, 5): 2, (1, 10): 3, (1, 11): 3}
WIN = [0, 2, 1, 3] + [b for h in range(RH) for b in (4 + h, 8 + h)]

STREAM = [("mod", m) for m in range(FIRST_MOD)]
ROUND_MODS = []
_m = FIRST_MOD
for _r in range(12):
    ROUND_MODS.append(list(range(_m, _m + (1 if _r >= 4 and _r % 2 else 2))))
    _m += len(ROUND_MODS[-1])
    STREAM += [("win", _r)] + [("mod", m) for m in ROUND_MODS[-1]]
LAST_MODS = list(range(_m, len(MOD)))
STREAM += [("wout", i) for i in range(3)] + [("mod", m) for m in LAST_MODS] + [("wout", 3)]
N_RET = len(STREAM)
MOE_AT = [N_RET, N_RET + 6 * PAIRS + 6]
MLA_AT = N_RET + 6 * PAIRS
MLA_ITEMS = ["kva", "qa", "kvb", "qb", "wo0", "wo1"]
AT = {item: i for i, item in enumerate(STREAM)}
AT.update({(name, 0): MLA_AT + i for i, name in enumerate(MLA_ITEMS)})


def build_kernel(nc, t, out):
    with ExitStack() as ctx:
        def sb(name, shape, dt=F32):
            return ctx.enter_context(nc.sbuf_tensor(name, shape, dt))

        def sem(name):
            return ctx.enter_context(nc.semaphore(name))

        ring = sb("ring", [P, RING, 4096])
        h = sb("h", [P, TT, D])
        y = sb("y", [P, TT, D])
        xnT = sb("xnT", [P, KT, SEQ])
        acc = sb("acc", [P, TT, D])
        gate = sb("gate", [P, 4, D])
        part = sb("part", [P, 2, 512])
        cst = sb("cst", [P, C_ALL])
        rows = sb("rows", [120, P])
        gains = sb("gains", [43, P])
        cols = sb("cols", [P, 120])
        gcol = sb("gcol", [P, 43])
        cact = sb("cact", [P, KT])
        modc = sb("modc", [P, 112])
        scale = sb("scale", [P, 5, KT])
        wr = sb("wr", [P, KT, NE])
        br = sb("br", [P, NE])
        stat = sb("stat", [P, 32])
        msq, var, root, rstd = stat[:, 0:4], stat[:, 4:8], stat[:, 8:12], stat[:, 12:16]
        mv = stat[:, 16:20].rearrange("p (t s) -> p t s", t=2)
        bn = sb("bn", [P, 2, 6])
        score = sb("score", [P, TT, NE])
        biased = sb("biased", [P, TT, NE])
        cmp1 = sb("cmp1", [P, TT * NG * EG * EG])
        cmp2 = sb("cmp2", [P, TT * NG * EG * EG])
        chosen = sb("chosen", [P, TT, NE])
        rank = sb("rank", [P, TT * NE])
        gsum = sb("gsum", [P, TT * NG])
        grank = sb("grank", [P, TT * NG])
        den = sb("den", [P, TT])
        combine = sb("combine", [P, TT, NE])
        place = sb("place", [P, TT, NE])
        most = sb("most", [P, 3, PAIRS])
        bounds = [sb(f"bounds{l}", [P, 16], I32) for l in range(2)]
        boundf = sb("boundf", [1, 16])
        zeros = sb("zeros", [1, 16])
        slot_id = sb("slot_id", [P, SLOTS])

        arena = sb("arena", [P, 11800])
        at = [0]

        def take(n):
            at[0] += n
            assert at[0] <= 11800, at[0]
            return arena[:, at[0] - n:at[0]]

        trig = take(1024).rearrange("p (w f s) -> p w f s", w=2, f=2)
        kept = at[0]
        qT = take(2048).rearrange("p (k s) -> p k s", s=SEQ)
        kT = take(2048).rearrange("p (k s) -> p k s", s=SEQ)
        vh = take(2048).rearrange("p (b t n) -> p b t n", b=2, t=TT)
        inner = take(384)
        prod = take(1024).rearrange("p (f s) -> p f s", f=2)
        on, sg = acc[:, :, 0:512], acc[:, :, 512:1024]
        yTs = [y[:].rearrange("p t d -> p (t d)").rearrange("p (k s) -> p k s", s=SEQ),
               take(2048).rearrange("p (k s) -> p k s", s=SEQ)]

        def yT(k):
            return yTs[k // 8][:, k % 8, :]

        ang, turns, rem, crem = (qT[:, 2 * i:2 * i + 2, :] for i in range(4))
        posi = kT[:, 0, :].bitcast(I32)
        posf = kT[:, 1, :]
        at[0] = kept
        xgT = take(1024).rearrange("p (k s) -> p k s", s=P)
        sil = take(DE)
        hid = take(DE)
        hidT = take(DE).rearrange("p (k s) -> p k s", s=P)
        yg = take(D)
        pick = take(256).rearrange("p (t s) -> p t s", t=TT)
        pickw = take(256).rearrange("p (t s) -> p t s", t=TT)
        pickwT = take(256).rearrange("p (t s) -> p t s", t=TT)
        at[0] = kept
        hnT = take(2048).rearrange("p (k s) -> p k s", s=SEQ)
        oT = hnT
        knT = take(2048).rearrange("p (k s) -> p k s", s=SEQ)
        vm = take(2048).rearrange("p (t n) -> p t n", t=TT)
        qnT = take(2048).rearrange("p (k s) -> p k s", s=SEQ)
        ckT = take(256)
        qaT = take(512).rearrange("p (k s) -> p k s", s=SEQ)
        krT = take(512).rearrange("p (f s) -> p f s", f=2)
        qrT = take(1024).rearrange("p (f g s) -> p f g s", f=2, g=2)
        mprod = acc[:].rearrange("p t d -> p (t d)").rearrange("p (i s) -> p i s", i=4)
        cn = take(256).rearrange("p (t n) -> p t n", t=TT)
        qn = xnT[:, 0:2, :]
        prob, probT = y[:, :, 0:384], y[:, :, 384:768]
        smax = take(6).rearrange("p (b n) -> p b n", b=3)
        ssum = take(4).rearrange("p (b n) -> p b n", b=2)
        srec = take(4).rearrange("p (b n) -> p b n", b=2)

        bank = [ctx.enter_context(nc.psum_tensor(f"bank{i}", [P, 512], F32)) for i in range(8)]

        mla_bank = bank[4:] + bank[:4]
        att_bank = [mla_bank[7], mla_bank[0], mla_bank[5]]

        ident = cst[:, C_IDENT:C_IDENT + P]
        tri = cst[:, C_TRI:C_TRI + P]
        ones = cst[:, C_ONES:C_ONES + P]
        slots0 = cst[:, C_SLOT:C_SLOT + SLOTS]

        def tok(tt):
            return slice(tt * P, (tt + 1) * P)

        def slot(i):
            return ring[:, i % RING, :]

        kr_w = slot(MLA_AT)[:, 2048:4096].rearrange("p (f k n) -> p f k n", f=2, k=KT)
        qr_w = slot(MLA_AT + 3)[:, 3072:4096].rearrange("p (f k n) -> p f k n", f=2, k=2)

        landed = [sem(f"landed{i}") for i in range(RING)]
        wo_used = sem("wo_used")
        gains_in, gains_turned, gcol_copied = (sem(n) for n in ("gains_in", "gains_turned", "gcol_copied"))
        small_in, x_in, pos_in, cst_in, decay_in, gb_in, fn_in, router_in = (
            sem(n) for n in ("small_in", "x_in", "pos_in", "cst_in", "decay_in", "gb_in", "fn_in", "router_in"))
        rows_turned, cols_copied, c_silu = (sem(n) for n in ("rows_turned", "cols_copied", "c_silu"))
        angles_ready, trig_ready = sem("angles_ready"), sem("trig_ready")
        dstep = sem("dstep")
        squares, meansq, roots, y_ready = (sem(n) for n in ("squares", "meansq", "roots", "y_ready"))
        y_turned, xn_dve, xn_act = sem("y_turned"), sem("xn_dve"), sem("xn_act")
        scales_ready = sem("scales_ready")
        mod_step, mod_sum, mod_folded, mod_stored = (
            sem(n) for n in ("mod_step", "mod_sum", "mod_folded", "mod_stored"))
        win_done, rope_mult, rope_done, v_copied, g_silu = (
            sem(n) for n in ("win_done", "rope_mult", "rope_done", "v_copied", "g_silu"))
        ret_scores, inner_ready, o_done, o_var, o_root, o_norm, yh_ready, yh_turned, yT_copied = (
            sem(n) for n in ("ret_scores", "inner_ready", "o_done", "o_var", "o_root", "o_norm",
                             "yh_ready", "yh_turned", "yT_copied"))
        mix_done, h_prod, h_ready = sem("mix_done"), sem("h_prod"), sem("h_ready")
        logits, sig_ready, chosen_ready, ranked, bounds_ready = (
            sem(n) for n in ("logits", "sig_ready", "chosen_ready", "ranked", "bounds_ready"))
        stored = sem("stored")
        rope_w = sem("rope_w")
        ck_raw, kr_raw, qa_raw, lat_sq, lat_ms, lat_root, lat_norm, lat_turned, ckT_ready, qaT_ready = (
            sem(n) for n in ("ck_raw", "kr_raw", "qa_raw", "lat_sq", "lat_ms", "lat_root", "lat_norm",
                             "lat_turned", "ckT_ready", "qaT_ready"))
        kv_done, kv_act, kv_dve, qb_done, qb_act, qb_dve, kr_mult, kr_ready, qr_mult, qr_ready = (
            sem(n) for n in ("kv_done", "kv_act", "kv_dve", "qb_done", "qb_act", "qb_dve", "kr_mult",
                             "kr_ready", "qr_mult", "qr_ready"))
        att_masked, att_top = sem("att_masked"), sem("att_top")
        att_score, att_max, att_exp, att_prob, prob_turned, probT_ready, att_o, oT_ready = (
            sem(n) for n in ("att_score", "att_max", "att_exp", "att_prob", "prob_turned",
                             "probT_ready", "att_o", "oT_ready"))
        MOE = ["slots_ready", "picked", "weights_turned", "gathered", "xg_dve", "xg_act", "pickwT_ready", "gate_done", "up_done",
               "sil_ready", "hid_ready", "hid_turned", "hidT_act", "hidT_dve", "down_done", "yg_ready",
               "comb_done", "acc_added"]
        moe = [{n: sem(f"{n}{l}") for n in MOE} for l in range(2)]

        class Count:

            def __init__(self, s):
                self.s, self.n = s, 0

            def step(self, eng, ins):
                self.n += 1
                ins.then_inc(self.s, 1)
                eng.wait_ge(self.s, self.n)

        block = ctx.enter_context(nc.Block())

        @block.sync
        def _(sp):
            def source(kind, n):
                if kind == "mod":
                    m, b = MOD[n]
                    w = t["w_mod_kv"] if m == 2 else t["w_mod"][m]
                    return w[:, b * 512:(b + 1) * 512].rearrange("(k p) n -> p k n", p=P)
                if kind == "win":
                    b = WIN[n]
                    return t["ret_w_in"][0, :, b * 512:(b + 1) * 512].rearrange("(k p) n -> p k n", p=P)
                if kind == "wout":
                    return t["ret_w_out"][0, n * 512:(n + 1) * 512, :].rearrange("(k p) n -> p k n", p=P)
                if kind == "kva":
                    return t["mla_w_kv_a"].rearrange("(k p) n -> p k n", p=P)
                if kind == "qa":
                    return t["mla_w_q_a"][0].rearrange("(k p) n -> p k n", p=P)
                if kind == "kvb":
                    return t["mla_w_kv_b"].rearrange("(k p) n -> p k n", p=P)
                if kind == "qb":
                    return t["mla_w_q_b"][0].rearrange("(k p) n -> p k n", p=P)
                n = int(kind[2])
                return t["mla_w_o"][0, n * 512:(n + 1) * 512, :].rearrange("(k p) n -> p k n", p=P)

            def load(i, src):
                k, n = src.shape[1], src.shape[2]
                dst = slot(i)[:, 0:k * n].rearrange("p (k n) -> p k n", k=k)
                sp.dma_start(dst, src).then_inc(landed[i % RING], 16)

            def experts(l, pair, before):
                base = MOE_AT[l]
                for j in range(6):
                    w = t[("moe_w_gate", "moe_w_up", "moe_w_down")[j // 2]][l]
                    w = w[bass.ds(pair * 2 + j % 2, 1)]
                    before(j)
                    load(base + j, w.rearrange("e (k p) n -> p (e k) n", p=P))

            def released(i):
                kind, n = STREAM[i] if i < N_RET else (MLA_ITEMS[i - MLA_AT], 0)
                s, v = {"mod": (mod_sum, n + 1), "win": (win_done, 2 * n + 2), "wout": (wo_used, n + 1),
                        "kva": (kr_raw, 1), "qa": (qa_raw, 1), "kvb": (kv_done, 8), "qb": (qb_done, 6),
                        "wo0": (wo_used, 4), "wo1": (mix_done, 8)}[kind]
                if (kind, n) == ("wout", 3):
                    s, v = mix_done, 4
                sp.wait_ge(s, v)

            sp.dma_start(rows[0:8, :], t["c"].rearrange("b (r c) -> (b r) c", c=P)).then_inc(small_in, 16)
            sp.dma_start(rows[8:104, :], t["b_mod"].rearrange("l (r c) -> (l r) c", c=P)).then_inc(small_in, 16)
            for i, (kind, n) in enumerate(STREAM):
                if i >= RING:
                    released(i - RING)
                load(i, source(kind, n))
                if i == 1:
                    sp.dma_start(h[:], t["x"].rearrange("b (t p) d -> p (b t) d", p=P)).then_inc(x_in, 16)
            for l in range(2):
                S = moe[l]
                base = MOE_AT[l]

                def first(j):
                    released(base - RING + j)

                experts(l, 0, first)
                sp.wait_ge(bounds_ready, l + 1)
                with sp.Fori(1, PAIRS) as pair:
                    begun = sp.value_load(bounds[l][0:1, bass.ds(pair, 1)], min_val=1, max_val=ROUNDS * PAIRS)

                    def rest(j):
                        if j == 0:
                            sp.wait_ge(S["gate_done"], begun)
                        if j == 2:
                            sp.wait_ge(S["up_done"], begun * 2)
                        if j == 4:
                            sp.wait_ge(S["down_done"], begun * 2)

                    experts(l, pair, rest)
                if l == 0:
                    total = sp.value_load(bounds[l][0:1, PAIRS:PAIRS + 1], min_val=PAIRS, max_val=ROUNDS * PAIRS)
                    for j, kind in enumerate(MLA_ITEMS):
                        if j == 0:
                            sp.wait_ge(S["gate_done"], total)
                        if j == 2:
                            sp.wait_ge(S["up_done"], total * 2)
                        if j == 4:
                            sp.wait_ge(S["down_done"], total * 2)
                        load(MLA_AT + j, source(kind, 0))
            for tt in range(TT):
                sp.wait_ge(h_ready, 16 + tt + 1)
                sp.dma_start(out[0, tok(tt), :], acc[:, tt, :]).then_inc(stored, 16)
            sp.wait_ge(stored, 16 * TT)

        @block.tensor
        def _(pe):
            def arrived(i, extra=None):
                v = 16 * (i // RING + 1)
                pe.wait_ge(landed[i % RING], v if extra is None else extra * 16 + v)

            def turn_y(n):
                for tt in range(TT):
                    pe.wait_ge(y_ready, 2 * n + tt + 1)
                    for b in range(4):
                        for f in range(2):
                            k = 2 * b + f
                            ins = pe.transpose(bank[4 + b][:, f * SEQ + tt * P:f * SEQ + (tt + 1) * P],
                                               y[:, tt, k * P:(k + 1) * P], ident)
                        if tt == TT - 1:
                            ins.then_inc(y_turned, 1)

            pe.wait_ge(cst_in, 16)
            pe.wait_ge(small_in, 16 * 3)
            pe.transpose(bank[4][:, 0:120], rows[:], ident[0:120, 0:120]).then_inc(rows_turned, 1)

            def mod_fold(m):
                b = bank[4 + m % 2]
                pe.wait_ge(mod_sum, m + 1)
                if m == 0:
                    pe.wait_ge(cols_copied, 1)
                elif m >= 2:
                    pe.wait_ge(mod_stored, m - 1)
                if MOD[m] in GATES:
                    ins = pe.matmul(b[:], ones, part[:, m % 2, :], start=True, stop=True)
                else:
                    for j in range(4):
                        ins = pe.matmul(b[:, j:j + 1], part[:, m % 2, j * P:(j + 1) * P],
                                        ones[:, 0:1], start=True, stop=True)
                ins.then_inc(mod_folded, 1)

            for m in range(FIRST_MOD):
                mod_fold(m)
            pe.wait_ge(gains_in, 16 * 5)
            pe.transpose(bank[0][:, 0:43], gains[:], ident[0:43, 0:43]).then_inc(gains_turned, 1)
            pe.wait_ge(mod_stored, FIRST_MOD)
            turn_y(0)

            def turn_head(hd, g):
                pe.wait_ge(yh_ready, 2 * hd + 2)
                if 2 * hd + g:
                    pe.wait_ge(yT_copied, 2 * hd + g)
                for j in range(2):
                    for tt in range(TT):
                        ins = pe.transpose(bank[7][:, (2 * j + tt) * P:(2 * j + tt + 1) * P],
                                           on[:, tt, (2 * g + j) * P:(2 * g + j + 1) * P], ident)
                ins.then_inc(yh_turned, 1)

            for r in range(12):
                i = AT[("win", r)]
                w = slot(i).rearrange("p (k n) -> p k n", k=KT)
                arrived(i)
                hd = (r - 4) // 2
                pair = (bank[0], bank[1]) if r % 2 == 0 else (bank[2], bank[3])
                if r == 0:
                    pe.wait_ge(gcol_copied, 1)
                    pe.wait_ge(xn_dve, 4)
                    pe.wait_ge(xn_act, 4)
                elif 2 <= r < 6:
                    pe.wait_ge(rope_mult, 2 * (r - 1))
                elif r >= 6 and r % 2 == 0:
                    pe.wait_ge(v_copied, 2 * hd)
                elif r >= 6:
                    pe.wait_ge(o_norm, 2 * hd)
                if r < 4:
                    for b in range(2):
                        for f in range(2):
                            c = (2 * b + f) * P
                            for k in range(KT):
                                ins = pe.matmul(pair[b][:, f * SEQ:(f + 1) * SEQ], w[:, k, c:c + P], xnT[:, k, :],
                                                start=(k == 0), stop=(k == KT - 1))
                        ins.then_inc(win_done, 1)
                else:
                    for tt in range(TT):
                        for k in range(KT):
                            ins = pe.matmul(pair[tt][:], xnT[:, k, tok(tt)], w[:, k, :],
                                            start=(k == 0), stop=(k == KT - 1))
                        ins.then_inc(win_done, 1)
                if r >= 4 and r % 2 == 0:
                    if hd:
                        turn_head(hd - 1, 0)
                    pe.wait_ge(rope_done, 8)
                    if hd:
                        pe.wait_ge(inner_ready, 2 * hd)
                    for f in range(2):
                        pe.matmul(bank[6][:, 0:SEQ], kT[:, 2 * hd + f, 0:P], qT[:, 2 * hd + f, :],
                                  start=(f == 0), stop=(f == 1))
                    for f in range(2):
                        ins = pe.matmul(bank[6][:, SEQ:SEQ + P], kT[:, 2 * hd + f, P:SEQ], qT[:, 2 * hd + f, P:SEQ],
                                        start=(f == 0), stop=(f == 1))
                    ins.then_inc(ret_scores, 1)
                if r == 0:
                    pe.wait_ge(xn_dve, 4)
                    pe.wait_ge(xn_act, 4)
                for m in ROUND_MODS[r]:
                    mod_fold(m)
                if r >= 4 and r % 2 == 0 and hd:
                    turn_head(hd - 1, 1)
                if r >= 4 and r % 2 == 1:
                    pe.wait_ge(g_silu, 2 * hd + 2)
                    pe.wait_ge(v_copied, 2 * hd + 2)
                    pe.wait_ge(inner_ready, 2 * hd + 2)
                    v = vh[:, hd % 2]
                    pe.matmul(bank[2][:], inner[:, 0:P], v[:, 0, :], start=True, stop=True).then_inc(o_done, 1)
                    pe.matmul(bank[3][:], inner[:, P:SEQ], v[:, 0, :], start=True, stop=False)
                    pe.matmul(bank[3][:], inner[:, SEQ:SEQ + P], v[:, 1, :], start=False, stop=True).then_inc(o_done, 1)

            def wout(i, tt):
                it = AT[("wout", i)]
                w = slot(it).rearrange("p (k n) -> p k n", k=4)
                arrived(it)
                for n in range(2):
                    for kk in range(4):
                        ins = pe.matmul(bank[2 * tt + n][:], yT(4 * i + kk)[:, tok(tt)], w[:, kk, n * 512:(n + 1) * 512],
                                        start=(i == 0 and kk == 0), stop=(i == 3 and kk == 3))
                    if i == 3:
                        ins.then_inc(mix_done, 1)
                return ins

            pe.wait_ge(yT_copied, 6)
            for i in range(3):
                wout(i, 0)
            turn_head(3, 0)
            pe.wait_ge(o_norm, 8)
            wout(0, 1).then_inc(wo_used, 1)
            turn_head(3, 1)
            wout(1, 1).then_inc(wo_used, 1)
            wout(2, 1).then_inc(wo_used, 1)
            for m in LAST_MODS:
                mod_fold(m)
            pe.wait_ge(yT_copied, 8)
            wout(3, 0)
            wout(3, 1)

            def experts(l):
                n = 1 + 2 * l
                S = moe[l]
                turn_y(n)
                pe.wait_ge(h_prod, 8 * l + 4)
                pe.wait_ge(router_in, 32)
                for k in range(KT):
                    if k % 2 == 0:
                        pe.wait_ge(*((xn_dve, xn_act)[k // 2 % 2], 4 + 12 * l + 2 * (k // 4) + 2))
                    for tt in range(TT):
                        ins = pe.matmul(bank[tt][:, 0:NE], xnT[:, k, tok(tt)], wr[:, k, :],
                                        start=(k == 0), stop=(k == KT - 1))
                ins.then_inc(logits, 1)
                pe.wait_ge(chosen_ready, l + 1)
                pe.matmul(bank[2][:, 0:NE], tri, chosen[:, 0, :], start=True, stop=True)
                pe.matmul(bank[2][:, NE:2 * NE], ones, chosen[:, 0, :], start=True, stop=False)
                pe.matmul(bank[2][:, NE:2 * NE], tri, chosen[:, 1, :], start=False, stop=True)
                pe.matmul(bank[2][:, 2 * NE:3 * NE], ones, chosen[:, 0, :], start=True, stop=False)
                pe.matmul(bank[2][:, 2 * NE:3 * NE], ones, chosen[:, 1, :], start=False, stop=True).then_inc(ranked, 1)
                pe.wait_ge(bounds_ready, l + 1)
                base = MOE_AT[l]
                wv = [slot(base + j).rearrange("p (k n) -> p k n", k=(KT if j < 4 else 4)) for j in range(6)]
                with pe.Fori(0, PAIRS) as pair:
                    begin = pe.value_load(bounds[l][0:1, bass.ds(pair, 1)], min_val=0, max_val=ROUNDS * PAIRS)
                    end = pe.value_load(bounds[l][0:1, bass.ds(pair + 1, 1)], min_val=1, max_val=ROUNDS * PAIRS)
                    with pe.Fori(begin, end) as u:
                        pe.wait_ge(S["picked"], u * 2 + 1)
                        pe.wait_ge(S["acc_added"], u * 4 + 1)
                        for k in range(KT):
                            for tt in range(TT):
                                ins = pe.matmul(bank[2 + k // 4][:, (k % 4) * P:(k % 4 + 1) * P],
                                                y[:, tt, k * P:(k + 1) * P], pick[:, tt, :],
                                                start=(tt == 0), stop=(tt == TT - 1))
                            if k % 4 == 3:
                                ins.then_inc(S["gathered"], 1)
                        pe.wait_ge(S["picked"], u * 2 + 2)
                        for tt in range(TT):
                            ins = pe.transpose(bank[5][:, tok(tt)], pickw[:, tt, :], ident)
                        ins.then_inc(S["weights_turned"], 1)
                        arrived(base, pair)
                        arrived(base + 1, pair)
                        pe.wait_ge(S["xg_dve"], u + 1)
                        for k in range(KT):
                            if k == 4:
                                pe.wait_ge(S["xg_act"], u + 1)
                            for e in range(2):
                                ins = pe.matmul(bank[0][e * 64:(e + 1) * 64, :], xgT[:, k, e * 64:(e + 1) * 64],
                                                wv[e][:, k, :], start=(k == 0), stop=(k == KT - 1))
                        ins.then_inc(S["gate_done"], 1)
                        arrived(base + 2, pair)
                        arrived(base + 3, pair)
                        for f in range(2):
                            for k in range(KT):
                                for e in range(2):
                                    ins = pe.matmul(bank[(1, 6)[f]][e * 64:(e + 1) * 64, 0:256],
                                                    xgT[:, k, e * 64:(e + 1) * 64],
                                                    wv[2 + e][:, k, f * 256:(f + 1) * 256],
                                                    start=(k == 0), stop=(k == KT - 1))
                            ins.then_inc(S["up_done"], 1)
                        for f in range(2):
                            pe.wait_ge(S["hid_ready"], u * 2 + f + 1)
                            for j in range(2):
                                ins = pe.transpose(bank[(4, 7)[f]][:, j * P:(j + 1) * P],
                                                   hid[:, (2 * f + j) * P:(2 * f + j + 1) * P], ident)
                            ins.then_inc(S["hid_turned"], 1)
                        arrived(base + 4, pair)
                        arrived(base + 5, pair)
                        pe.wait_ge(S["hidT_act"], u + 1)
                        pe.wait_ge(S["hidT_dve"], u + 1)
                        for n2 in range(2):
                            for k in range(4):
                                for e in range(2):
                                    ins = pe.matmul(bank[6 + n2][e * 64:(e + 1) * 64, :],
                                                    hidT[:, k, e * 64:(e + 1) * 64],
                                                    wv[4 + e][:, k, n2 * 512:(n2 + 1) * 512],
                                                    start=(k == 0), stop=(k == 3))
                            ins.then_inc(S["down_done"], 1)
                        pe.wait_ge(S["pickwT_ready"], u + 1)
                        for n2 in range(2):
                            pe.wait_ge(S["yg_ready"], u * 2 + n2 + 1)
                            for tt in range(TT):
                                pe.matmul(bank[(2, 3, 0, 1)[2 * n2 + tt]][:], pickwT[:, tt, :],
                                          yg[:, n2 * 512:(n2 + 1) * 512], start=True, stop=True).then_inc(S["comb_done"], 1)

            experts(0)

            pe.wait_ge(h_ready, 8)
            turn_y(2)

            def item(name, k):
                i = AT[(name, 0)]
                arrived(i)
                return slot(i)

            kva = item("kva", 0)[:, 0:KT * 192].rearrange("p (k n) -> p k n", k=KT)
            pe.wait_ge(xn_dve, 12)
            pe.wait_ge(xn_act, 12)
            for tt in range(TT):
                for k in range(KT):
                    ins = pe.matmul(mla_bank[4][:, tt * KVL:(tt + 1) * KVL], hnT[:, k, tok(tt)], kva[:, k, 0:KVL],
                                    start=(k == 0), stop=(k == KT - 1))
            ins.then_inc(ck_raw, 1)
            for f in range(2):
                pe.wait_ge(rope_w, f + 1)
                for k in range(KT):
                    ins = pe.matmul(mla_bank[5][:, f * SEQ:(f + 1) * SEQ], kr_w[:, f, k, :], hnT[:, k, :],
                                    start=(k == 0), stop=(k == KT - 1))
            ins.then_inc(kr_raw, 1)
            qa = item("qa", 0)[:, 0:KT * QL].rearrange("p (k n) -> p k n", k=KT)
            pe.wait_ge(xn_dve, 16)
            pe.wait_ge(xn_act, 16)
            for tt in range(TT):
                for k in range(KT):
                    ins = pe.matmul(mla_bank[6][:, tt * QL:(tt + 1) * QL], xnT[:, k, tok(tt)], qa[:, k, :],
                                    start=(k == 0), stop=(k == KT - 1))
            ins.then_inc(qa_raw, 1)
            pe.wait_ge(lat_norm, 2)
            for tt in range(TT):
                ins = pe.transpose(mla_bank[7][:, tok(tt)], cn[:, tt, :], ident)
            ins.then_inc(lat_turned, 1)
            pe.wait_ge(lat_norm, 4)
            for j in range(2):
                for tt in range(TT):
                    ins = pe.transpose(mla_bank[0][:, (2 * j + tt) * P:(2 * j + tt + 1) * P], qn[:, tt, j * P:(j + 1) * P], ident)
            ins.then_inc(lat_turned, 1)
            kvb = item("kvb", 0)[:, 0:2048].rearrange("p (h n) -> p h n", h=MH)
            pe.wait_ge(ckT_ready, 1)
            for b in range(4):
                for j in range(2):
                    ins = pe.matmul(mla_bank[1 + b][:, j * SEQ:(j + 1) * SEQ], kvb[:, 2 * b + j, 0:NOPE], ckT, start=True, stop=True)
                ins.then_inc(kv_done, 1)
            pe.wait_ge(kr_mult, 2)
            pe.wait_ge(qaT_ready, 2)
            for tt in range(TT):
                for n in range(2):
                    b = (5, 6, 7, 0)[2 * tt + n]
                    ins = pe.matmul(mla_bank[b][:], ckT[:, tok(tt)], kvb[:, 4 * n:4 * n + 4, NOPE:NOPE + VH], start=True, stop=True)
                    ins.then_inc(kv_done, 1)
            qb = item("qb", 0)[:, 0:2 * 1536].rearrange("p (k h n) -> p k h n", k=2, h=MH)
            for b in range(4):
                if b % 2 == 0:
                    pe.wait_ge(kv_act, b // 2 + 1)
                else:
                    pe.wait_ge(kv_dve, b // 2 + 1)
                for j in range(2):
                    for k in range(2):
                        ins = pe.matmul(mla_bank[1 + b][:, j * SEQ:(j + 1) * SEQ], qb[:, k, 2 * b + j, 0:NOPE], qaT[:, k, :],
                                        start=(k == 0), stop=(k == 1))
                ins.then_inc(qb_done, 1)
            pe.wait_ge(kv_act, 4)
            pe.wait_ge(kv_dve, 4)
            for f in range(2):
                pe.wait_ge(rope_w, 3 + f)
                for g in range(2):
                    for k in range(2):
                        ins = pe.matmul(mla_bank[5 + f][:, g * SEQ:(g + 1) * SEQ],
                                        qr_w[:, f, k, g * P:(g + 1) * P],
                                        qaT[:, k, :], start=(k == 0), stop=(k == 1))
                ins.then_inc(qb_done, 1)

            def scores(hd):
                b = att_bank[hd % 3]
                if hd >= 3:
                    pe.wait_ge(att_exp, 2 * (hd - 2))
                q = 32 * (hd % 4)
                for tt in range(TT):
                    o = b[:, 0:P] if tt == 0 else b[:, P:P + SEQ]
                    keys = slice(0, P * (tt + 1))
                    pe.matmul(o, qnT[:, hd, tok(tt)], knT[:, hd, keys], start=True, stop=False)
                    for f in range(2):
                        ins = pe.matmul(o, qrT[q:q + HALF, f, hd // 4, tok(tt)], krT[q:q + HALF, f, keys],
                                        start=False, stop=(f == 1), tile_position=(q, 0))
                ins.then_inc(att_score, 1)

            def turn_probs(hd):
                b = mla_bank[1 + hd % 2]
                pe.wait_ge(att_prob, 2 * (hd + 1))
                if hd >= 2:
                    pe.wait_ge(probT_ready, hd - 1)
                for j in range(3):
                    ins = pe.transpose(b[:, tok(j)], prob[:, hd % 2, tok(j)], ident)
                ins.then_inc(prob_turned, 1)

            def attend(hd):
                b = mla_bank[3 + hd % 2]
                pe.wait_ge(probT_ready, hd + 1)
                if hd >= 2:
                    pe.wait_ge(oT_ready, hd - 1)
                v = vm[:, :, hd * VH:(hd + 1) * VH]
                pe.matmul(b[:, 0:P], v[:, 0, :], probT[:, hd % 2, 0:P], start=True, stop=True)
                pe.matmul(b[:, P:SEQ], v[:, 0, :], probT[:, hd % 2, P:SEQ], start=True, stop=False)
                pe.matmul(b[:, P:SEQ], v[:, 1, :], probT[:, hd % 2, SEQ:SEQ + P], start=False, stop=True).then_inc(att_o, 1)

            pe.wait_ge(qb_act, 2)
            pe.wait_ge(qb_dve, 2)
            pe.wait_ge(qr_ready, 2)
            pe.wait_ge(kr_ready, 2)
            scores(0)
            scores(1)
            for hd in range(MH):
                if hd + 2 < MH:
                    scores(hd + 2)
                turn_probs(hd)
                if hd:
                    attend(hd - 1)
            attend(MH - 1)
            pe.wait_ge(att_exp, 2 * MH)
            pe.wait_ge(oT_ready, MH)
            for i in range(2):
                w = item(f"wo{i}", 0).rearrange("p (k n) -> p k n", k=4)
                for tt in range(TT):
                    for n in range(2):
                        for kk in range(4):
                            ins = pe.matmul(mla_bank[(5, 6, 7, 0)[2 * tt + n]][:], oT[:, 4 * i + kk, tok(tt)],
                                            w[:, kk, n * 512:(n + 1) * 512],
                                            start=(i == 0 and kk == 0), stop=(i == 1 and kk == 3))
                        if i == 1:
                            ins.then_inc(mix_done, 1)
                        elif tt == 1 and n == 1:
                            ins.then_inc(wo_used, 1)
            experts(1)

        @block.scalar
        def _(act):
            A = act.activation
            act.dma_start(cst[:, 0:C_DECAY], t["constants"][:, 0:C_DECAY]).then_inc(cst_in, 16)
            act.dma_start(rows[104:120, :], t["norm_mix"].rearrange("l (r c) -> (l r) c", c=P)).then_inc(small_in, 16)
            act.dma_start(posi, t["positions"].to_broadcast([P, SEQ])).then_inc(pos_in, 16)
            act.dma_start(gains[0:16, :], t["b_mod_kv"].rearrange("(r c) -> r c", c=P)).then_inc(gains_in, 16)
            act.dma_start(gains[16:32, :], t["norm_ffn"].rearrange("l (r c) -> (l r) c", c=P)).then_inc(gains_in, 16)
            act.dma_start(gains[32:40, :], t["norm_kv"].rearrange("(r c) -> r c", c=P)).then_inc(gains_in, 16)
            act.dma_start(gains[40:41, :], t["mla_kv_norm"].rearrange("(r c) -> r c", c=P)).then_inc(gains_in, 16)
            act.dma_start(gains[41:43, :], t["mla_q_norm"].rearrange("l (r c) -> (l r) c", c=P)).then_inc(gains_in, 16)

            def late_loads():
                act.dma_start(cst[:, C_DECAY:C_ALL], t["constants"][:, C_DECAY:C_ALL]).then_inc(decay_in, 16)
                act.dma_start(wr[:], t["router_w"].rearrange("(k p) n -> p k n", p=P)).then_inc(router_in, 16)
                act.dma_start(br[:], t["router_b"].unsqueeze(0).to_broadcast([P, NE])).then_inc(router_in, 16)
                for i, (l, g) in enumerate(((0, 2), (0, 5), (1, 2), (1, 5))):
                    act.dma_start(gate[:, i, :], t["b_mod"][l:l + 1, g * D:(g + 1) * D].to_broadcast([P, D])).then_inc(gb_in, 16)

            def squares_of(n):
                for tt in range(TT):
                    if n:
                        act.wait_ge(h_ready, 4 * (n - 1) + 2 * (tt + 1))
                    else:
                        act.wait_ge(x_in, 16)
                    A(y[:, tt, :], h[:, tt, :], ACT.Square, accum_out=msq[:, tt:tt + 1]).then_inc(squares, 1)
                    act.wait_ge(meansq, 2 * n + tt + 1)
                    A(root[:, tt:tt + 1], var[:, tt:tt + 1], ACT.Sqrt).then_inc(roots, 1)

            def modulate(n, dst, which, shift):
                for b in (1, 3):
                    act.wait_ge(y_turned, 4 * n + b + 1)
                    for f in range(2):
                        k = 2 * b + f
                        A(dst[:, k, :], bank[4 + b][:, f * SEQ:(f + 1) * SEQ], ACT.Identity,
                          bias=modc[:, shift + k:shift + k + 1],
                          scale=scale[:, which, k:k + 1]).then_inc(xn_act, 1)

            act.wait_ge(cols_copied, 1)
            A(cact[:], cols[:, 0:8], ACT.Silu).then_inc(c_silu, 1)
            act.wait_ge(angles_ready, 2)
            A(trig[:, :, 1, :], rem, ACT.Sin).then_inc(trig_ready, 1)
            A(trig[:, :, 0, :], crem, ACT.Sin).then_inc(trig_ready, 1)
            squares_of(0)
            late_loads()

            def copy_head(hd, g):
                act.wait_ge(yh_turned, 2 * hd + g + 1)
                k = 4 * hd + 2 * g
                A(yTs[k // 8][:, k % 8:k % 8 + 2, :], bank[7][:].rearrange("p (k s) -> p k s", k=2),
                  ACT.Copy).then_inc(yT_copied, 1)

            act.wait_ge(scales_ready, 1)
            modulate(0, xnT, 0, MOD_COL[0])
            for r in range(12):
                hd = (r - 4) // 2
                if r >= 4 and r % 2 == 0:
                    for tt in range(TT):
                        act.wait_ge(win_done, 2 * r + tt + 1)
                        if hd >= 2:
                            act.wait_ge(o_done, 2 * (hd - 1))
                        A(vh[:, hd % 2, tt, :], bank[tt][:], ACT.Copy).then_inc(v_copied, 1)
                    if hd:
                        copy_head(hd - 1, 0)
                if r >= 4 and r % 2 == 1:
                    for tt in range(TT):
                        act.wait_ge(win_done, 2 * r + tt + 1)
                        if hd:
                            act.wait_ge(yh_ready, 2 * hd)
                        A(sg[:, tt, :], bank[2 + tt][:], ACT.Silu).then_inc(g_silu, 1)
                if r >= 4 and r % 2 == 0 and hd:
                    copy_head(hd - 1, 1)
                if r >= 4 and r % 2 == 1:
                    act.wait_ge(o_var, hd + 1)
                    A(root[:, 0:2], var[:, 0:2], ACT.Sqrt).then_inc(o_root, 1)
            copy_head(3, 0)
            copy_head(3, 1)

            def experts(l):
                n = 1 + 2 * l
                S = moe[l]
                squares_of(n)
                modulate(n, xnT, 1 + 2 * l, MOD_COL[l] + 24)
                act.wait_ge(logits, l + 1)
                for tt in range(TT):
                    A(score[:, tt, :], bank[tt][:, 0:NE], ACT.Sigmoid).then_inc(sig_ready, 1)
                act.wait_ge(bounds_ready, l + 1)
                with act.Fori(0, PAIRS) as pair:
                    begin = act.value_load(bounds[l][0:1, bass.ds(pair, 1)], min_val=0, max_val=ROUNDS * PAIRS)
                    end = act.value_load(bounds[l][0:1, bass.ds(pair + 1, 1)], min_val=1, max_val=ROUNDS * PAIRS)
                    with act.Fori(begin, end) as u:
                        act.wait_ge(S["gathered"], u * 2 + 2)
                        for j in range(4):
                            k = 4 + j
                            ins = A(xgT[:, k, :], bank[3][:, tok(j)], ACT.Identity,
                                    bias=modc[:, MOD_COL[l] + 24 + k:MOD_COL[l] + 25 + k],
                                    scale=scale[:, 1 + 2 * l, k:k + 1])
                        ins.then_inc(S["xg_act"], 1)
                        act.wait_ge(S["weights_turned"], u + 1)
                        A(pickwT.rearrange("p t s -> p (t s)"), bank[5][:, 0:SEQ], ACT.Copy).then_inc(S["pickwT_ready"], 1)
                        act.wait_ge(S["gate_done"], u + 1)
                        A(sil, bank[0][:], ACT.Silu).then_inc(S["sil_ready"], 1)
                        act.wait_ge(S["hid_turned"], u * 2 + 1)
                        A(hidT[:, 0:2, :], bank[4][:, 0:SEQ].rearrange("p (k s) -> p k s", k=2), ACT.Copy).then_inc(S["hidT_act"], 1)
                        for n2 in range(2):
                            act.wait_ge(S["down_done"], u * 2 + n2 + 1)
                            A(yg[:, n2 * 512:(n2 + 1) * 512], bank[6 + n2][:], ACT.Copy).then_inc(S["yg_ready"], 1)

            experts(0)
            act.dma_start(gate[:, 0, :], t["final_norm"].unsqueeze(0).to_broadcast([P, D])).then_inc(fn_in, 16)
            squares_of(2)
            modulate(2, hnT, 4, MOD_COL[2])
            modulate(2, xnT, 2, MOD_COL[1])
            for tt in range(TT):
                act.wait_ge(ck_raw, 1)
                A(cn[:, tt, :], mla_bank[4][:, tt * KVL:(tt + 1) * KVL], ACT.Square, accum_out=msq[:, tt:tt + 1]).then_inc(lat_sq, 1)
            for tt in range(TT):
                act.wait_ge(qa_raw, 1)
                A(qn[:, tt, :], mla_bank[6][:, tt * QL:(tt + 1) * QL], ACT.Square, accum_out=msq[:, 2 + tt:3 + tt]).then_inc(lat_sq, 1)
            act.wait_ge(lat_ms, 2)
            A(root[:, 0:4], var[:, 0:4], ACT.Sqrt).then_inc(lat_root, 1)
            act.wait_ge(lat_turned, 1)
            A(ckT, mla_bank[7][:, 0:SEQ], ACT.Copy, scale=gcol[:, 40:41]).then_inc(ckT_ready, 1)
            for b in (1, 3):
                act.wait_ge(kv_done, b)
                A(knT[:, 2 * (b - 1):2 * b, :], mla_bank[b][:].rearrange("p (k s) -> p k s", k=2), ACT.Copy).then_inc(kv_act, 1)
            for b in (0, 2):
                act.wait_ge(kv_done, 4 + b + 1)
                A(vm[:, b // 2, 0:512], mla_bank[5 + b][:], ACT.Copy).then_inc(kv_act, 1)
            for b in (1, 3):
                act.wait_ge(qb_done, b)
                A(qnT[:, 2 * (b - 1):2 * b, :], mla_bank[b][:].rearrange("p (k s) -> p k s", k=2), ACT.Copy).then_inc(qb_act, 1)

            def head_exp(hd):
                act.wait_ge(att_max, hd + 1)
                if hd >= 2:
                    act.wait_ge(prob_turned, hd - 1)
                b = att_bank[hd % 3]
                for tt in range(TT):
                    s = slice(0, P) if tt == 0 else slice(P, P + SEQ)
                    A(prob[:, hd % 2, s], b[:, s], ACT.Exp, bias=smax[:, hd % 3, tt:tt + 1], scale=SOFT,
                      accum_out=ssum[:, hd % 2, tt:tt + 1]).then_inc(att_exp, 1)

            def head_turned(hd):
                act.wait_ge(prob_turned, hd + 1)
                if hd >= 2:
                    act.wait_ge(att_o, hd - 1)
                A(probT[:, hd % 2, :], mla_bank[1 + hd % 2][:, 0:384], ACT.Copy).then_inc(probT_ready, 1)

            def head_out(hd):
                act.wait_ge(att_o, hd + 1)
                A(oT[:, hd, :], mla_bank[3 + hd % 2][:, 0:SEQ], ACT.Copy).then_inc(oT_ready, 1)

            head_exp(0)
            for hd in range(MH):
                if hd + 1 < MH:
                    head_exp(hd + 1)
                head_turned(hd)
                if hd:
                    head_out(hd - 1)
            head_out(MH - 1)
            experts(1)
            squares_of(4)

        @block.vector
        def _(dve):
            own = Count(dstep)

            def normed(n):
                for tt in range(TT):
                    one = slice(tt, tt + 1)
                    dve.wait_ge(squares, 2 * n + tt + 1)
                    dve.tensor_scalar(var[:, one], msq[:, one], 1.0 / D, EPS, ALU.mult, ALU.add).then_inc(meansq, 1)
                    dve.wait_ge(roots, 2 * n + tt + 1)
                    own.step(dve, dve.reciprocal(rstd[:, one], root[:, one]))
                    dve.tensor_scalar(y[:, tt, :], h[:, tt, :], rstd[:, one], None, ALU.mult).then_inc(y_ready, 1)

            def modulate(n, dst, which, shift):
                for b in (0, 2):
                    dve.wait_ge(y_turned, 4 * n + b + 1)
                    for f in range(2):
                        k = 2 * b + f
                        dve.tensor_scalar(dst[:, k, :], bank[4 + b][:, f * SEQ:(f + 1) * SEQ], scale[:, which, k:k + 1],
                                          modc[:, shift + k:shift + k + 1], ALU.mult, ALU.add).then_inc(xn_dve, 1)

            own.step(dve, dve.memset(zeros[:], 0.0))
            own.step(dve, dve.memset(boundf[:], 0.0))
            dve.wait_ge(rows_turned, 1)
            dve.tensor_copy(cols[:], bank[4][:, 0:120]).then_inc(cols_copied, 1)
            dve.wait_ge(pos_in, 16)
            own.step(dve, dve.tensor_copy(posf, posi))
            own.step(dve, dve.tensor_scalar(ang[:, 0, :], posf, cst[:, C_FREQ:C_FREQ + 1], None, ALU.mult))
            own.step(dve, dve.tensor_scalar(ang[:, 1, :], posf, cst[:, C_FREQ + 1:C_FREQ + 2], None, ALU.mult))
            nearest = 12582912.0
            own.step(dve, dve.tensor_scalar(turns, ang, float(1 / (2 * np.pi)), nearest, ALU.mult, ALU.add))
            own.step(dve, dve.tensor_scalar(turns, turns, nearest, None, ALU.subtract))
            first = 6.28125
            second = float(np.float32(round((2 * np.pi - first) * 2 ** 22) / 2 ** 22))
            third = float(2 * np.pi - first - second)
            own.step(dve, dve.scalar_tensor_tensor(rem, turns, -first, ang, ALU.mult, ALU.add))
            own.step(dve, dve.scalar_tensor_tensor(rem, turns, -second, rem, ALU.mult, ALU.add))
            own.step(dve, dve.scalar_tensor_tensor(rem, turns, -third, rem, ALU.mult, ALU.add))
            dve.tensor_scalar(rem, rem, -3.1415925, 3.1415925, ALU.max, ALU.min).then_inc(angles_ready, 1)
            dve.wait_ge(angles_ready, 1)
            own.step(dve, dve.scalar_tensor_tensor(crem, rem, -1.0, rem, ALU.mult, ALU.max))
            dve.tensor_scalar(crem, crem, -1.0, float(np.pi / 2), ALU.mult, ALU.add).then_inc(angles_ready, 1)

            steps = Count(mod_step)

            def mod_main(m):
                i = AT[("mod", m)]
                w = slot(i).rearrange("p (k n) -> p k n", k=KT)
                o = part[:, m % 2, :]
                dve.wait_ge(landed[i % RING], 16 * (i // RING + 1))
                if m >= 2:
                    dve.wait_ge(mod_folded, m - 1)
                steps.step(dve, dve.tensor_scalar(o, w[:, 0, :], cact[:, 0:1], None, ALU.mult))
                for k in range(1, KT):
                    ins = dve.scalar_tensor_tensor(o, w[:, k, :], cact[:, k:k + 1], o, ALU.mult, ALU.add)
                    if k < KT - 1:
                        steps.step(dve, ins)
                ins.then_inc(mod_sum, 1)

            def mod_store(m):
                w, b = MOD[m]
                src = bank[4 + m % 2]
                dve.wait_ge(mod_folded, m + 1)
                if (w, b) in GATES:
                    g = GATES[(w, b)]
                    if m == 4:
                        dve.wait_ge(gb_in, 16 * 4)
                    o = gate[:, g, (b % 2) * 512:(b % 2) * 512 + 512]
                    dve.tensor_tensor(o, src[:], o, ALU.add).then_inc(mod_stored, 1)
                else:
                    c = MOD_COL[w] + 4 * b
                    bias = gcol[:, 4 * b:4 * b + 4] if w == 2 else cols[:, 8 + c:12 + c]
                    dve.tensor_tensor(modc[:, c:c + 4], src[:, 0:4], bias, ALU.add).then_inc(mod_stored, 1)

            scale_steps = Count(scales_ready)

            def scales(which, scol, gain):
                scale_steps.step(dve, dve.scalar_tensor_tensor(scale[:, which, :], modc[:, scol:scol + 8], 1.0,
                                                               gain, ALU.add, ALU.mult))

            dve.wait_ge(c_silu, 1)
            for m in range(FIRST_MOD):
                mod_main(m)
                if m == 1:
                    normed(0)
                if m:
                    mod_store(m - 1)
            mod_store(FIRST_MOD - 1)
            dve.wait_ge(mod_stored, FIRST_MOD)
            scales(0, MOD_COL[0] + 8, cols[:, 104:112])
            dve.wait_ge(gains_turned, 1)
            dve.tensor_copy(gcol[:], bank[0][:, 0:43]).then_inc(gcol_copied, 1)
            modulate(0, xnT, 0, MOD_COL[0])

            for r in range(12):
                hd = (r - 4) // 2
                for m in ROUND_MODS[r]:
                    mod_main(m)
                if r < 4:
                    for b in range(2):
                        n = 2 * r + b
                        dve.wait_ge(win_done, n + 1)
                        dve.wait_ge(trig_ready, 2)
                        if n:
                            dve.wait_ge(rope_done, n)
                        src = bank[2 * (r % 2) + b][:].rearrange("p (f s) -> p f s", f=2)
                        for i in range(2):
                            w = trig[:, 0, i:i + 1, :].to_broadcast([P, 2, SEQ])
                            ins = dve.tensor_tensor(prod[:, i, :].rearrange("p (f s) -> p f s", f=2), src, w, ALU.mult)
                        ins.then_inc(rope_mult, 1)
                if r >= 4 and r % 2 == 0:
                    dec = cst[:, C_DECAY + hd * SEQ:C_DECAY + (hd + 1) * SEQ]
                    dve.wait_ge(ret_scores, hd + 1)
                    dve.wait_ge(decay_in, 16)
                    dve.tensor_tensor(inner[:, 0:SEQ], bank[6][:, 0:SEQ], dec, ALU.mult).then_inc(inner_ready, 1)
                    dve.tensor_tensor(inner[:, SEQ:SEQ + P], bank[6][:, SEQ:SEQ + P], dec[:, 0:P], ALU.mult).then_inc(inner_ready, 1)
                for m in ROUND_MODS[r]:
                    mod_store(m)
                if r >= 4 and r % 2 == 1:
                    for tt in range(TT):
                        dve.wait_ge(o_done, 2 * hd + tt + 1)
                        own.step(dve, dve.bn_stats(bn[:, tt, :], bank[2 + tt][:]))
                        own.step(dve, dve.bn_aggr(mv[:, tt, :], bn[:, tt, :]))
                    dve.tensor_scalar(var[:, 0:2], mv[:, :, 1], EPS, None, ALU.add).then_inc(o_var, 1)
                    dve.wait_ge(o_root, hd + 1)
                    own.step(dve, dve.reciprocal(rstd[:, 0:2], root[:, 0:2]))
                    if hd:
                        dve.wait_ge(yh_turned, 2 * hd)
                    for tt in range(TT):
                        dve.tensor_scalar(on[:, tt, :], bank[2 + tt][:], mv[:, tt, 0:1], rstd[:, tt:tt + 1],
                                          ALU.subtract, ALU.mult).then_inc(o_norm, 1)
                    for tt in range(TT):
                        dve.wait_ge(o_norm, 2 * hd + tt + 1)
                        dve.wait_ge(g_silu, 2 * hd + tt + 1)
                        dve.tensor_tensor(on[:, tt, :], on[:, tt, :], sg[:, tt, :], ALU.mult).then_inc(yh_ready, 1)
            for m in LAST_MODS:
                mod_main(m)
            for m in LAST_MODS:
                mod_store(m)
            dve.wait_ge(mod_stored, len(MOD))
            scales(1, MOD_COL[0] + 32, gcol[:, 16:24])
            scales(2, MOD_COL[1] + 8, cols[:, 112:120])
            scales(3, MOD_COL[1] + 32, gcol[:, 24:32])
            scales(4, MOD_COL[2] + 8, gcol[:, 32:40])

            def mixed(l, banks):
                for i in range(4):
                    tt, n = i // 2, i % 2
                    s = slice(n * 512, (n + 1) * 512)
                    dve.wait_ge(mix_done, 4 * l + i + 1)
                    dve.tensor_tensor(acc[:, tt, s], bank[banks[i]][:], gate[:, 2 * l, s], ALU.mult).then_inc(h_prod, 1)

            def experts(l):
                n = 1 + 2 * l
                S = moe[l]
                normed(n)
                modulate(n, xnT, 1 + 2 * l, MOD_COL[l] + 24)
                dve.wait_ge(sig_ready, 2 * l + 2)
                G = TT * NG
                own.step(dve, dve.tensor_tensor(biased[:], score[:], br[:].unsqueeze(1).to_broadcast([P, TT, NE]), ALU.add))
                flat = biased[:].rearrange("p t (g e) -> p (t g) e", g=NG)

                def ranks(values, groups, dst):
                    n = groups * EG * EG
                    c1 = cmp1[:, 0:n].rearrange("p (g i j) -> p g i j", i=EG, j=EG)
                    c2 = cmp2[:, 0:n].rearrange("p (g i j) -> p g i j", i=EG, j=EG)
                    mine = values.unsqueeze(3).to_broadcast([P, groups, EG, EG])
                    theirs = values.unsqueeze(2).to_broadcast([P, groups, EG, EG])
                    earlier = cst[:, C_EARLIER:C_EARLIER + EG * EG].unsqueeze(1).to_broadcast([P, groups, EG * EG])
                    own.step(dve, dve.tensor_tensor(c1, theirs, mine, ALU.is_gt))
                    own.step(dve, dve.tensor_tensor(c2, theirs, mine, ALU.is_equal))
                    f2 = cmp2[:, 0:n].rearrange("p (g i) -> p g i", i=EG * EG)
                    own.step(dve, dve.tensor_tensor(f2, f2, earlier, ALU.mult))
                    own.step(dve, dve.tensor_tensor(cmp1[:, 0:n], cmp1[:, 0:n], cmp2[:, 0:n], ALU.add))
                    own.step(dve, dve.tensor_reduce(dst, cmp1[:, 0:n].rearrange("p (i j) -> p i j", j=EG), AX.X, ALU.add))

                ranks(flat, G, rank[:])
                own.step(dve, dve.tensor_scalar(rank[:], rank[:], 2.0, None, ALU.is_lt))
                two = cmp1[:, 0:TT * NE]
                own.step(dve, dve.tensor_tensor(two, rank[:], biased[:].rearrange("p t e -> p (t e)"), ALU.mult))
                own.step(dve, dve.tensor_reduce(gsum[:], two.rearrange("p (g e) -> p g e", e=EG), AX.X, ALU.add))
                ranks(gsum[:].rearrange("p (t g) -> p t g", g=NG), TT, grank[:])
                own.step(dve, dve.tensor_scalar(grank[:], grank[:], 1.0, None, ALU.is_lt))
                dve.tensor_tensor(chosen[:].rearrange("p t (g e) -> p (t g) e", g=NG),
                                  rank[:].rearrange("p (g e) -> p g e", e=EG),
                                  grank[:].unsqueeze(2).to_broadcast([P, G, EG]), ALU.mult).then_inc(chosen_ready, 1)
                dve.wait_ge(chosen_ready, l + 1)
                own.step(dve, dve.tensor_tensor(combine[:], score[:], chosen[:], ALU.mult))
                own.step(dve, dve.tensor_reduce(den[:], combine[:], AX.X, ALU.add))
                own.step(dve, dve.reciprocal(den[:], den[:]))
                own.step(dve, dve.tensor_tensor(combine[:], combine[:], den[:].unsqueeze(2).to_broadcast([P, TT, NE]), ALU.mult))
                dve.wait_ge(ranked, l + 1)
                own.step(dve, dve.tensor_copy(cmp2[:, 0:3 * NE], bank[2][:, 0:3 * NE]))
                own.step(dve, dve.scalar_tensor_tensor(place[:].rearrange("p t e -> p (t e)"), cmp2[:, 0:2 * NE], 1.0,
                                                       chosen[:].rearrange("p t e -> p (t e)"), ALU.add, ALU.mult))
                own.step(dve, dve.tensor_scalar(place[:], place[:], 1.0, None, ALU.subtract))
                own.step(dve, dve.tensor_reduce(most[:, 0, :], cmp2[:, 2 * NE:3 * NE].rearrange("p (g e) -> p g e", e=2), AX.X, ALU.max))
                own.step(dve, dve.tensor_scalar(most[:, 1, :], most[:, 0, :], float(SLOTS) + 0.5, 1.0, ALU.is_gt, ALU.add))
                for r in range(2, ROUNDS):
                    own.step(dve, dve.scalar_tensor_tensor(most[:, 1, :], most[:, 0, :], float(r * SLOTS) + 0.5, most[:, 1, :], ALU.is_gt, ALU.add))
                own.step(dve, dve.tensor_tensor_scan(boundf[:, 1:PAIRS + 1], zeros[:, 0:PAIRS], most[0:1, 1, :], 0.0,
                                                     ALU.add, ALU.add))
                dve.tensor_copy(bounds[l][0:1, :], boundf[:]).then_inc(bounds_ready, 1)
                dve.wait_ge(bounds_ready, l + 1)
                with dve.Fori(0, PAIRS) as pair:
                    begin = dve.value_load(bounds[l][0:1, bass.ds(pair, 1)], min_val=0, max_val=ROUNDS * PAIRS)
                    end = dve.value_load(bounds[l][0:1, bass.ds(pair + 1, 1)], min_val=1, max_val=ROUNDS * PAIRS)
                    dve.tensor_copy(slot_id[:], slots0).then_inc(S["slots_ready"], 1)
                    with dve.Fori(begin, end) as u:
                        dve.wait_ge(S["slots_ready"], pair + u + 1)
                        four = [P, TT, 2, SLOTS]
                        v, vw = (x.rearrange("p t (e s) -> p t e s", e=2) for x in (pick, pickw))
                        dve.tensor_tensor(v, slot_id[:].unsqueeze(1).unsqueeze(1).to_broadcast(four),
                                          place[:, :, bass.ds(pair * 2, 2)].unsqueeze(3).to_broadcast(four),
                                          ALU.is_equal).then_inc(S["picked"], 1)
                        dve.wait_ge(S["picked"], u * 2 + 1)
                        dve.tensor_tensor(vw, v, combine[:, :, bass.ds(pair * 2, 2)].unsqueeze(3).to_broadcast(four),
                                          ALU.mult).then_inc(S["picked"], 1)
                        dve.tensor_scalar(slot_id[:], slot_id[:], float(SLOTS), None, ALU.add).then_inc(S["slots_ready"], 1)
                        dve.wait_ge(S["gathered"], u * 2 + 1)
                        for k in range(4):
                            ins = dve.tensor_scalar(xgT[:, k, :], bank[2][:, tok(k)], scale[:, 1 + 2 * l, k:k + 1],
                                                    modc[:, MOD_COL[l] + 24 + k:MOD_COL[l] + 25 + k], ALU.mult, ALU.add)
                        ins.then_inc(S["xg_dve"], 1)
                        dve.wait_ge(S["sil_ready"], u + 1)
                        for f in range(2):
                            s = slice(f * 256, (f + 1) * 256)
                            dve.wait_ge(S["up_done"], u * 2 + f + 1)
                            dve.tensor_tensor(hid[:, s], bank[(1, 6)[f]][:, 0:256], sil[:, s], ALU.mult).then_inc(S["hid_ready"], 1)
                        dve.wait_ge(S["hid_turned"], u * 2 + 2)
                        dve.tensor_copy(hidT[:, 2:4, :], bank[7][:, 0:SEQ].rearrange("p (k s) -> p k s", k=2)).then_inc(S["hidT_dve"], 1)
                        for i in range(4):
                            n2, tt = i // 2, i % 2
                            a = acc[:, tt, n2 * 512:(n2 + 1) * 512]
                            dve.wait_ge(S["comb_done"], u * 4 + i + 1)
                            dve.tensor_tensor(a, bank[(2, 3, 0, 1)[i]][:], a, ALU.add).then_inc(S["acc_added"], 1)
                total = dve.value_load(bounds[l][0:1, PAIRS:PAIRS + 1], min_val=PAIRS, max_val=ROUNDS * PAIRS)
                dve.wait_ge(S["acc_added"], total * 4 + 1)
                for i in range(4):
                    tt, n2 = i // 2, i % 2
                    s = slice(n2 * 512, (n2 + 1) * 512)
                    dve.tensor_tensor(acc[:, tt, s], acc[:, tt, s], gate[:, 2 * l + 1, s], ALU.mult).then_inc(h_prod, 1)

            mixed(0, (0, 1, 2, 3))
            experts(0)
            normed(2)
            modulate(2, hnT, 4, MOD_COL[2])
            modulate(2, xnT, 2, MOD_COL[1])
            dve.wait_ge(kr_raw, 1)
            for i in range(2):
                w = trig[:, 1, i:i + 1, :].to_broadcast([P, 2, SEQ])
                dve.tensor_tensor(mprod[:, i, :].rearrange("p (f s) -> p f s", f=2),
                                  mla_bank[5][:].rearrange("p (f s) -> p f s", f=2), w, ALU.mult).then_inc(kr_mult, 1)
            dve.wait_ge(lat_sq, 4)
            dve.tensor_scalar(var[:, 0:2], msq[:, 0:2], 1.0 / KVL, EPS, ALU.mult, ALU.add).then_inc(lat_ms, 1)
            dve.tensor_scalar(var[:, 2:4], msq[:, 2:4], 1.0 / QL, EPS, ALU.mult, ALU.add).then_inc(lat_ms, 1)
            dve.wait_ge(lat_root, 1)
            own.step(dve, dve.reciprocal(rstd[:, 0:4], root[:, 0:4]))
            for tt in range(TT):
                dve.tensor_scalar(cn[:, tt, :], mla_bank[4][:, tt * KVL:(tt + 1) * KVL], rstd[:, tt:tt + 1], None, ALU.mult).then_inc(lat_norm, 1)
            for tt in range(TT):
                dve.tensor_scalar(qn[:, tt, :], mla_bank[6][:, tt * QL:(tt + 1) * QL], rstd[:, 2 + tt:3 + tt], None, ALU.mult).then_inc(lat_norm, 1)
            dve.wait_ge(lat_turned, 2)
            for j in range(2):
                dve.tensor_scalar(qaT[:, j, :], mla_bank[0][:, j * SEQ:(j + 1) * SEQ], gcol[:, 41 + j:42 + j], None, ALU.mult).then_inc(qaT_ready, 1)
            for b in (2, 4):
                dve.wait_ge(kv_done, b)
                dve.tensor_copy(knT[:, 2 * (b - 1):2 * b, :], mla_bank[b][:].rearrange("p (k s) -> p k s", k=2)).then_inc(kv_dve, 1)
            for b in (1, 3):
                dve.wait_ge(kv_done, 4 + b + 1)
                dve.tensor_copy(vm[:, b // 2, 512:1024], mla_bank[(5, 6, 7, 0)[b]][:]).then_inc(kv_dve, 1)
            for b in (2, 4):
                dve.wait_ge(qb_done, b)
                dve.tensor_copy(qnT[:, 2 * (b - 1):2 * b, :], mla_bank[b][:].rearrange("p (k s) -> p k s", k=2)).then_inc(qb_dve, 1)
            dve.wait_ge(kr_ready, 2)
            for f in range(2):
                dve.wait_ge(qb_done, 5 + f)
                for i in range(2):
                    w = trig[:, 1, i:i + 1, :].to_broadcast([P, 2, SEQ])
                    dve.tensor_tensor(mprod[:, 2 * f + i, :].rearrange("p (f s) -> p f s", f=2),
                                      mla_bank[5 + f][:].rearrange("p (f s) -> p f s", f=2), w, ALU.mult).then_inc(qr_mult, 1)

            def head_max(hd):
                b = att_bank[hd % 3]
                m = smax[:, hd % 3, :]
                dve.wait_ge(att_score, hd + 1)
                if hd >= 3:
                    dve.wait_ge(att_exp, 2 * (hd - 2))
                for s in (slice(CH, P), slice(P + 3 * CH, P + 4 * CH)):
                    dve.tensor_scalar(b[0:CH, s], b[0:CH, s], -3e38, None, ALU.add).then_inc(att_masked, 1)
                for tt, s in enumerate((slice(0, P), slice(P, P + SEQ))):
                    dve.wait_ge(att_masked, 2 * hd + tt + 1)
                    dve.tensor_reduce(m[:, tt:tt + 1], b[:, s], AX.X, ALU.max).then_inc(att_top, 1)
                dve.wait_ge(att_top, 2 * hd + 2)
                dve.tensor_scalar(m, m, -SOFT, None, ALU.mult).then_inc(att_max, 1)

            def head_scale(hd):
                dve.wait_ge(att_exp, 2 * (hd + 1))
                own.step(dve, dve.reciprocal(srec[:, hd % 2, :], ssum[:, hd % 2, :]))
                for tt, s in enumerate((slice(0, P), slice(P, P + SEQ))):
                    dve.tensor_scalar(prob[:, hd % 2, s], prob[:, hd % 2, s], srec[:, hd % 2, tt:tt + 1], None,
                                      ALU.mult).then_inc(att_prob, 1)

            head_max(0)
            head_max(1)
            for hd in range(MH):
                head_scale(hd)
                if hd + 2 < MH:
                    head_max(hd + 2)
            mixed(1, (1, 2, 3, 4))
            experts(1)
            dve.wait_ge(fn_in, 16)
            normed(4)
            for tt in range(TT):
                dve.wait_ge(y_ready, 8 + tt + 1)
                dve.tensor_tensor(acc[:, tt, :], y[:, tt, :], gate[:, 0, :], ALU.mult).then_inc(h_ready, 1)

        @block.gpsimd
        def _(pool):
            for n in range(8):
                pool.wait_ge(rope_mult, n + 1)
                r, b = n // 2, n % 2
                dst = (qT, kT)[r % 2]
                k = 4 * (r // 2) + 2 * b
                pool.tensor_tensor(dst[:, k, :], prod[:, 0, 0:SEQ], prod[:, 1, SEQ:2 * SEQ], ALU.subtract)
                pool.tensor_tensor(dst[:, k + 1, :], prod[:, 1, 0:SEQ], prod[:, 0, SEQ:2 * SEQ], ALU.add).then_inc(rope_done, 1)

            def into_h(s):
                for i in range(4):
                    tt, n = i // 2, i % 2
                    c = slice(n * 512, (n + 1) * 512)
                    pool.wait_ge(h_prod, 4 * s + i + 1)
                    pool.tensor_tensor(h[:, tt, c], h[:, tt, c], acc[:, tt, c], ALU.add).then_inc(h_ready, 1)

            def experts(l):
                S = moe[l]
                pool.wait_ge(h_ready, 8 * l + 4)
                pool.memset(acc[:].rearrange("p t n -> p (t n)"), 0.0).then_inc(S["acc_added"], 1)
                into_h(1 + 2 * l)

            into_h(0)
            experts(0)
            kva = slot(MLA_AT)[:, 0:KT * 192].rearrange("p (k n) -> p k n", k=KT)
            pool.wait_ge(landed[MLA_AT % RING], 16 * (MLA_AT // RING + 1))
            for f in range(2):
                src = kva[:, :, KVL + f * HALF:KVL + (f + 1) * HALF]
                pool.tensor_copy(kr_w[:, f].rearrange("p k (c n) -> p k c n", c=4),
                                 src.unsqueeze(2).to_broadcast([P, KT, 4, HALF])).then_inc(rope_w, 1)
            qb = slot(MLA_AT + 3)[:, 0:3072].rearrange("p (k h n) -> p k h n", k=2, h=MH)
            pool.wait_ge(landed[(MLA_AT + 3) % RING], 16 * ((MLA_AT + 3) // RING + 1))
            for f in range(2):
                pool.tensor_copy(qr_w[:, f].rearrange("p k (h n) -> p k h n", h=MH),
                                 qb[:, :, :, NOPE + f * HALF:NOPE + (f + 1) * HALF]).then_inc(rope_w, 1)
            pool.wait_ge(kr_mult, 2)
            pool.tensor_tensor(krT[:, 0, :], mprod[:, 0, 0:SEQ], mprod[:, 1, SEQ:2 * SEQ], ALU.subtract).then_inc(kr_ready, 1)
            pool.tensor_tensor(krT[:, 1, :], mprod[:, 1, 0:SEQ], mprod[:, 0, SEQ:2 * SEQ], ALU.add).then_inc(kr_ready, 1)
            pool.wait_ge(qr_mult, 4)
            pool.tensor_tensor(qrT[:, 0, :, :].rearrange("p g s -> p (g s)"), mprod[:, 0, :], mprod[:, 3, :], ALU.subtract).then_inc(qr_ready, 1)
            pool.tensor_tensor(qrT[:, 1, :, :].rearrange("p g s -> p (g s)"), mprod[:, 1, :], mprod[:, 2, :], ALU.add).then_inc(qr_ready, 1)
            into_h(2)
            experts(1)


_INS = ["x", "c", "positions", "w_mod", "b_mod", "norm_mix", "norm_ffn", "ret_w_in", "ret_w_out", "w_mod_kv",
        "b_mod_kv", "norm_kv", "mla_w_kv_a", "mla_kv_norm", "mla_w_kv_b", "mla_w_q_a", "mla_q_norm", "mla_w_q_b",
        "mla_w_o", "router_w", "router_b", "moe_w_gate", "moe_w_up", "moe_w_down", "final_norm"]


def kernel(**inputs):
    import concourse.bacc as bacc
    from concourse.bass_utils import run_bass_kernel_spmd as run

    nc = bacc.Bacc("TRN2", target_bir_lowering=False, num_devices=1)
    arrays = {"constants": constants()}
    arrays.update({name: np.ascontiguousarray(inputs[name]) for name in _INS})
    args = {name: nc.dram_tensor(f"in_{name}", a.shape, mybir.dt.from_np(a.dtype), kind="ExternalInput").ap()
            for name, a in arrays.items()}
    out = nc.dram_tensor("out", (1, SEQ, D), F32, kind="ExternalOutput").ap()
    build_kernel(nc, args, out)
    r = run(nc, [{f"in_{name}": a for name, a in arrays.items()}], core_ids=[0])
    return r.results[0]["out"]
```

```python
from contextlib import ExitStack

import numpy as np

import concourse.bass as bass
from concourse import mybir

F32 = mybir.dt.float32
I32 = mybir.dt.int32
ALU = mybir.AluOpType
ACT = mybir.ActivationFunctionType
AX = mybir.AxisListType

P = 128
D = 1024
KT = D // P
SEQ = 256
TT = SEQ // P
EPS = 1e-6
RH, RDK = 4, 256
MH, NOPE, ROPE, VH = 8, 128, 64, 128
HALF = ROPE // 2
QL, KVL = 256, 128
NE, NG, EG = 16, 4, 4
DE = 512
PAIRS = NE // 2
SLOTS = 64
ROUNDS = SEQ // SLOTS
CH = 64
SOFT = float(NOPE + ROPE) ** -0.5
RING = 6

C_IDENT = 0
C_TRI = C_IDENT + P
C_ONES = C_TRI + P
C_SLOT = C_ONES + P
C_EARLIER = C_SLOT + SLOTS
C_SUM4 = C_EARLIER + EG * EG
C_ROW = C_SUM4 + NE
C_FREQ = C_ROW + 2 * P - 1
C_DECAY = C_FREQ + 2
C_ALL = C_DECAY + RH * SEQ


def constants():
    c = np.zeros((P, C_ALL), np.float32)
    i = np.arange(P)
    c[:, C_IDENT:C_IDENT + P] = np.eye(P)
    c[:, C_TRI:C_TRI + P] = i[:, None] < i[None, :]
    c[:, C_ONES:C_ONES + P] = 1
    c[:, C_SLOT:C_SLOT + SLOTS] = np.arange(SLOTS)
    for e in range(NE):
        c[e::32, C_SUM4 + e] = 1
    c[:, C_ROW + P - 1] = 1
    j = np.arange(EG)
    c[:, C_EARLIER:C_EARLIER + EG * EG] = (j[None, :] < j[:, None]).reshape(-1)
    c[:, C_FREQ] = 10000.0 ** (-i / P)
    c[:, C_FREQ + 1] = np.tile(10000.0 ** (-i[:HALF] / HALF), P // HALF)
    n = np.arange(SEQ)
    for h in range(RH):
        g = np.log1p(-(2.0 ** (-5.0 - h)))
        d = n[None, :] - i[:, None]
        c[:, C_DECAY + h * SEQ:C_DECAY + (h + 1) * SEQ] = np.where(d >= 0, np.exp(g * np.maximum(d, 0)), 0) * RDK ** -0.5
    return c


MOD = [(0, b) for b in range(12)] + [(2, b) for b in range(4)] + [(1, b) for b in range(12)]
FIRST_MOD = 4
MOD_COL = {0: 0, 1: 48, 2: 96}
GATES = {(0, 4): 0, (0, 5): 0, (0, 10): 1, (0, 11): 1, (1, 4): 2, (1, 5): 2, (1, 10): 3, (1, 11): 3}
VECS = [(0, 6, 24), (2, 0, 96), (1, 0, 48), (1, 6, 72)]
ROW_OF = {(w, b0 + i): (i % 2, 2 * n + i // 2) for n, (w, b0, _) in enumerate(VECS) for i in range(4)}
LAST_VEC = max(m for m in range(len(MOD)) if MOD[m] not in GATES)
WIN = [0, 2, 1, 3] + [b for h in range(RH) for b in (4 + h, 8 + h)]

STREAM = [("mod", m) for m in range(FIRST_MOD)]
MODS_PER_ROUND = (0, 1, 1, 2, 2, 2, 2, 2, 2, 2, 2, 2)
ROUND_MODS = []
_m = FIRST_MOD
for _r in range(12):
    ROUND_MODS.append(list(range(_m, _m + MODS_PER_ROUND[_r])))
    _m += len(ROUND_MODS[-1])
    STREAM += [("win", _r)] + [("mod", m) for m in ROUND_MODS[-1]]
LAST_MODS = list(range(_m, len(MOD)))
STREAM += [("wout", i) for i in range(3)] + [("mod", m) for m in LAST_MODS[:3]] + [("wout", 3)]
STREAM += [("mod", m) for m in LAST_MODS[3:]]
N_RET = len(STREAM)
OUTSIDE = 4
ARENA = 11520
MOE_AT = [N_RET, N_RET + 6 * PAIRS - OUTSIDE + 6]
MLA_AT = N_RET + 6 * PAIRS - OUTSIDE
MLA_ITEMS = ["kva", "qa", "kvb", "qb", "wo0", "wo1"]
AT = {item: i for i, item in enumerate(STREAM)}
AT.update({(name, 0): MLA_AT + i for i, name in enumerate(MLA_ITEMS)})


def build_kernel(nc, t, out):
    with ExitStack() as ctx:
        def sb(name, shape, dt=F32):
            return ctx.enter_context(nc.sbuf_tensor(name, shape, dt))

        def sem(name):
            return ctx.enter_context(nc.semaphore(name))

        ring = sb("ring", [P, RING, 4096])
        h = sb("h", [P, TT, D])
        y = sb("y", [P, TT, D])
        xnT = sb("xnT", [P, KT, SEQ])
        acc = sb("acc", [P, TT, D])
        gate = sb("gate", [P, 4, D])
        part = sb("part", [P, 2, 512])
        cst = sb("cst", [P, C_ALL])
        rows = sb("rows", [120, P])
        gains = sb("gains", [43, P])
        cols = sb("cols", [P, 120])
        gcol = sb("gcol", [P, 43])
        cpad = sb("cpad", [P, KT, 32])
        modc = sb("modc", [P, 112])
        scale = sb("scale", [P, 5, KT])
        wr = sb("wr", [P, KT, 32])
        br = sb("br", [P, NE])
        stat = sb("stat", [P, 32])
        msq, var, root, rstd = stat[:, 0:4], stat[:, 4:8], stat[:, 8:12], stat[:, 12:16]
        mv = stat[:, 16:20].rearrange("p (t s) -> p t s", t=2)
        bn = sb("bn", [P, 2, 6])
        score = sb("score", [P, TT, NE])
        biased = sb("biased", [P, TT, NE])
        cmp1 = sb("cmp1", [P, TT * NG * EG * EG])
        cmp2 = sb("cmp2", [P, TT * NG * EG * EG])
        chosen = sb("chosen", [P, TT, NE])
        rank = sb("rank", [P, TT * NE])
        gsum = sb("gsum", [P, TT * NG])
        grank = sb("grank", [P, TT * NG])
        den = sb("den", [P, TT])
        combine = sb("combine", [P, TT, NE])
        place = sb("place", [P, TT, NE])
        most = sb("most", [P, 2, PAIRS])
        bounds = [sb(f"bounds{l}", [P, 16], I32) for l in range(2)]
        boundf = sb("boundf", [1, 16])
        zeros = sb("zeros", [1, 16])
        slot_id = sb("slot_id", [P, SLOTS])

        arena = sb("arena", [P, ARENA])
        at = [0]

        def take(n):
            at[0] += n
            assert at[0] <= ARENA, at[0]
            return arena[:, at[0] - n:at[0]]

        trig = take(1024).rearrange("p (w f s) -> p w f s", w=2, f=2)
        kept = at[0]
        spare = ARENA - 6144
        down0 = arena[:, spare:spare + 4096].rearrange("p (k n) -> p k n", k=4)
        down1 = [arena[:, spare + 4096:spare + 6144].rearrange("p (k n) -> p k n", k=2), acc[:]]
        gate0 = arena[:, spare:spare + 4096].rearrange("p (k n) -> p k n", k=KT)
        gate1 = [arena[:, spare + 4096:spare + 6144].rearrange("p (k n) -> p k n", k=4),
                 acc[:].rearrange("p t d -> p (t d)").rearrange("p (k n) -> p k n", k=4)]
        yT_late = take(2048).rearrange("p (k s) -> p k s", s=SEQ)
        inner = take(384)
        prod = take(1024).rearrange("p (f s) -> p f s", f=2)
        at[0] = spare
        qT = take(2048).rearrange("p (k s) -> p k s", s=SEQ)
        kT = take(2048).rearrange("p (k s) -> p k s", s=SEQ)
        vh = take(2048).rearrange("p (b t n) -> p b t n", b=2, t=TT)
        modrow = prod[0:64, 0, :]
        on, sg = acc[:, :, 0:512], acc[:, :, 512:1024]
        yTs = [y[:].rearrange("p t d -> p (t d)").rearrange("p (k s) -> p k s", s=SEQ),
               yT_late]

        def yT(k):
            return yTs[k // 8][:, k % 8, :]

        ang, turns, rem, crem = (qT[:, 2 * i:2 * i + 2, :] for i in range(4))
        posi = kT[:, 0, :].bitcast(I32)
        posf = kT[:, 1, :]
        at[0] = kept
        xgT = take(1024).rearrange("p (k s) -> p k s", s=P)
        sil = take(DE)
        hid = take(DE)
        hidT = take(DE).rearrange("p (k s) -> p k s", s=P)
        yg = take(D)
        parts = sil[:, 0:SEQ]
        pick = take(256).rearrange("p (t s) -> p t s", t=TT)
        pickw = take(256).rearrange("p (t s) -> p t s", t=TT)
        pickwT = take(256).rearrange("p (t s) -> p t s", t=TT)
        assert at[0] <= spare
        at[0] = kept
        hnT = take(2048).rearrange("p (k s) -> p k s", s=SEQ)
        oT = hnT
        small = take(14)
        smax = small[:, 0:6].rearrange("p (b n) -> p b n", b=3)
        ssum = small[:, 6:10].rearrange("p (b n) -> p b n", b=2)
        srec = small[:, 10:14].rearrange("p (b n) -> p b n", b=2)
        knT = take(2048).rearrange("p (k s) -> p k s", s=SEQ)
        vm = take(2048).rearrange("p (t n) -> p t n", t=TT)
        qnT = take(2048).rearrange("p (k s) -> p k s", s=SEQ)
        ckT = take(256)
        qaT = take(512).rearrange("p (k s) -> p k s", s=SEQ)
        krT = xnT[:].rearrange("p k s -> p (k s)").rearrange("p (g f s) -> p g f s", g=4, f=2)
        qrT = take(1024).rearrange("p (f g s) -> p f g s", f=2, g=2)
        mprod = acc[:].rearrange("p t d -> p (t d)").rearrange("p (i s) -> p i s", i=4)
        cn = take(256).rearrange("p (t n) -> p t n", t=TT)
        qn = xnT[:, 0:2, :]
        prob, probT = y[:, :, 0:384], y[:, :, 384:768]

        bank = [ctx.enter_context(nc.psum_tensor(f"bank{i}", [P, 512], F32)) for i in range(8)]

        mla_bank = bank[4:] + bank[:4]
        att_bank = [mla_bank[7], mla_bank[0], mla_bank[5]]

        ident = cst[:, C_IDENT:C_IDENT + P]
        tri = cst[:, C_TRI:C_TRI + P]
        ones = cst[:, C_ONES:C_ONES + P]
        slots0 = cst[:, C_SLOT:C_SLOT + SLOTS]

        def tok(tt):
            return slice(tt * P, (tt + 1) * P)

        def slot(i):
            return ring[:, i % RING, :]

        kr_w = slot(MLA_AT)[:, 2048:4096].rearrange("p (f k n) -> p f k n", f=2, k=KT)
        qr_w = slot(MLA_AT + 3)[:, 3072:4096].rearrange("p (f k n) -> p f k n", f=2, k=2)

        landed = [[sem(f"landed{f}_{i}") for i in range(RING)] for f in range(2)]
        spare_in = [sem(f"spare_in{i}") for i in range(2)]
        wo_used = sem("wo_used")
        gains_in, gains_turned, gcol_copied = (sem(n) for n in ("gains_in", "gains_turned", "gcol_copied"))
        small_in, x_in, pos_in, cst_in, decay_in, gb_in, fn_in, router_in = (
            sem(n) for n in ("small_in", "x_in", "pos_in", "cst_in", "decay_in", "gb_in", "fn_in", "router_in"))
        rows_turned, cols_copied, c_silu = (sem(n) for n in ("rows_turned", "cols_copied", "c_silu"))
        angles_ready, trig_ready = sem("angles_ready"), sem("trig_ready")
        dstep = sem("dstep")
        squares, meansq, roots, y_ready = (sem(n) for n in ("squares", "meansq", "roots", "y_ready"))
        y_turned, xn_dve, xn_act = sem("y_turned"), sem("xn_dve"), sem("xn_act")
        scales_ready, rows_copied, vecs_turned, vecs_ready = (
            sem(n) for n in ("scales_ready", "rows_copied", "vecs_turned", "vecs_ready"))
        mod_step, mod_sum, mod_folded, mod_stored = (
            sem(n) for n in ("mod_step", "mod_sum", "mod_folded", "mod_stored"))
        win_done, rope_mult, rope_done, v_copied, g_silu = (
            sem(n) for n in ("win_done", "rope_mult", "rope_done", "v_copied", "g_silu"))
        ret_scores, inner_ready, o_done, o_var, o_root, o_norm, yh_ready, yh_turned, yT_copied = (
            sem(n) for n in ("ret_scores", "inner_ready", "o_done", "o_var", "o_root", "o_norm",
                             "yh_ready", "yh_turned", "yT_copied"))
        mix_done, h_prod, h_ready = sem("mix_done"), sem("h_prod"), sem("h_ready")
        logits, sig_ready, chosen_ready, ranked, bounds_ready = (
            sem(n) for n in ("logits", "sig_ready", "chosen_ready", "ranked", "bounds_ready"))
        stored = sem("stored")
        cpad_cleared, mod_parts = sem("cpad_cleared"), sem("mod_parts")
        wr_cleared, logit_parts, parts_copied = sem("wr_cleared"), sem("logit_parts"), sem("parts_copied")
        rope_w = sem("rope_w")
        ck_raw, kr_raw, qa_raw, lat_sq, lat_ms, lat_root, lat_norm, lat_turned, ckT_ready, qaT_ready = (
            sem(n) for n in ("ck_raw", "kr_raw", "qa_raw", "lat_sq", "lat_ms", "lat_root", "lat_norm",
                             "lat_turned", "ckT_ready", "qaT_ready"))
        kv_done, kv_act, kv_dve, qb_done, qb_act, qb_dve, kr_mult, kr_ready, qr_mult, qr_ready = (
            sem(n) for n in ("kv_done", "kv_act", "kv_dve", "qb_done", "qb_act", "qb_dve", "kr_mult",
                             "kr_ready", "qr_mult", "qr_ready"))
        att_masked, att_top = sem("att_masked"), sem("att_top")
        att_score, att_max, att_exp, att_prob, prob_turned, probT_ready, att_o, oT_ready = (
            sem(n) for n in ("att_score", "att_max", "att_exp", "att_prob", "prob_turned",
                             "probT_ready", "att_o", "oT_ready"))
        MOE = ["slots_ready", "picked", "weights_turned", "gathered", "xg_dve", "xg_act", "pickwT_ready", "gate_half", "gate_done", "up_done",
               "sil_ready", "hid_ready", "hid_turned", "hidT_act", "hidT_dve", "down_done", "yg_ready",
               "comb_done", "h_added"]
        moe = [{n: sem(f"{n}{l}") for n in MOE} for l in range(2)]

        class Count:

            def __init__(self, s):
                self.s, self.n = s, 0

            def step(self, eng, ins):
                self.n += 1
                ins.then_inc(self.s, 1)
                eng.wait_ge(self.s, self.n)

        block = ctx.enter_context(nc.Block())

        @block.sync
        def _(sp):
            def source(kind, n):
                if kind == "mod":
                    m, b = MOD[n]
                    w = t["w_mod_kv"] if m == 2 else t["w_mod"][m]
                    return w[:, b * 512:(b + 1) * 512].rearrange("(k p) n -> p k n", p=P)
                if kind == "win":
                    b = WIN[n]
                    return t["ret_w_in"][0, :, b * 512:(b + 1) * 512].rearrange("(k p) n -> p k n", p=P)
                if kind == "wout":
                    return t["ret_w_out"][0, n * 512:(n + 1) * 512, :].rearrange("(k p) n -> p k n", p=P)
                if kind == "kva":
                    return t["mla_w_kv_a"].rearrange("(k p) n -> p k n", p=P)
                if kind == "qa":
                    return t["mla_w_q_a"][0].rearrange("(k p) n -> p k n", p=P)
                if kind == "kvb":
                    return t["mla_w_kv_b"].rearrange("(k p) n -> p k n", p=P)
                if kind == "qb":
                    return t["mla_w_q_b"][0].rearrange("(k p) n -> p k n", p=P)
                n = int(kind[2])
                return t["mla_w_o"][0, n * 512:(n + 1) * 512, :].rearrange("(k p) n -> p k n", p=P)

            def load(i, src, halves=(0, 1)):
                k, n = src.shape[1], src.shape[2]
                dst = slot(i)[:, 0:k * n].rearrange("p (k n) -> p k n", k=k)
                for f in halves:
                    ks, ns = slice(0, k), slice(f * n // 2, (f + 1) * n // 2)
                    if k > 1:
                        ks, ns = slice(f * k // 2, (f + 1) * k // 2), slice(0, n)
                    sp.dma_start(dst[:, ks, ns], src[:, ks, ns]).then_inc(landed[f][i % RING], 16)

            def matrix(l, pair, j):
                w = t[("moe_w_gate", "moe_w_up", "moe_w_down")[j // 2]][l]
                return w[bass.ds(pair * 2 + j % 2, 1)].rearrange("e (k p) n -> p (e k) n", p=P)

            def released(i):
                kind, n = STREAM[i] if i < N_RET else (MLA_ITEMS[i - MLA_AT], 0)
                s, v = {"mod": (mod_sum, n + 1), "win": (win_done, 2 * n + 2), "wout": (wo_used, n + 1),
                        "kva": (kr_raw, 1), "qa": (qa_raw, 1), "kvb": (kv_done, 8), "qb": (qb_done, 6),
                        "wo0": (wo_used, 4), "wo1": (mix_done, 8)}[kind]
                if (kind, n) == ("wout", 3):
                    s, v = mix_done, 4
                sp.wait_ge(s, v)

            sp.dma_start(rows[0:8, :], t["c"].rearrange("b (r c) -> (b r) c", c=P)).then_inc(small_in, 16)
            sp.dma_start(rows[8:104, :], t["b_mod"].rearrange("l (r c) -> (l r) c", c=P)).then_inc(small_in, 16)
            for i, (kind, n) in enumerate(STREAM):
                if i >= RING:
                    released(i - RING)
                load(i, source(kind, n))
                if i == 1:
                    sp.dma_start(h[:], t["x"].rearrange("b (t p) d -> p (b t) d", p=P)).then_inc(x_in, 16)
            for l in range(2):
                S = moe[l]
                base = MOE_AT[l]
                for j in range(4):
                    released(base - RING + j)
                    load(base + j, matrix(l, 0, j))
                if l == 0:
                    sp.wait_ge(o_done, 2 * RH)
                else:
                    sp.wait_ge(att_o, MH)
                sp.dma_start(down0, matrix(l, 0, 4)).then_inc(spare_in[0], 16)
                last = matrix(l, 0, 5)
                sp.dma_start(down1[0], last[:, 0:2, :]).then_inc(spare_in[1], 16)
                for j in range(2):
                    released(base - 2 + j)
                    load(base + 4 + j, matrix(l, 1, j))
                sp.wait_ge(h_ready, 4 * l + 4)
                sp.dma_start(down1[1], last[:, 2:4, :]).then_inc(spare_in[1], 16)
                sp.wait_ge(bounds_ready, l + 1)

                def reload(i, pair, begun):
                    for f in range(2):
                        sp.wait_ge((S["gate_half"], S["gate_done"])[f], begun)
                        for j in range(2):
                            load(i + j, matrix(l, pair, j), (f,))
                    for j in range(2, 4):
                        freed(j, begun)
                        load(i + j, matrix(l, pair, j))
                    freed(4, begun)
                    for f in range(2):
                        for j in range(4, 6):
                            load(i + j, matrix(l, pair, j), (f,))

                def freed(j, begun):
                    if j == 0:
                        sp.wait_ge(S["gate_done"], begun)
                    if j == 2:
                        sp.wait_ge(S["up_done"], begun * 2)
                    if j == 4:
                        sp.wait_ge(S["down_done"], begun * 2)

                begun = sp.value_load(bounds[l][0:1, 1:2], min_val=1, max_val=ROUNDS * PAIRS)
                for f in range(2):
                    sp.wait_ge((S["gate_half"], S["gate_done"])[f], begun)
                    for j in (2, 3):
                        load(base + 4 + j, matrix(l, 1, j), (f,))
                sp.wait_ge(S["up_done"], begun * 2)
                for f in range(2):
                    for j in (4, 5):
                        load(base + 4 + j, matrix(l, 1, j), (f,))
                sp.wait_ge(S["down_done"], begun * 2)
                sp.dma_start(gate0, matrix(l, 2, 0)).then_inc(spare_in[0], 16)
                for f in range(2):
                    sp.dma_start(gate1[f], matrix(l, 2, 1)[:, 4 * f:4 * f + 4, :]).then_inc(spare_in[1], 16)
                begun = sp.value_load(bounds[l][0:1, 2:3], min_val=1, max_val=ROUNDS * PAIRS)
                for f in range(2):
                    sp.wait_ge((S["gate_half"], S["gate_done"])[f], begun)
                    for j in (2, 3):
                        load(base + 8 + j, matrix(l, 2, j), (f,))
                sp.wait_ge(S["up_done"], begun * 2)
                for f in range(2):
                    for j in (4, 5):
                        load(base + 8 + j, matrix(l, 2, j), (f,))
                sp.wait_ge(S["down_done"], begun * 2)
                for f in range(2):
                    for j in range(2):
                        load(base + 14 + j, matrix(l, 3, j), (f,))
                begun = sp.value_load(bounds[l][0:1, 3:4], min_val=1, max_val=ROUNDS * PAIRS)
                for j in range(2, 4):
                    freed(j, begun)
                    load(base + 14 + j, matrix(l, 3, j))
                freed(4, begun)
                for f in range(2):
                    for j in range(4, 6):
                        load(base + 14 + j, matrix(l, 3, j), (f,))
                with sp.Fori(4, PAIRS) as pair:
                    begun = sp.value_load(bounds[l][0:1, bass.ds(pair, 1)], min_val=1, max_val=ROUNDS * PAIRS)
                    reload(base + 14, pair, begun)
                if l == 0:
                    total = sp.value_load(bounds[l][0:1, PAIRS:PAIRS + 1], min_val=PAIRS, max_val=ROUNDS * PAIRS)
                    for j, kind in enumerate(MLA_ITEMS):
                        freed(j, total)
                        load(MLA_AT + j, source(kind, 0))
            for tt in range(TT):
                sp.wait_ge(h_ready, 8 + tt + 1)
                sp.dma_start(out[0, tok(tt), :], acc[:, tt, :]).then_inc(stored, 16)
            sp.wait_ge(stored, 16 * TT)

        @block.tensor
        def _(pe):
            def arrived(i, extra=None, halves=(0, 1)):
                v = 16 * (i // RING + 1)
                for f in halves:
                    pe.wait_ge(landed[f][i % RING], v if extra is None else extra * 16 + v)

            def keep_warm(n, b):
                for _ in range(n):
                    pe.matmul(bank[b][:], ones, cst[:, 0:512], start=True, stop=True)

            def turn_y(n):
                for tt in range(TT):
                    pe.wait_ge(y_ready, 2 * n + tt + 1)
                    for b in range(4):
                        for f in range(2):
                            k = 2 * b + f
                            ins = pe.transpose(bank[4 + b][:, f * SEQ + tt * P:f * SEQ + (tt + 1) * P],
                                               y[:, tt, k * P:(k + 1) * P], ident)
                        if tt == TT - 1:
                            ins.then_inc(y_turned, 1)

            pe.wait_ge(cst_in, 16)
            pe.wait_ge(small_in, 16 * 3)
            pe.transpose(bank[4][:, 0:120], rows[:], ident[0:120, 0:120]).then_inc(rows_turned, 1)

            def mod_parts_of(m):
                i = AT[("mod", m)]
                w = slot(i).rearrange("p (k n) -> p k n", k=KT)
                arrived(i)
                if m == 0:
                    pe.wait_ge(c_silu, 1)
                elif m >= 2:
                    pe.wait_ge(mod_sum, m - 1)
                for k in range(KT):
                    g = 32 * (k % 4)
                    ins = pe.matmul(bank[m % 2][g:g + 32, :], cpad[:, k, :], w[:, k, :], start=(k < 4), stop=(k >= 4))
                ins.then_inc(mod_parts, 1)

            def mod_fold(m):
                pe.wait_ge(mod_sum, m + 1)
                if m >= 2:
                    pe.wait_ge(mod_stored, m - 1)
                for j in range(4):
                    ins = pe.matmul(bank[2 + m % 2][:, j:j + 1], part[:, m % 2, j * P:(j + 1) * P],
                                    ones[:, 0:1], start=True, stop=True)
                ins.then_inc(mod_folded, 1)

            def mod_gather(m):
                if MOD[m] in GATES:
                    pe.wait_ge(mod_sum, m + 1)
                    n = list(GATES).index(MOD[m])
                    pe.wait_ge(mod_stored, FIRST_MOD + n)
                    pe.matmul(bank[5][:], ones, part[:, m % 2, :], start=True, stop=True).then_inc(mod_folded, 1)
                elif m % 2:
                    pe.wait_ge(mod_sum, m + 1)
                    first = min(x for x in range(FIRST_MOD, len(MOD)) if MOD[x] not in GATES)
                    for x in (m - 1, m):
                        g, row = ROW_OF[MOD[x]]
                        at = C_ROW + P - 1 - row
                        pe.matmul(bank[4][32 * g:32 * g + 32, :], cst[:, at:at + 32], part[:, x % 2, :],
                                  start=(m - 1 == first), stop=(m == LAST_VEC)).then_inc(mod_folded, 1)

            mod_parts_of(0)
            mod_parts_of(1)
            mod_fold(0)
            keep_warm(1, 7)
            pe.wait_ge(cols_copied, 1)
            turn_y(0)
            mod_parts_of(2)
            mod_fold(1)
            keep_warm(2, 1)
            mod_parts_of(3)
            mod_fold(2)
            mod_fold(3)
            pe.wait_ge(gains_in, 16 * 5)
            pe.transpose(bank[0][:, 0:43], gains[:], ident[0:43, 0:43]).then_inc(gains_turned, 1)
            keep_warm(2, 1)

            def turn_head(hd, g):
                pe.wait_ge(yh_ready, 2 * hd + 2)
                if 2 * hd + g:
                    pe.wait_ge(yT_copied, 2 * hd + g)
                for j in range(2):
                    for tt in range(TT):
                        ins = pe.transpose(bank[7][:, (2 * j + tt) * P:(2 * j + tt + 1) * P],
                                           on[:, tt, (2 * g + j) * P:(2 * g + j + 1) * P], ident)
                ins.then_inc(yh_turned, 1)

            for r in range(12):
                i = AT[("win", r)]
                w = slot(i).rearrange("p (k n) -> p k n", k=KT)
                arrived(i)
                hd = (r - 4) // 2
                pair = (bank[0], bank[1]) if r % 2 == 0 else (bank[2], bank[3])
                if r == 0:
                    pe.wait_ge(gcol_copied, 1)
                    pe.wait_ge(xn_dve, 4)
                    pe.wait_ge(xn_act, 4)
                elif 2 <= r < 6:
                    pe.wait_ge(rope_mult, 2 * (r - 1))
                elif r >= 6 and r % 2 == 0:
                    pe.wait_ge(v_copied, 2 * hd)
                elif r >= 6:
                    pe.wait_ge(o_norm, 2 * hd)
                if r < 4:
                    for b in range(2):
                        for f in range(2):
                            c = (2 * b + f) * P
                            for k in range(KT):
                                ins = pe.matmul(pair[b][:, f * SEQ:(f + 1) * SEQ], w[:, k, c:c + P], xnT[:, k, :],
                                                start=(k == 0), stop=(k == KT - 1))
                        ins.then_inc(win_done, 1)
                else:
                    for tt in range(TT):
                        for k in range(KT):
                            ins = pe.matmul(pair[tt][:], xnT[:, k, tok(tt)], w[:, k, :],
                                            start=(k == 0), stop=(k == KT - 1))
                        ins.then_inc(win_done, 1)
                if r >= 4 and r % 2 == 0:
                    if hd:
                        turn_head(hd - 1, 0)
                    pe.wait_ge(rope_done, 8)
                    if hd:
                        pe.wait_ge(inner_ready, 2 * hd)
                    for f in range(2):
                        pe.matmul(bank[6][:, 0:SEQ], kT[:, 2 * hd + f, 0:P], qT[:, 2 * hd + f, :],
                                  start=(f == 0), stop=(f == 1))
                    for f in range(2):
                        ins = pe.matmul(bank[6][:, SEQ:SEQ + P], kT[:, 2 * hd + f, P:SEQ], qT[:, 2 * hd + f, P:SEQ],
                                        start=(f == 0), stop=(f == 1))
                    ins.then_inc(ret_scores, 1)
                if r == 0:
                    pe.wait_ge(xn_dve, 4)
                    pe.wait_ge(xn_act, 4)
                for m in ROUND_MODS[r]:
                    mod_gather(m)
                if r >= 4 and r % 2 == 0 and hd:
                    turn_head(hd - 1, 1)
                if r >= 4 and r % 2 == 1:
                    pe.wait_ge(g_silu, 2 * hd + 2)
                    pe.wait_ge(v_copied, 2 * hd + 2)
                    pe.wait_ge(inner_ready, 2 * hd + 2)
                    v = vh[:, hd % 2]
                    pe.matmul(bank[2][:], inner[:, 0:P], v[:, 0, :], start=True, stop=True).then_inc(o_done, 1)
                    pe.matmul(bank[3][:], inner[:, P:SEQ], v[:, 0, :], start=True, stop=False)
                    pe.matmul(bank[3][:], inner[:, SEQ:SEQ + P], v[:, 1, :], start=False, stop=True).then_inc(o_done, 1)

            def wout(i, tt):
                it = AT[("wout", i)]
                w = slot(it).rearrange("p (k n) -> p k n", k=4)
                arrived(it)
                for n in range(2):
                    for kk in range(4):
                        ins = pe.matmul(bank[2 * tt + n][:], yT(4 * i + kk)[:, tok(tt)], w[:, kk, n * 512:(n + 1) * 512],
                                        start=(i == 0 and kk == 0), stop=(i == 3 and kk == 3))
                    if i == 3:
                        ins.then_inc(mix_done, 1)
                return ins

            pe.wait_ge(yT_copied, 6)
            wout(0, 0)
            wout(1, 0)
            turn_head(3, 0)
            pe.wait_ge(o_norm, 8)
            wout(0, 1).then_inc(wo_used, 1)
            turn_head(3, 1)
            wout(1, 1).then_inc(wo_used, 1)
            mod_gather(LAST_MODS[0])
            wout(2, 0)
            mod_gather(LAST_MODS[1])
            wout(2, 1).then_inc(wo_used, 1)
            mod_gather(LAST_MODS[2])
            pe.wait_ge(yT_copied, 8)
            wout(3, 0)
            for m in LAST_MODS[3:]:
                mod_gather(m)
            pe.wait_ge(rows_copied, 1)
            for j in range(4):
                ins = pe.transpose(bank[6][:, 64 * j:64 * j + 64], modrow[:, j * P:(j + 1) * P], ident[0:64, 0:64])
            ins.then_inc(vecs_turned, 1)
            wout(3, 1)

            def experts(l):
                n = 1 + 2 * l
                S = moe[l]
                turn_y(n)
                pe.wait_ge(h_prod, 4 * l + 4)
                pe.wait_ge(router_in, 32)
                for k in range(KT):
                    if k % 2 == 0:
                        pe.wait_ge(*((xn_dve, xn_act)[k // 2 % 2], 4 + 12 * l + 2 * (k // 4) + 2))
                    g = 32 * (k % 4)
                    ins = pe.matmul(bank[0][g:g + 32, 0:SEQ], wr[:, k, :], xnT[:, k, :], start=(k < 4), stop=(k >= 4))
                ins.then_inc(logit_parts, 1)
                pe.wait_ge(parts_copied, l + 1)
                for tt in range(TT):
                    ins = pe.matmul(bank[1][:, tt * NE:(tt + 1) * NE], parts[:, tok(tt)],
                                    cst[:, C_SUM4:C_SUM4 + NE], start=True, stop=True)
                ins.then_inc(logits, 1)
                keep_warm(4, 7)
                pe.wait_ge(chosen_ready, l + 1)
                pe.matmul(bank[2][:, 0:NE], tri, chosen[:, 0, :], start=True, stop=True)
                pe.matmul(bank[2][:, NE:2 * NE], ones, chosen[:, 0, :], start=True, stop=False)
                pe.matmul(bank[2][:, NE:2 * NE], tri, chosen[:, 1, :], start=False, stop=True)
                pe.matmul(bank[2][:, 2 * NE:3 * NE], ones, chosen[:, 0, :], start=True, stop=False)
                pe.matmul(bank[2][:, 2 * NE:3 * NE], ones, chosen[:, 1, :], start=False, stop=True).then_inc(ranked, 1)
                keep_warm(5, 7)
                pe.wait_ge(bounds_ready, l + 1)

                def rounds(begin, end, here, w):
                    with pe.Fori(begin, end) as u:
                        pe.wait_ge(S["picked"], u * 2 + 1)
                        for k in range(KT):
                            for tt in range(TT):
                                ins = pe.matmul(bank[4 + k // 4][:, (k % 4) * P:(k % 4 + 1) * P],
                                                y[:, tt, k * P:(k + 1) * P], pick[:, tt, :],
                                                start=(tt == 0), stop=(tt == TT - 1))
                            if k % 4 == 3:
                                ins.then_inc(S["gathered"], 1)
                        pe.wait_ge(S["picked"], u * 2 + 2)
                        for tt in range(TT):
                            ins = pe.transpose(bank[6][:, tok(tt)], pickw[:, tt, :], ident)
                        ins.then_inc(S["weights_turned"], 1)
                        here(0, 0)
                        here(1, 0)
                        pe.wait_ge(S["h_added"], u * 4 + 4)
                        pe.wait_ge(S["xg_dve"], u + 1)
                        for k in range(KT):
                            if k == KT // 2:
                                here(0, 1)
                                here(1, 1)
                                pe.wait_ge(S["xg_act"], u + 1)
                            for e in range(2):
                                ins = pe.matmul(bank[0][e * 64:(e + 1) * 64, :], xgT[:, k, e * 64:(e + 1) * 64],
                                                w(e, k), start=(k == 0), stop=(k == KT - 1))
                            if k == KT // 2 - 1:
                                ins.then_inc(S["gate_half"], 1)
                        ins.then_inc(S["gate_done"], 1)
                        for f in range(2):
                            here(2, f)
                            here(3, f)

                        def up(f, ks):
                            for k in ks:
                                for e in range(2):
                                    ins = pe.matmul(bank[1 + f][e * 64:(e + 1) * 64, 0:256],
                                                    xgT[:, k, e * 64:(e + 1) * 64],
                                                    w(2 + e, k)[:, f * 256:(f + 1) * 256],
                                                    start=(k == 0), stop=(k == KT - 1))
                            return ins

                        def turn_hidden(f):
                            pe.wait_ge(S["hid_ready"], u * 2 + f + 1)
                            for j in range(2):
                                ins = pe.transpose(bank[3 + f][:, j * P:(j + 1) * P],
                                                   hid[:, (2 * f + j) * P:(2 * f + j + 1) * P], ident)
                            ins.then_inc(S["hid_turned"], 1)

                        def down(n2, f):
                            for k in (2 * f, 2 * f + 1):
                                for e in range(2):
                                    ins = pe.matmul(bank[6 + n2][e * 64:(e + 1) * 64, :],
                                                    hidT[:, k, e * 64:(e + 1) * 64],
                                                    w(4 + e, k)[:, n2 * 512:(n2 + 1) * 512],
                                                    start=(k == 0), stop=(k == 3))
                            return ins

                        up(0, range(KT)).then_inc(S["up_done"], 1)
                        up(1, range(KT // 2))
                        turn_hidden(0)
                        up(1, range(KT // 2, KT)).then_inc(S["up_done"], 1)
                        here(4, 0)
                        here(5, 0)
                        pe.wait_ge(S["pickwT_ready"], u + 1)
                        pe.wait_ge(S["hidT_act"], u + 1)
                        down(0, 0)
                        turn_hidden(1)
                        down(1, 0)
                        here(4, 1)
                        here(5, 1)
                        pe.wait_ge(S["hidT_dve"], u + 1)
                        for n2 in range(2):
                            down(n2, 1).then_inc(S["down_done"], 1)
                        for n2 in range(2):
                            pe.wait_ge(S["yg_ready"], u * 2 + n2 + 1)
                            for tt in range(TT):
                                pe.matmul(bank[(2, 3, 0, 1)[2 * n2 + tt]][:], pickwT[:, tt, :],
                                          yg[:, n2 * 512:(n2 + 1) * 512], start=True, stop=True).then_inc(S["comb_done"], 1)

                base = MOE_AT[l]

                def outside(i, use):
                    pe.wait_ge(spare_in[i], 16 * (i + 1) * (2 * l + use))

                def here0(j, f):
                    if j < 4:
                        arrived(base + j, halves=(f,))
                    elif f == 0:
                        outside(j - 4, 1)

                def w0(j, k):
                    if j < 4:
                        return in_ring(base + j, j, k)
                    return down0[:, k, :] if j == 4 else down1[k // 2][:, k % 2, :]

                def here2(j, f):
                    if j >= 2:
                        arrived(base + 8 + j, halves=(f,))
                    elif f == 0:
                        outside(j, 2)

                def w2(j, k):
                    if j >= 2:
                        return in_ring(base + 8 + j, j, k)
                    return gate0[:, k, :] if j == 0 else gate1[k // 4][:, k % 4, :]

                def in_ring(i, j, k):
                    return slot(i).rearrange("p (k n) -> p k n", k=(KT if j < 4 else 4))[:, k, :]

                def bound(at, least):
                    return pe.value_load(bounds[l][0:1, at], min_val=least, max_val=ROUNDS * PAIRS)

                rounds(0, bound(slice(1, 2), 1), here0, w0)
                rounds(bound(slice(1, 2), 1), bound(slice(2, 3), 1),
                       lambda j, f: arrived(base + 4 + j, halves=(f,)), lambda j, k: in_ring(base + 4 + j, j, k))
                rounds(bound(slice(2, 3), 1), bound(slice(3, 4), 1), here2, w2)
                with pe.Fori(3, PAIRS) as pair:
                    begin = bound(bass.ds(pair, 1), 1)
                    end = bound(bass.ds(pair + 1, 1), 1)
                    rounds(begin, end, lambda j, f: arrived(base - 4 + j, pair, (f,)),
                           lambda j, k: in_ring(base - 4 + j, j, k))

            experts(0)

            keep_warm(3, 7)
            turn_y(2)

            def item(name, k):
                i = AT[(name, 0)]
                arrived(i)
                return slot(i)

            kva = item("kva", 0)[:, 0:KT * 192].rearrange("p (k n) -> p k n", k=KT)
            pe.wait_ge(xn_dve, 12)
            pe.wait_ge(xn_act, 12)
            for tt in range(TT):
                for k in range(KT):
                    ins = pe.matmul(mla_bank[4][:, tt * KVL:(tt + 1) * KVL], hnT[:, k, tok(tt)], kva[:, k, 0:KVL],
                                    start=(k == 0), stop=(k == KT - 1))
            ins.then_inc(ck_raw, 1)
            for f in range(2):
                pe.wait_ge(rope_w, f + 1)
                for k in range(KT):
                    ins = pe.matmul(mla_bank[5][:, f * SEQ:(f + 1) * SEQ], kr_w[:, f, k, :], hnT[:, k, :],
                                    start=(k == 0), stop=(k == KT - 1))
            ins.then_inc(kr_raw, 1)
            qa = item("qa", 0)[:, 0:KT * QL].rearrange("p (k n) -> p k n", k=KT)
            pe.wait_ge(xn_dve, 16)
            pe.wait_ge(xn_act, 16)
            for tt in range(TT):
                for k in range(KT):
                    ins = pe.matmul(mla_bank[6][:, tt * QL:(tt + 1) * QL], xnT[:, k, tok(tt)], qa[:, k, :],
                                    start=(k == 0), stop=(k == KT - 1))
            ins.then_inc(qa_raw, 1)
            pe.wait_ge(lat_norm, 2)
            for tt in range(TT):
                ins = pe.transpose(mla_bank[7][:, tok(tt)], cn[:, tt, :], ident)
            ins.then_inc(lat_turned, 1)
            pe.wait_ge(lat_norm, 4)
            for j in range(2):
                for tt in range(TT):
                    ins = pe.transpose(mla_bank[0][:, (2 * j + tt) * P:(2 * j + tt + 1) * P], qn[:, tt, j * P:(j + 1) * P], ident)
            ins.then_inc(lat_turned, 1)
            kvb = item("kvb", 0)[:, 0:2048].rearrange("p (h n) -> p h n", h=MH)
            pe.wait_ge(ckT_ready, 1)
            for b in range(4):
                for j in range(2):
                    ins = pe.matmul(mla_bank[1 + b][:, j * SEQ:(j + 1) * SEQ], kvb[:, 2 * b + j, 0:NOPE], ckT, start=True, stop=True)
                ins.then_inc(kv_done, 1)
            pe.wait_ge(kr_mult, 2)
            pe.wait_ge(qaT_ready, 2)
            for tt in range(TT):
                for n in range(2):
                    b = (5, 6, 7, 0)[2 * tt + n]
                    ins = pe.matmul(mla_bank[b][:], ckT[:, tok(tt)], kvb[:, 4 * n:4 * n + 4, NOPE:NOPE + VH], start=True, stop=True)
                    ins.then_inc(kv_done, 1)
            qb = item("qb", 0)[:, 0:2 * 1536].rearrange("p (k h n) -> p k h n", k=2, h=MH)
            pe.wait_ge(kv_act, 4)
            pe.wait_ge(kv_dve, 4)
            for f in range(2):
                pe.wait_ge(rope_w, 3 + f)
                for g in range(2):
                    for k in range(2):
                        ins = pe.matmul(mla_bank[5 + f][:, g * SEQ:(g + 1) * SEQ],
                                        qr_w[:, f, k, g * P:(g + 1) * P],
                                        qaT[:, k, :], start=(k == 0), stop=(k == 1))
                ins.then_inc(qb_done, 1)

            for b in range(4):
                if b % 2 == 0:
                    pe.wait_ge(kv_act, b // 2 + 1)
                else:
                    pe.wait_ge(kv_dve, b // 2 + 1)
                for j in range(2):
                    for k in range(2):
                        ins = pe.matmul(mla_bank[1 + b][:, j * SEQ:(j + 1) * SEQ], qb[:, k, 2 * b + j, 0:NOPE], qaT[:, k, :],
                                        start=(k == 0), stop=(k == 1))
                ins.then_inc(qb_done, 1)

            def scores(hd):
                b = att_bank[hd % 3]
                if hd >= 3:
                    pe.wait_ge(att_exp, 2 * (hd - 2))
                for tt in range(TT):
                    o = b[:, 0:P] if tt == 0 else b[:, P:P + SEQ]
                    keys = slice(0, P * (tt + 1))
                    pe.matmul(o, qnT[:, hd, tok(tt)], knT[:, hd, keys], start=True, stop=False)
                    for f in range(2):
                        ins = pe.matmul(o, qrT[:, f, hd // 4, tok(tt)], krT[:, hd % 4, f, keys],
                                        start=False, stop=(f == 1))
                ins.then_inc(att_score, 1)

            def turn_probs(hd):
                b = mla_bank[1 + hd % 2]
                pe.wait_ge(att_prob, 2 * (hd + 1))
                if hd >= 2:
                    pe.wait_ge(probT_ready, hd - 1)
                for j in range(3):
                    ins = pe.transpose(b[:, tok(j)], prob[:, hd % 2, tok(j)], ident)
                ins.then_inc(prob_turned, 1)

            def attend(hd):
                b = mla_bank[3 + hd % 2]
                pe.wait_ge(probT_ready, hd + 1)
                if hd >= 2:
                    pe.wait_ge(oT_ready, hd - 1)
                v = vm[:, :, hd * VH:(hd + 1) * VH]
                pe.matmul(b[:, 0:P], v[:, 0, :], probT[:, hd % 2, 0:P], start=True, stop=True)
                pe.matmul(b[:, P:SEQ], v[:, 0, :], probT[:, hd % 2, P:SEQ], start=True, stop=False)
                pe.matmul(b[:, P:SEQ], v[:, 1, :], probT[:, hd % 2, SEQ:SEQ + P], start=False, stop=True).then_inc(att_o, 1)

            pe.wait_ge(qb_act, 2)
            pe.wait_ge(qb_dve, 2)
            pe.wait_ge(qr_ready, 2)
            pe.wait_ge(kr_ready, 5)
            scores(0)
            scores(1)
            for hd in range(MH):
                if hd + 2 < MH:
                    scores(hd + 2)
                turn_probs(hd)
                if hd:
                    attend(hd - 1)
            attend(MH - 1)
            pe.wait_ge(att_exp, 2 * MH)
            pe.wait_ge(oT_ready, MH)
            for i in range(2):
                w = item(f"wo{i}", 0).rearrange("p (k n) -> p k n", k=4)
                for tt in range(TT):
                    for n in range(2):
                        for kk in range(4):
                            ins = pe.matmul(mla_bank[(5, 6, 7, 0)[2 * tt + n]][:], oT[:, 4 * i + kk, tok(tt)],
                                            w[:, kk, n * 512:(n + 1) * 512],
                                            start=(i == 0 and kk == 0), stop=(i == 1 and kk == 3))
                        if i == 1:
                            ins.then_inc(mix_done, 1)
                        elif tt == 1 and n == 1:
                            ins.then_inc(wo_used, 1)
            experts(1)

        @block.scalar
        def _(act):
            A = act.activation
            act.dma_start(cst[:, 0:C_DECAY], t["constants"][:, 0:C_DECAY]).then_inc(cst_in, 16)
            act.dma_start(rows[104:120, :], t["norm_mix"].rearrange("l (r c) -> (l r) c", c=P)).then_inc(small_in, 16)
            act.dma_start(posi, t["positions"].to_broadcast([P, SEQ])).then_inc(pos_in, 16)
            act.dma_start(gains[0:16, :], t["b_mod_kv"].rearrange("(r c) -> r c", c=P)).then_inc(gains_in, 16)
            act.dma_start(gains[16:32, :], t["norm_ffn"].rearrange("l (r c) -> (l r) c", c=P)).then_inc(gains_in, 16)
            act.dma_start(gains[32:40, :], t["norm_kv"].rearrange("(r c) -> r c", c=P)).then_inc(gains_in, 16)
            act.dma_start(gains[40:41, :], t["mla_kv_norm"].rearrange("(r c) -> r c", c=P)).then_inc(gains_in, 16)
            act.dma_start(gains[41:43, :], t["mla_q_norm"].rearrange("l (r c) -> (l r) c", c=P)).then_inc(gains_in, 16)

            def late_loads():
                act.dma_start(cst[:, C_DECAY:C_ALL], t["constants"][:, C_DECAY:C_ALL]).then_inc(decay_in, 16)
                act.wait_ge(wr_cleared, 1)
                act.dma_start(wr[:, :, 0:NE], t["router_w"].rearrange("(k p) n -> p k n", p=P)).then_inc(router_in, 16)
                act.dma_start(br[:], t["router_b"].unsqueeze(0).to_broadcast([P, NE])).then_inc(router_in, 16)
                for i, (l, g) in enumerate(((0, 2), (0, 5), (1, 2), (1, 5))):
                    act.dma_start(gate[:, i, :], t["b_mod"][l:l + 1, g * D:(g + 1) * D].to_broadcast([P, D])).then_inc(gb_in, 16)

            def squares_of(n):
                if n == 2 or n == 4:
                    l = n // 2 - 1
                    total = act.value_load(bounds[l][0:1, PAIRS:PAIRS + 1], min_val=PAIRS, max_val=ROUNDS * PAIRS)
                for tt in range(TT):
                    if n == 0:
                        act.wait_ge(x_in, 16)
                    elif n % 2:
                        act.wait_ge(h_ready, 2 * (n - 1) + 2 * (tt + 1))
                    else:
                        act.wait_ge(moe[l]["h_added"], total * 4 + 3 + tt)
                    A(y[:, tt, :], h[:, tt, :], ACT.Square, accum_out=msq[:, tt:tt + 1]).then_inc(squares, 1)
                    act.wait_ge(meansq, 2 * n + tt + 1)
                    A(root[:, tt:tt + 1], var[:, tt:tt + 1], ACT.Sqrt).then_inc(roots, 1)

            def modulate(n, dst, which, shift):
                for b in (1, 3):
                    act.wait_ge(y_turned, 4 * n + b + 1)
                    for f in range(2):
                        k = 2 * b + f
                        A(dst[:, k, :], bank[4 + b][:, f * SEQ:(f + 1) * SEQ], ACT.Identity,
                          bias=modc[:, shift + k:shift + k + 1],
                          scale=scale[:, which, k:k + 1]).then_inc(xn_act, 1)

            act.wait_ge(cols_copied, 1)
            act.wait_ge(cpad_cleared, 1)
            A(cpad[:, :, 0], cols[:, 0:8], ACT.Silu).then_inc(c_silu, 1)
            act.wait_ge(angles_ready, 2)
            A(trig[:, :, 1, :], rem, ACT.Sin).then_inc(trig_ready, 1)
            A(trig[:, :, 0, :], crem, ACT.Sin).then_inc(trig_ready, 1)
            squares_of(0)
            late_loads()

            def copy_head(hd, g):
                act.wait_ge(yh_turned, 2 * hd + g + 1)
                k = 4 * hd + 2 * g
                A(yTs[k // 8][:, k % 8:k % 8 + 2, :], bank[7][:].rearrange("p (k s) -> p k s", k=2),
                  ACT.Copy).then_inc(yT_copied, 1)

            act.wait_ge(scales_ready, 1)
            modulate(0, xnT, 0, MOD_COL[0])
            for r in range(12):
                hd = (r - 4) // 2
                if r >= 4 and r % 2 == 0:
                    for tt in range(TT):
                        act.wait_ge(win_done, 2 * r + tt + 1)
                        if hd >= 2:
                            act.wait_ge(o_done, 2 * (hd - 1))
                        A(vh[:, hd % 2, tt, :], bank[tt][:], ACT.Copy).then_inc(v_copied, 1)
                    if hd:
                        copy_head(hd - 1, 0)
                if r >= 4 and r % 2 == 1:
                    for tt in range(TT):
                        act.wait_ge(win_done, 2 * r + tt + 1)
                        if hd:
                            act.wait_ge(yh_ready, 2 * hd)
                        A(sg[:, tt, :], bank[2 + tt][:], ACT.Silu).then_inc(g_silu, 1)
                if r >= 4 and r % 2 == 0 and hd:
                    copy_head(hd - 1, 1)
                if r >= 4 and r % 2 == 1:
                    act.wait_ge(o_var, hd + 1)
                    A(root[:, 0:2], var[:, 0:2], ACT.Sqrt).then_inc(o_root, 1)
            copy_head(3, 0)
            copy_head(3, 1)
            act.wait_ge(mod_folded, LAST_VEC + 1)
            A(modrow, bank[4][0:64, :], ACT.Copy).then_inc(rows_copied, 1)

            def experts(l):
                n = 1 + 2 * l
                S = moe[l]
                squares_of(n)
                modulate(n, xnT, 1 + 2 * l, MOD_COL[l] + 24)
                act.wait_ge(logits, l + 1)
                A(score[:].rearrange("p t e -> p (t e)"), bank[1][:, 0:TT * NE], ACT.Sigmoid).then_inc(sig_ready, 1)
                act.wait_ge(bounds_ready, l + 1)
                with act.Fori(0, PAIRS) as pair:
                    begin = act.value_load(bounds[l][0:1, bass.ds(pair, 1)], min_val=0, max_val=ROUNDS * PAIRS)
                    end = act.value_load(bounds[l][0:1, bass.ds(pair + 1, 1)], min_val=1, max_val=ROUNDS * PAIRS)
                    with act.Fori(begin, end) as u:
                        act.wait_ge(S["gathered"], u * 2 + 2)
                        for j in range(4):
                            k = 4 + j
                            ins = A(xgT[:, k, :], bank[5][:, tok(j)], ACT.Identity,
                                    bias=modc[:, MOD_COL[l] + 24 + k:MOD_COL[l] + 25 + k],
                                    scale=scale[:, 1 + 2 * l, k:k + 1])
                        ins.then_inc(S["xg_act"], 1)
                        act.wait_ge(S["weights_turned"], u + 1)
                        A(pickwT.rearrange("p t s -> p (t s)"), bank[6][:, 0:SEQ], ACT.Copy).then_inc(S["pickwT_ready"], 1)
                        act.wait_ge(S["gate_done"], u + 1)
                        A(sil, bank[0][:], ACT.Silu).then_inc(S["sil_ready"], 1)
                        act.wait_ge(S["hid_turned"], u * 2 + 1)
                        A(hidT[:, 0:2, :], bank[3][:, 0:SEQ].rearrange("p (k s) -> p k s", k=2), ACT.Copy).then_inc(S["hidT_act"], 1)

            experts(0)
            act.dma_start(gate[:, 0, :], t["final_norm"].unsqueeze(0).to_broadcast([P, D])).then_inc(fn_in, 16)
            squares_of(2)
            modulate(2, hnT, 4, MOD_COL[2])
            modulate(2, xnT, 2, MOD_COL[1])
            for tt in range(TT):
                act.wait_ge(ck_raw, 1)
                A(cn[:, tt, :], mla_bank[4][:, tt * KVL:(tt + 1) * KVL], ACT.Square, accum_out=msq[:, tt:tt + 1]).then_inc(lat_sq, 1)
            for tt in range(TT):
                act.wait_ge(qa_raw, 1)
                A(qn[:, tt, :], mla_bank[6][:, tt * QL:(tt + 1) * QL], ACT.Square, accum_out=msq[:, 2 + tt:3 + tt]).then_inc(lat_sq, 1)
            act.wait_ge(lat_ms, 2)
            A(root[:, 0:4], var[:, 0:4], ACT.Sqrt).then_inc(lat_root, 1)
            act.wait_ge(lat_turned, 1)
            A(ckT, mla_bank[7][:, 0:SEQ], ACT.Copy, scale=gcol[:, 40:41]).then_inc(ckT_ready, 1)
            for b in (1, 3):
                act.wait_ge(kv_done, b)
                A(knT[:, 2 * (b - 1):2 * b, :], mla_bank[b][:].rearrange("p (k s) -> p k s", k=2), ACT.Copy).then_inc(kv_act, 1)
            for b in (0, 2):
                act.wait_ge(kv_done, 4 + b + 1)
                A(vm[:, b // 2, 0:512], mla_bank[5 + b][:], ACT.Copy).then_inc(kv_act, 1)
            for b in (1, 3):
                act.wait_ge(qb_done, 2 + b)
                A(qnT[:, 2 * (b - 1):2 * b, :], mla_bank[b][:].rearrange("p (k s) -> p k s", k=2), ACT.Copy).then_inc(qb_act, 1)

            def head_exp(hd):
                act.wait_ge(att_max, hd + 1)
                if hd >= 2:
                    act.wait_ge(prob_turned, hd - 1)
                b = att_bank[hd % 3]
                for tt in range(TT):
                    s = slice(0, P) if tt == 0 else slice(P, P + SEQ)
                    A(prob[:, hd % 2, s], b[:, s], ACT.Exp, bias=smax[:, hd % 3, tt:tt + 1], scale=SOFT,
                      accum_out=ssum[:, hd % 2, tt:tt + 1]).then_inc(att_exp, 1)

            def head_turned(hd):
                act.wait_ge(prob_turned, hd + 1)
                if hd >= 2:
                    act.wait_ge(att_o, hd - 1)
                A(probT[:, hd % 2, :], mla_bank[1 + hd % 2][:, 0:384], ACT.Copy).then_inc(probT_ready, 1)

            def head_out(hd):
                act.wait_ge(att_o, hd + 1)
                A(oT[:, hd, :], mla_bank[3 + hd % 2][:, 0:SEQ], ACT.Copy).then_inc(oT_ready, 1)

            head_exp(0)
            for hd in range(MH):
                if hd + 1 < MH:
                    head_exp(hd + 1)
                head_turned(hd)
                if hd:
                    head_out(hd - 1)
            head_out(MH - 1)
            experts(1)
            squares_of(4)

        @block.vector
        def _(dve):
            own = Count(dstep)

            def inverse_rms(n, tt):
                one = slice(tt, tt + 1)
                dve.wait_ge(squares, 2 * n + tt + 1)
                dve.tensor_scalar(var[:, one], msq[:, one], 1.0 / D, EPS, ALU.mult, ALU.add).then_inc(meansq, 1)
                dve.wait_ge(roots, 2 * n + tt + 1)
                own.step(dve, dve.reciprocal(rstd[:, one], root[:, one]))

            def normed(n):
                for tt in range(TT):
                    inverse_rms(n, tt)
                    dve.tensor_scalar(y[:, tt, :], h[:, tt, :], rstd[:, tt:tt + 1], None, ALU.mult).then_inc(y_ready, 1)

            def modulate(n, dst, which, shift):
                for b in (0, 2):
                    dve.wait_ge(y_turned, 4 * n + b + 1)
                    for f in range(2):
                        k = 2 * b + f
                        dve.tensor_scalar(dst[:, k, :], bank[4 + b][:, f * SEQ:(f + 1) * SEQ], scale[:, which, k:k + 1],
                                          modc[:, shift + k:shift + k + 1], ALU.mult, ALU.add).then_inc(xn_dve, 1)

            own.step(dve, dve.memset(zeros[:], 0.0))
            own.step(dve, dve.memset(boundf[:], 0.0))
            dve.wait_ge(rows_turned, 1)
            dve.tensor_copy(cols[:], bank[4][:, 0:120]).then_inc(cols_copied, 1)
            dve.wait_ge(pos_in, 16)
            own.step(dve, dve.tensor_copy(posf, posi))
            own.step(dve, dve.tensor_scalar(ang[:, 0, :], posf, cst[:, C_FREQ:C_FREQ + 1], None, ALU.mult))
            own.step(dve, dve.tensor_scalar(ang[:, 1, :], posf, cst[:, C_FREQ + 1:C_FREQ + 2], None, ALU.mult))
            nearest = 12582912.0
            own.step(dve, dve.tensor_scalar(turns, ang, float(1 / (2 * np.pi)), nearest, ALU.mult, ALU.add))
            own.step(dve, dve.tensor_scalar(turns, turns, nearest, None, ALU.subtract))
            first = 6.28125
            second = float(np.float32(round((2 * np.pi - first) * 2 ** 22) / 2 ** 22))
            third = float(2 * np.pi - first - second)
            own.step(dve, dve.scalar_tensor_tensor(rem, turns, -first, ang, ALU.mult, ALU.add))
            own.step(dve, dve.scalar_tensor_tensor(rem, turns, -second, rem, ALU.mult, ALU.add))
            own.step(dve, dve.scalar_tensor_tensor(rem, turns, -third, rem, ALU.mult, ALU.add))
            dve.tensor_scalar(rem, rem, -3.1415925, 3.1415925, ALU.max, ALU.min).then_inc(angles_ready, 1)
            dve.wait_ge(angles_ready, 1)
            own.step(dve, dve.scalar_tensor_tensor(crem, rem, -1.0, rem, ALU.mult, ALU.max))
            dve.tensor_scalar(crem, crem, -1.0, float(np.pi / 2), ALU.mult, ALU.add).then_inc(angles_ready, 1)

            steps = Count(mod_step)

            def mod_main(m):
                i = AT[("mod", m)]
                w = slot(i).rearrange("p (k n) -> p k n", k=KT)
                o = part[:, m % 2, :]
                if m < FIRST_MOD:
                    dve.wait_ge(mod_parts, m + 1)
                    if m >= 2:
                        dve.wait_ge(mod_folded, m - 1)
                    dve.tensor_copy(o, bank[m % 2][:]).then_inc(mod_sum, 1)
                    return
                for f in range(2):
                    dve.wait_ge(landed[f][i % RING], 16 * (i // RING + 1))
                if m >= 2:
                    dve.wait_ge(mod_folded, m - 1)
                steps.step(dve, dve.tensor_scalar(o, w[:, 0, :], cpad[:, 0, 0:1], None, ALU.mult))
                for k in range(1, KT):
                    ins = dve.scalar_tensor_tensor(o, w[:, k, :], cpad[:, k, 0:1], o, ALU.mult, ALU.add)
                    if k < KT - 1:
                        steps.step(dve, ins)
                ins.then_inc(mod_sum, 1)

            def mod_store(m):
                w, b = MOD[m]
                if m < FIRST_MOD:
                    dve.wait_ge(mod_folded, m + 1)
                    c = 4 * b
                    dve.tensor_tensor(modc[:, c:c + 4], bank[2 + m % 2][:, 0:4], cols[:, 8 + c:12 + c],
                                      ALU.add).then_inc(mod_stored, 1)
                elif (w, b) in GATES:
                    dve.wait_ge(mod_folded, m + 1)
                    dve.wait_ge(gb_in, 16 * 4)
                    o = gate[:, GATES[(w, b)], (b % 2) * 512:(b % 2) * 512 + 512]
                    dve.tensor_tensor(o, bank[5][:], o, ALU.add).then_inc(mod_stored, 1)

            scale_steps = Count(scales_ready)

            def scales(which, scol, gain):
                scale_steps.step(dve, dve.scalar_tensor_tensor(scale[:, which, :], modc[:, scol:scol + 8], 1.0,
                                                               gain, ALU.add, ALU.mult))

            dve.wait_ge(c_silu, 1)
            for m in range(FIRST_MOD):
                mod_main(m)
                if m == 1:
                    normed(0)
                if m:
                    mod_store(m - 1)
            mod_store(FIRST_MOD - 1)
            dve.wait_ge(mod_stored, FIRST_MOD)
            scales(0, MOD_COL[0] + 8, cols[:, 104:112])
            dve.wait_ge(gains_turned, 1)
            dve.tensor_copy(gcol[:], bank[0][:, 0:43]).then_inc(gcol_copied, 1)
            modulate(0, xnT, 0, MOD_COL[0])

            for r in range(12):
                hd = (r - 4) // 2
                for m in ROUND_MODS[r]:
                    mod_main(m)
                if r < 4:
                    for b in range(2):
                        n = 2 * r + b
                        dve.wait_ge(win_done, n + 1)
                        dve.wait_ge(trig_ready, 2)
                        if n:
                            dve.wait_ge(rope_done, n)
                        src = bank[2 * (r % 2) + b][:].rearrange("p (f s) -> p f s", f=2)
                        for i in range(2):
                            w = trig[:, 0, i:i + 1, :].to_broadcast([P, 2, SEQ])
                            ins = dve.tensor_tensor(prod[:, i, :].rearrange("p (f s) -> p f s", f=2), src, w, ALU.mult)
                        ins.then_inc(rope_mult, 1)
                if r >= 4 and r % 2 == 0:
                    dec = cst[:, C_DECAY + hd * SEQ:C_DECAY + (hd + 1) * SEQ]
                    dve.wait_ge(ret_scores, hd + 1)
                    dve.wait_ge(decay_in, 16)
                    dve.tensor_tensor(inner[:, 0:SEQ], bank[6][:, 0:SEQ], dec, ALU.mult).then_inc(inner_ready, 1)
                    dve.tensor_tensor(inner[:, SEQ:SEQ + P], bank[6][:, SEQ:SEQ + P], dec[:, 0:P], ALU.mult).then_inc(inner_ready, 1)
                for m in ROUND_MODS[r]:
                    mod_store(m)
                if r >= 4 and r % 2 == 1:
                    for tt in range(TT):
                        dve.wait_ge(o_done, 2 * hd + tt + 1)
                        own.step(dve, dve.bn_stats(bn[:, tt, :], bank[2 + tt][:]))
                        own.step(dve, dve.bn_aggr(mv[:, tt, :], bn[:, tt, :]))
                    dve.tensor_scalar(var[:, 0:2], mv[:, :, 1], EPS, None, ALU.add).then_inc(o_var, 1)
                    dve.wait_ge(o_root, hd + 1)
                    own.step(dve, dve.reciprocal(rstd[:, 0:2], root[:, 0:2]))
                    if hd:
                        dve.wait_ge(yh_turned, 2 * hd)
                    for tt in range(TT):
                        dve.tensor_scalar(on[:, tt, :], bank[2 + tt][:], mv[:, tt, 0:1], rstd[:, tt:tt + 1],
                                          ALU.subtract, ALU.mult).then_inc(o_norm, 1)
                    for tt in range(TT):
                        dve.wait_ge(o_norm, 2 * hd + tt + 1)
                        dve.wait_ge(g_silu, 2 * hd + tt + 1)
                        dve.tensor_tensor(on[:, tt, :], on[:, tt, :], sg[:, tt, :], ALU.mult).then_inc(yh_ready, 1)
            for i, m in enumerate(LAST_MODS):
                mod_main(m)
                if i:
                    mod_store(m - 1)
            mod_store(LAST_MODS[-1])
            dve.wait_ge(vecs_turned, 1)
            for n, (w, b, c) in enumerate(VECS):
                src = bank[6][:, 0:256].rearrange("p (j g r) -> p r g j", j=4, g=2)[:, 2 * n:2 * n + 2]
                bias = gcol[:, 0:16] if w == 2 else cols[:, 8 + c:24 + c]
                dve.tensor_tensor(modc[:, c:c + 16].rearrange("p (r g j) -> p r g j", r=2, g=2), src,
                                  bias.rearrange("p (r g j) -> p r g j", r=2, g=2), ALU.add).then_inc(vecs_ready, 1)
            dve.wait_ge(vecs_ready, 4)
            scales(1, MOD_COL[0] + 32, gcol[:, 16:24])
            scales(2, MOD_COL[1] + 8, cols[:, 112:120])
            scales(3, MOD_COL[1] + 32, gcol[:, 24:32])
            scales(4, MOD_COL[2] + 8, gcol[:, 32:40])

            def mixed(l, banks):
                for i in range(4):
                    tt, n = i // 2, i % 2
                    s = slice(n * 512, (n + 1) * 512)
                    dve.wait_ge(mix_done, 4 * l + i + 1)
                    dve.tensor_tensor(acc[:, tt, s], bank[banks[i]][:], gate[:, 2 * l, s], ALU.mult).then_inc(h_prod, 1)
                dve.wait_ge(h_prod, 4 * l + 4)
                dve.wait_ge(h_ready, 4 * l + 3)
                dve.tensor_tensor(h[:, 1, s], h[:, 1, s], acc[:, 1, s], ALU.add).then_inc(h_ready, 1)

            def experts(l):
                n = 1 + 2 * l
                S = moe[l]
                normed(n)
                modulate(n, xnT, 1 + 2 * l, MOD_COL[l] + 24)
                dve.wait_ge(logit_parts, l + 1)
                dve.tensor_copy(parts, bank[0][:, 0:SEQ]).then_inc(parts_copied, 1)
                dve.wait_ge(sig_ready, l + 1)
                G = TT * NG
                own.step(dve, dve.tensor_tensor(biased[:], score[:], br[:].unsqueeze(1).to_broadcast([P, TT, NE]), ALU.add))
                flat = biased[:].rearrange("p t (g e) -> p (t g) e", g=NG)

                def ranks(values, groups, dst):
                    n = groups * EG * EG
                    c1 = cmp1[:, 0:n].rearrange("p (g i j) -> p g i j", i=EG, j=EG)
                    c2 = cmp2[:, 0:n].rearrange("p (g i j) -> p g i j", i=EG, j=EG)
                    mine = values.unsqueeze(3).to_broadcast([P, groups, EG, EG])
                    theirs = values.unsqueeze(2).to_broadcast([P, groups, EG, EG])
                    earlier = cst[:, C_EARLIER:C_EARLIER + EG * EG].unsqueeze(1).to_broadcast([P, groups, EG * EG])
                    own.step(dve, dve.tensor_tensor(c1, theirs, mine, ALU.is_gt))
                    own.step(dve, dve.tensor_tensor(c2, theirs, mine, ALU.is_equal))
                    f2 = cmp2[:, 0:n].rearrange("p (g i) -> p g i", i=EG * EG)
                    own.step(dve, dve.tensor_tensor(f2, f2, earlier, ALU.mult))
                    own.step(dve, dve.tensor_tensor(cmp1[:, 0:n], cmp1[:, 0:n], cmp2[:, 0:n], ALU.add))
                    own.step(dve, dve.tensor_reduce(dst, cmp1[:, 0:n].rearrange("p (i j) -> p i j", j=EG), AX.X, ALU.add))

                ranks(flat, G, rank[:])
                own.step(dve, dve.tensor_scalar(rank[:], rank[:], 2.0, None, ALU.is_lt))
                two = cmp1[:, 0:TT * NE]
                own.step(dve, dve.tensor_tensor(two, rank[:], biased[:].rearrange("p t e -> p (t e)"), ALU.mult))
                own.step(dve, dve.tensor_reduce(gsum[:], two.rearrange("p (g e) -> p g e", e=EG), AX.X, ALU.add))
                ranks(gsum[:].rearrange("p (t g) -> p t g", g=NG), TT, grank[:])
                own.step(dve, dve.tensor_scalar(grank[:], grank[:], 1.0, None, ALU.is_lt))
                dve.tensor_tensor(chosen[:].rearrange("p t (g e) -> p (t g) e", g=NG),
                                  rank[:].rearrange("p (g e) -> p g e", e=EG),
                                  grank[:].unsqueeze(2).to_broadcast([P, G, EG]), ALU.mult).then_inc(chosen_ready, 1)
                dve.wait_ge(chosen_ready, l + 1)
                own.step(dve, dve.tensor_tensor(combine[:], score[:], chosen[:], ALU.mult))
                own.step(dve, dve.tensor_reduce(den[:], combine[:], AX.X, ALU.add))
                own.step(dve, dve.reciprocal(den[:], den[:]))
                own.step(dve, dve.tensor_tensor(combine[:], combine[:], den[:].unsqueeze(2).to_broadcast([P, TT, NE]), ALU.mult))
                for i in (0, 1, 3):
                    dve.memset(bank[i][:], 0.0).then_inc(S["comb_done"], 1)
                dve.wait_ge(ranked, l + 1)
                own.step(dve, dve.tensor_copy(cmp2[:, 0:3 * NE], bank[2][:, 0:3 * NE]))
                dve.memset(bank[2][:], 0.0).then_inc(S["comb_done"], 1)
                own.step(dve, dve.scalar_tensor_tensor(place[:].rearrange("p t e -> p (t e)"), cmp2[:, 0:2 * NE], 1.0,
                                                       chosen[:].rearrange("p t e -> p (t e)"), ALU.add, ALU.mult))
                own.step(dve, dve.tensor_scalar(place[:], place[:], 1.0, None, ALU.subtract))
                own.step(dve, dve.tensor_reduce(most[:, 0, :], cmp2[:, 2 * NE:3 * NE].rearrange("p (g e) -> p g e", e=2), AX.X, ALU.max))
                own.step(dve, dve.tensor_scalar(most[:, 1, :], most[:, 0, :], float(SLOTS) + 0.5, 1.0, ALU.is_gt, ALU.add))
                for r in range(2, ROUNDS):
                    own.step(dve, dve.scalar_tensor_tensor(most[:, 1, :], most[:, 0, :], float(r * SLOTS) + 0.5, most[:, 1, :], ALU.is_gt, ALU.add))
                own.step(dve, dve.tensor_tensor_scan(boundf[:, 1:PAIRS + 1], zeros[:, 0:PAIRS], most[0:1, 1, :], 0.0,
                                                     ALU.add, ALU.add))
                dve.tensor_copy(bounds[l][0:1, :], boundf[:]).then_inc(bounds_ready, 1)
                dve.wait_ge(bounds_ready, l + 1)

                def into_h(u):
                    for i in range(4):
                        n2, tt = i // 2, i % 2
                        a = h[:, tt, n2 * 512:(n2 + 1) * 512]
                        dve.wait_ge(S["comb_done"], u * 4 + i + 1)
                        dve.tensor_tensor(a, bank[(2, 3, 0, 1)[i]][:], a, ALU.add).then_inc(S["h_added"], 1)

                dve.wait_ge(S["comb_done"], 4)
                with dve.Fori(0, PAIRS) as pair:
                    begin = dve.value_load(bounds[l][0:1, bass.ds(pair, 1)], min_val=0, max_val=ROUNDS * PAIRS)
                    end = dve.value_load(bounds[l][0:1, bass.ds(pair + 1, 1)], min_val=1, max_val=ROUNDS * PAIRS)
                    dve.tensor_copy(slot_id[:], slots0).then_inc(S["slots_ready"], 1)
                    with dve.Fori(begin, end) as u:
                        dve.wait_ge(S["slots_ready"], pair + u + 1)
                        four = [P, TT, 2, SLOTS]
                        v, vw = (x.rearrange("p t (e s) -> p t e s", e=2) for x in (pick, pickw))
                        dve.tensor_tensor(v, slot_id[:].unsqueeze(1).unsqueeze(1).to_broadcast(four),
                                          place[:, :, bass.ds(pair * 2, 2)].unsqueeze(3).to_broadcast(four),
                                          ALU.is_equal).then_inc(S["picked"], 1)
                        dve.wait_ge(S["picked"], u * 2 + 1)
                        dve.tensor_tensor(vw, v, combine[:, :, bass.ds(pair * 2, 2)].unsqueeze(3).to_broadcast(four),
                                          ALU.mult).then_inc(S["picked"], 1)
                        dve.tensor_scalar(slot_id[:], slot_id[:], float(SLOTS), None, ALU.add).then_inc(S["slots_ready"], 1)
                        into_h(u)
                        dve.wait_ge(S["gathered"], u * 2 + 1)
                        for k in range(4):
                            ins = dve.tensor_scalar(xgT[:, k, :], bank[4][:, tok(k)], scale[:, 1 + 2 * l, k:k + 1],
                                                    modc[:, MOD_COL[l] + 24 + k:MOD_COL[l] + 25 + k], ALU.mult, ALU.add)
                        ins.then_inc(S["xg_dve"], 1)
                        dve.wait_ge(S["sil_ready"], u + 1)
                        for f in range(2):
                            s = slice(f * 256, (f + 1) * 256)
                            dve.wait_ge(S["up_done"], u * 2 + f + 1)
                            dve.tensor_tensor(hid[:, s], bank[1 + f][:, 0:256], sil[:, s], ALU.mult).then_inc(S["hid_ready"], 1)
                        dve.wait_ge(S["hid_turned"], u * 2 + 2)
                        dve.tensor_copy(hidT[:, 2:4, :], bank[4][:, 0:SEQ].rearrange("p (k s) -> p k s", k=2)).then_inc(S["hidT_dve"], 1)
                        for n2 in range(2):
                            s = slice(n2 * 512, (n2 + 1) * 512)
                            dve.wait_ge(S["down_done"], u * 2 + n2 + 1)
                            dve.tensor_tensor(yg[:, s], bank[6 + n2][:], gate[:, 2 * l + 1, s], ALU.mult).then_inc(S["yg_ready"], 1)
                total = dve.value_load(bounds[l][0:1, PAIRS:PAIRS + 1], min_val=PAIRS, max_val=ROUNDS * PAIRS)
                into_h(total)

            mixed(0, (0, 1, 2, 3))
            experts(0)
            normed(2)
            modulate(2, hnT, 4, MOD_COL[2])
            modulate(2, xnT, 2, MOD_COL[1])
            dve.wait_ge(kr_raw, 1)
            for i in range(2):
                w = trig[:, 1, i:i + 1, :].to_broadcast([P, 2, SEQ])
                dve.tensor_tensor(mprod[:, i, :].rearrange("p (f s) -> p f s", f=2),
                                  mla_bank[5][:].rearrange("p (f s) -> p f s", f=2), w, ALU.mult).then_inc(kr_mult, 1)
            dve.wait_ge(lat_sq, 4)
            dve.tensor_scalar(var[:, 0:2], msq[:, 0:2], 1.0 / KVL, EPS, ALU.mult, ALU.add).then_inc(lat_ms, 1)
            dve.tensor_scalar(var[:, 2:4], msq[:, 2:4], 1.0 / QL, EPS, ALU.mult, ALU.add).then_inc(lat_ms, 1)
            dve.wait_ge(lat_root, 1)
            own.step(dve, dve.reciprocal(rstd[:, 0:4], root[:, 0:4]))
            for tt in range(TT):
                dve.tensor_scalar(cn[:, tt, :], mla_bank[4][:, tt * KVL:(tt + 1) * KVL], rstd[:, tt:tt + 1], None, ALU.mult).then_inc(lat_norm, 1)
            for tt in range(TT):
                dve.tensor_scalar(qn[:, tt, :], mla_bank[6][:, tt * QL:(tt + 1) * QL], rstd[:, 2 + tt:3 + tt], None, ALU.mult).then_inc(lat_norm, 1)
            dve.wait_ge(lat_turned, 2)
            for j in range(2):
                dve.tensor_scalar(qaT[:, j, :], mla_bank[0][:, j * SEQ:(j + 1) * SEQ], gcol[:, 41 + j:42 + j], None, ALU.mult).then_inc(qaT_ready, 1)
            for b in (2, 4):
                dve.wait_ge(kv_done, b)
                dve.tensor_copy(knT[:, 2 * (b - 1):2 * b, :], mla_bank[b][:].rearrange("p (k s) -> p k s", k=2)).then_inc(kv_dve, 1)
            for b in (1, 3):
                dve.wait_ge(kv_done, 4 + b + 1)
                dve.tensor_copy(vm[:, b // 2, 512:1024], mla_bank[(5, 6, 7, 0)[b]][:]).then_inc(kv_dve, 1)
            dve.wait_ge(kr_ready, 5)
            for f in range(2):
                dve.wait_ge(qb_done, 1 + f)
                for i in range(2):
                    w = trig[:, 1, i:i + 1, :].to_broadcast([P, 2, SEQ])
                    dve.tensor_tensor(mprod[:, 2 * f + i, :].rearrange("p (f s) -> p f s", f=2),
                                      mla_bank[5 + f][:].rearrange("p (f s) -> p f s", f=2), w, ALU.mult).then_inc(qr_mult, 1)
            for b in (2, 4):
                dve.wait_ge(qb_done, 2 + b)
                dve.tensor_copy(qnT[:, 2 * (b - 1):2 * b, :], mla_bank[b][:].rearrange("p (k s) -> p k s", k=2)).then_inc(qb_dve, 1)

            def head_max(hd):
                b = att_bank[hd % 3]
                m = smax[:, hd % 3, :]
                dve.wait_ge(att_score, hd + 1)
                if hd >= 3:
                    dve.wait_ge(att_exp, 2 * (hd - 2))
                for s in (slice(CH, P), slice(P + 3 * CH, P + 4 * CH)):
                    dve.tensor_scalar(b[0:CH, s], b[0:CH, s], -3e38, None, ALU.add).then_inc(att_masked, 1)
                for tt, s in enumerate((slice(0, P), slice(P, P + SEQ))):
                    dve.wait_ge(att_masked, 2 * hd + tt + 1)
                    dve.tensor_reduce(m[:, tt:tt + 1], b[:, s], AX.X, ALU.max).then_inc(att_top, 1)
                dve.wait_ge(att_top, 2 * hd + 2)
                dve.tensor_scalar(m, m, -SOFT, None, ALU.mult).then_inc(att_max, 1)

            def head_scale(hd):
                dve.wait_ge(att_exp, 2 * (hd + 1))
                own.step(dve, dve.reciprocal(srec[:, hd % 2, :], ssum[:, hd % 2, :]))
                for tt, s in enumerate((slice(0, P), slice(P, P + SEQ))):
                    dve.tensor_scalar(prob[:, hd % 2, s], prob[:, hd % 2, s], srec[:, hd % 2, tt:tt + 1], None,
                                      ALU.mult).then_inc(att_prob, 1)

            head_max(0)
            head_max(1)
            for hd in range(MH):
                head_scale(hd)
                if hd + 2 < MH:
                    head_max(hd + 2)
            mixed(1, (1, 2, 3, 4))
            experts(1)
            dve.wait_ge(fn_in, 16)
            for tt in range(TT):
                inverse_rms(4, tt)
                dve.scalar_tensor_tensor(acc[:, tt, :], h[:, tt, :], rstd[:, tt:tt + 1], gate[:, 0, :],
                                         ALU.mult, ALU.mult).then_inc(h_ready, 1)

        @block.gpsimd
        def _(pool):
            pool.memset(cpad[:].rearrange("p k n -> p (k n)"), 0.0).then_inc(cpad_cleared, 1)
            pool.memset(wr[:].rearrange("p k n -> p (k n)"), 0.0).then_inc(wr_cleared, 1)
            for n in range(8):
                pool.wait_ge(rope_mult, n + 1)
                r, b = n // 2, n % 2
                dst = (qT, kT)[r % 2]
                k = 4 * (r // 2) + 2 * b
                pool.tensor_tensor(dst[:, k, :], prod[:, 0, 0:SEQ], prod[:, 1, SEQ:2 * SEQ], ALU.subtract)
                pool.tensor_tensor(dst[:, k + 1, :], prod[:, 1, 0:SEQ], prod[:, 0, SEQ:2 * SEQ], ALU.add).then_inc(rope_done, 1)

            def into_h(s):
                for i in range(3):
                    tt, n = i // 2, i % 2
                    c = slice(n * 512, (n + 1) * 512)
                    pool.wait_ge(h_prod, 4 * s + i + 1)
                    pool.tensor_tensor(h[:, tt, c], h[:, tt, c], acc[:, tt, c], ALU.add).then_inc(h_ready, 1)

            into_h(0)
            kva = slot(MLA_AT)[:, 0:KT * 192].rearrange("p (k n) -> p k n", k=KT)
            for f in range(2):
                pool.wait_ge(landed[f][MLA_AT % RING], 16 * (MLA_AT // RING + 1))
            for f in range(2):
                src = kva[:, :, KVL + f * HALF:KVL + (f + 1) * HALF]
                pool.tensor_copy(kr_w[:, f].rearrange("p k (c n) -> p k c n", c=4),
                                 src.unsqueeze(2).to_broadcast([P, KT, 4, HALF])).then_inc(rope_w, 1)
            qb = slot(MLA_AT + 3)[:, 0:3072].rearrange("p (k h n) -> p k h n", k=2, h=MH)
            for f in range(2):
                pool.wait_ge(landed[f][(MLA_AT + 3) % RING], 16 * ((MLA_AT + 3) // RING + 1))
            for f in range(2):
                pool.tensor_copy(qr_w[:, f].rearrange("p k (h n) -> p k h n", h=MH),
                                 qb[:, :, :, NOPE + f * HALF:NOPE + (f + 1) * HALF]).then_inc(rope_w, 1)
            pool.wait_ge(kr_mult, 2)
            pool.wait_ge(lat_turned, 2)
            pool.memset(xnT[:].rearrange("p k s -> p (k s)"), 0.0).then_inc(kr_ready, 1)
            pool.wait_ge(kr_ready, 1)
            for g in range(4):
                q = slice(32 * g, 32 * g + 32)
                pool.tensor_tensor(krT[q, g, 0, :], mprod[q, 0, 0:SEQ], mprod[q, 1, SEQ:2 * SEQ], ALU.subtract)
                pool.tensor_tensor(krT[q, g, 1, :], mprod[q, 1, 0:SEQ], mprod[q, 0, SEQ:2 * SEQ], ALU.add).then_inc(kr_ready, 1)
            pool.wait_ge(qr_mult, 4)
            pool.tensor_tensor(qrT[:, 0, :, :].rearrange("p g s -> p (g s)"), mprod[:, 0, :], mprod[:, 3, :], ALU.subtract).then_inc(qr_ready, 1)
            pool.tensor_tensor(qrT[:, 1, :, :].rearrange("p g s -> p (g s)"), mprod[:, 1, :], mprod[:, 2, :], ALU.add).then_inc(qr_ready, 1)
            into_h(1)


_INS = ["x", "c", "positions", "w_mod", "b_mod", "norm_mix", "norm_ffn", "ret_w_in", "ret_w_out", "w_mod_kv",
        "b_mod_kv", "norm_kv", "mla_w_kv_a", "mla_kv_norm", "mla_w_kv_b", "mla_w_q_a", "mla_q_norm", "mla_w_q_b",
        "mla_w_o", "router_w", "router_b", "moe_w_gate", "moe_w_up", "moe_w_down", "final_norm"]


def kernel(**inputs):
    import concourse.bacc as bacc
    from concourse.bass_utils import run_bass_kernel_spmd as run

    nc = bacc.Bacc("TRN2", target_bir_lowering=False, num_devices=1)
    arrays = {"constants": constants()}
    arrays.update({name: np.ascontiguousarray(inputs[name]) for name in _INS})
    args = {name: nc.dram_tensor(f"in_{name}", a.shape, mybir.dt.from_np(a.dtype), kind="ExternalInput").ap()
            for name, a in arrays.items()}
    out = nc.dram_tensor("out", (1, SEQ, D), F32, kind="ExternalOutput").ap()
    build_kernel(nc, args, out)
    r = run(nc, [{f"in_{name}": a for name, a in arrays.items()}], core_ids=[0])
    return r.results[0]["out"]
```
